# Optimizing a Trainium2 kernel written in Bass

```python
import math
import jax
import jax.numpy as jnp
from jax import lax
import numpy as np

D_MODEL = 1024
BATCH = 1
SEQ = 256
DEPTH = 4
DEC_BATCH = 8
DEC_SEQ = 1
PAST_LEN = 1024
PAGE_SIZE = 128

N_MIXERS = 3
PLE_DIM = 256
D_FF = 4 * D_MODEL
NORM_EPS = 1e-6
CONV_W = 4

SSD_EXPAND = 2
SSD_D_INNER = SSD_EXPAND * D_MODEL
SSD_HEAD_DIM = 64
SSD_HEADS = SSD_D_INNER // SSD_HEAD_DIM
SSD_GROUPS = 8
SSD_STATE = 128
SSD_CONV_DIM = SSD_D_INNER + 2 * SSD_GROUPS * SSD_STATE
SSD_IN_DIM = SSD_D_INNER + SSD_CONV_DIM + SSD_HEADS
SSD_CHUNK = 128

MOBA_HEADS = 8
MOBA_HEAD_DIM = D_MODEL // MOBA_HEADS
MOBA_BLOCK = 256
MOBA_TOPK = 3
MOBA_QBLOCK = 8

LRU_WIDTH = D_MODEL
LRU_BLOCKS = 8
LRU_BLOCK_W = LRU_WIDTH // LRU_BLOCKS
LRU_C = 8.0

N_SSD_LAYERS = (DEPTH + 2) // 3
N_MOBA_LAYERS = (DEPTH + 1) // 3
N_LRU_LAYERS = DEPTH // 3

N_PAGES = PAST_LEN // PAGE_SIZE
N_POOL_PAGES = (DEC_BATCH * N_PAGES * 5) // 4

kernel_name = 'ssd_moba_rglru_hybrid_step'

def rmsnorm(x, g):
    xf = x.astype(jnp.float32)
    var = jnp.mean(xf * xf, axis=-1, keepdims=True)
    return (xf * lax.rsqrt(var + NORM_EPS)).astype(x.dtype) * g

def causal_dwconv(x, buf, w, b):
    L = x.shape[1]
    xp = jnp.concatenate([buf, x], axis=1)
    y = sum(xp[:, k:k + L] * w[k] for k in range(CONV_W)) + b
    return y, xp[:, -(CONV_W - 1):]

def ssd_scan(x, dt, A, B, C, h0):
    b, L, H, P = x.shape
    G, N = B.shape[2], B.shape[3]
    R = H // G
    T = min(SSD_CHUNK, L)
    nc = -(-L // T)
    pad = nc * T - L
    xdt = x * dt[..., None]
    dA = dt * A
    if pad:
        padl = lambda a: jnp.pad(a, [(0, 0), (0, pad)] + [(0, 0)] * (a.ndim - 2))
        xdt, dA, B, C = padl(xdt), padl(dA), padl(B), padl(C)
    xdt = xdt.reshape(b, nc, T, G, R, P)
    dA = dA.reshape(b, nc, T, G, R)
    B = B.reshape(b, nc, T, G, N)
    C = C.reshape(b, nc, T, G, N)
    a_cum = jnp.cumsum(dA, axis=2)
    causal = jnp.tril(jnp.ones((T, T), bool))[:, :, None, None]
    seg = a_cum[:, :, :, None] - a_cum[:, :, None, :]
    decay_ts = jnp.where(causal, jnp.exp(jnp.where(causal, seg, 0.0)), 0.0)
    cb = jnp.einsum('bctgn,bcsgn->bctsg', C, B)
    y_diag = jnp.einsum('bctsg,bctsgr,bcsgrp->bctgrp', cb, decay_ts, xdt)
    decay_to_end = jnp.exp(a_cum[:, :, -1:] - a_cum)
    chunk_states = jnp.einsum('bcsgn,bcsgr,bcsgrp->bcgrpn', B, decay_to_end, xdt)
    chunk_decay = jnp.exp(a_cum[:, :, -1])

    def step(h, inp):
        st, dec = inp
        return h * dec[..., None, None] + st, h

    h_last, h_in = lax.scan(step, h0.reshape(b, G, R, P, N).astype(chunk_states.dtype),
                            (jnp.moveaxis(chunk_states, 1, 0), jnp.moveaxis(chunk_decay, 1, 0)))
    h_in = jnp.moveaxis(h_in, 0, 1)
    y_off = jnp.einsum('bctgn,bcgrpn,bctgr->bctgrp', C, h_in, jnp.exp(a_cum))
    y = (y_diag + y_off).reshape(b, nc * T, H, P)[:, :L]
    return y, h_last.reshape(b, H, P, N)

def ssd_mixer(xn, conv_buf, ssm_state, w_in, conv_w, conv_b, dt_bias, a_log, d_skip, norm_g, w_out):
    b, L, _ = xn.shape
    z, xbc, dt = jnp.split(xn @ w_in, [SSD_D_INNER, SSD_D_INNER + SSD_CONV_DIM], axis=-1)
    xbc, new_buf = causal_dwconv(xbc, conv_buf, conv_w, conv_b)
    xbc = jax.nn.silu(xbc)
    xs, B, C = jnp.split(xbc, [SSD_D_INNER, SSD_D_INNER + SSD_GROUPS * SSD_STATE], axis=-1)
    xs = xs.reshape(b, L, SSD_HEADS, SSD_HEAD_DIM)
    B = B.reshape(b, L, SSD_GROUPS, SSD_STATE)
    C = C.reshape(b, L, SSD_GROUPS, SSD_STATE)
    dt = jax.nn.softplus(dt + dt_bias)
    A = -jnp.exp(a_log)
    y, new_state = ssd_scan(xs, dt, A, B, C, ssm_state)
    y = y + xs * d_skip[:, None]
    y = y.reshape(b, L, SSD_D_INNER) * jax.nn.silu(z)
    y = rmsnorm(y.reshape(b, L, SSD_GROUPS, -1), norm_g.reshape(SSD_GROUPS, -1)).reshape(b, L, SSD_D_INNER)
    return y @ w_out, new_buf, new_state

def gather_pages(pool, li, table, new_pages, b_idx, lp, h_idx):
    n_new = new_pages.shape[1]
    if table is None:
        return new_pages[b_idx, jnp.clip(lp, 0, n_new - 1), :, h_idx]
    n_past = table.shape[1]
    new_rows = new_pages[b_idx, jnp.clip(lp - n_past, 0, n_new - 1), :, h_idx]
    past_rows = pool[li, table[b_idx, jnp.clip(lp, 0, n_past - 1)], :, h_idx]
    return jnp.where((lp < n_past)[..., None, None], past_rows, new_rows)

def moba_mixer(xn, pos0, w_qkv, w_o, k_pool, v_pool, li, table):
    b, L, _ = xn.shape
    H, HD = MOBA_HEADS, MOBA_HEAD_DIM
    q, k, v = jnp.split(xn @ w_qkv, 3, axis=-1)
    q = q.reshape(b, L, H, HD)
    k = k.reshape(b, L, H, HD)
    v = v.reshape(b, L, H, HD)
    ppb = MOBA_BLOCK // PAGE_SIZE
    n_new = -(-L // PAGE_SIZE)
    row_pad = ((0, 0), (0, n_new * PAGE_SIZE - L), (0, 0), (0, 0))
    k_new = jnp.pad(k, row_pad).reshape(b, n_new, PAGE_SIZE, H, HD)
    v_new = jnp.pad(v, row_pad).reshape(b, n_new, PAGE_SIZE, H, HD)
    page_sums = jnp.sum(k_new, axis=2, dtype=jnp.float32)
    n_past = 0
    if table is not None:
        n_past = table.shape[1]
        pool_sums = jnp.sum(k_pool[li], axis=1, dtype=jnp.float32)
        page_sums = jnp.concatenate([pool_sums[table], page_sums], axis=1)
    n_tot = n_past + n_new
    nb = -(-n_tot // ppb)
    page_sums = jnp.pad(page_sums, ((0, 0), (0, nb * ppb - n_tot), (0, 0), (0, 0)))
    block_mean = page_sums.reshape(b, nb, ppb, H, HD).sum(axis=2) / MOBA_BLOCK
    pos = pos0 + jnp.arange(L, dtype=jnp.int32)
    own = pos // MOBA_BLOCK
    gate = jnp.einsum('blhd,bnhd->blhn', q.astype(jnp.float32), block_mean)
    eligible = jnp.arange(nb)[None, :] < own[:, None]
    gate = jnp.where(eligible[None, :, None, :], gate, -jnp.inf)
    k_sel = min(MOBA_TOPK, nb)
    _, sel = lax.top_k(gate, k_sel)
    blocks = jnp.concatenate([sel.astype(jnp.int32), jnp.broadcast_to(own[None, :, None, None], (b, L, H, 1))], axis=-1)
    slot_ok = jnp.concatenate([jnp.arange(k_sel)[None, :] < own[:, None], jnp.ones((L, 1), bool)], axis=-1)
    n_slots = k_sel + 1
    qb = min(MOBA_QBLOCK, L)
    ng = -(-L // qb)
    q_pad = ng * qb - L

    def to_groups(a):
        a = jnp.pad(a, [(0, 0), (0, q_pad)] + [(0, 0)] * (a.ndim - 2))
        return jnp.moveaxis(a.reshape((b, ng, qb) + a.shape[2:]), 1, 0)

    pos_g = jnp.pad(pos, (0, q_pad)).reshape(ng, qb)
    ok_g = jnp.pad(slot_ok, ((0, q_pad), (0, 0)), constant_values=True).reshape(ng, qb, n_slots)
    b_idx = jnp.arange(b)[:, None, None, None, None]
    h_idx = jnp.arange(H)[None, None, :, None, None]
    scale = HD ** -0.5

    def attend(args):
        qg, blk, pg, okg = args
        lp = blk[..., None] * ppb + jnp.arange(ppb)
        kg = gather_pages(k_pool, li, table, k_new, b_idx, lp, h_idx).reshape(b, qb, H, n_slots, MOBA_BLOCK, HD)
        vg = gather_pages(v_pool, li, table, v_new, b_idx, lp, h_idx).reshape(b, qb, H, n_slots, MOBA_BLOCK, HD)
        key_pos = blk[..., None] * MOBA_BLOCK + jnp.arange(MOBA_BLOCK)
        mask = okg[None, :, None, :, None] & (key_pos <= pg[None, :, None, None, None])
        s = jnp.einsum('bqhd,bqhkld->bqhkl', qg, kg).astype(jnp.float32) * scale
        s = jnp.where(mask, s, -jnp.inf).reshape(b, qb, H, n_slots * MOBA_BLOCK)
        p = jax.nn.softmax(s, axis=-1).reshape(b, qb, H, n_slots, MOBA_BLOCK).astype(vg.dtype)
        return jnp.einsum('bqhkl,bqhkld->bqhd', p, vg)

    out = lax.map(attend, (to_groups(q), to_groups(blocks), pos_g, ok_g))
    out = jnp.moveaxis(out, 0, 1).reshape(b, ng * qb, H * HD)[:, :L]
    return out @ w_o, k, v

def rglru_mixer(xn, conv_buf, h0, w_in, conv_w, conv_b, w_a, b_a, w_x, b_x, lam, w_out):
    b, L, _ = xn.shape
    gate_br, x_br = jnp.split(xn @ w_in, 2, axis=-1)
    x_br, new_buf = causal_dwconv(x_br, conv_buf, conv_w, conv_b)
    xb = x_br.reshape(b, L, LRU_BLOCKS, LRU_BLOCK_W)
    r = jax.nn.sigmoid(jnp.einsum('blnc,ncd->blnd', xb, w_a) + b_a).reshape(b, L, LRU_WIDTH)
    i = jax.nn.sigmoid(jnp.einsum('blnc,ncd->blnd', xb, w_x) + b_x).reshape(b, L, LRU_WIDTH)
    log_a = -LRU_C * r * jax.nn.softplus(-lam)
    a = jnp.exp(log_a)
    u = jnp.sqrt(-jnp.expm1(2.0 * log_a)) * (i * x_br)

    def step(h, au):
        a_t, u_t = au
        h = a_t * h + u_t
        return h, h

    h_last, hs = lax.scan(step, h0.astype(u.dtype), (jnp.moveaxis(a, 1, 0), jnp.moveaxis(u, 1, 0)))
    hs = jnp.moveaxis(hs, 0, 1)
    y = jax.nn.gelu(gate_br) * hs
    return y @ w_out, new_buf, h_last

def trunk(h, p, pos0, ssd_conv, ssd_state, k_pool, v_pool, table, lru_conv, lru_state, W):
    b = h.shape[0]
    n_ssd_conv, n_ssd_state, n_k, n_v, n_lru_conv, n_lru_state = [], [], [], [], [], []
    for i in range(DEPTH):
        j = i // N_MIXERS
        kind = i % N_MIXERS
        xn = rmsnorm(h, W['norm_mix'][i])
        if kind == 0:
            buf = jnp.zeros((b, CONV_W - 1, SSD_CONV_DIM), h.dtype) if ssd_conv is None else ssd_conv[j]
            st = jnp.zeros((b, SSD_HEADS, SSD_HEAD_DIM, SSD_STATE), h.dtype) if ssd_state is None else ssd_state[j]
            out, buf, st = ssd_mixer(xn, buf, st, W['ssd_w_in'][j], W['ssd_conv_w'][j], W['ssd_conv_b'][j],
                                     W['ssd_dt_bias'][j], W['ssd_a_log'][j], W['ssd_d'][j], W['ssd_norm'][j],
                                     W['ssd_w_out'][j])
            n_ssd_conv.append(buf)
            n_ssd_state.append(st)
        elif kind == 1:
            out, kr, vr = moba_mixer(xn, pos0, W['moba_w_qkv'][j], W['moba_w_o'][j], k_pool, v_pool, j, table)
            n_k.append(kr)
            n_v.append(vr)
        else:
            buf = jnp.zeros((b, CONV_W - 1, LRU_WIDTH), h.dtype) if lru_conv is None else lru_conv[j]
            st = jnp.zeros((b, LRU_WIDTH), h.dtype) if lru_state is None else lru_state[j]
            out, buf, st = rglru_mixer(xn, buf, st, W['lru_w_in'][j], W['lru_conv_w'][j], W['lru_conv_b'][j],
                                       W['lru_w_a'][j], W['lru_b_a'][j], W['lru_w_x'][j], W['lru_b_x'][j],
                                       W['lru_lambda'][j], W['lru_w_out'][j])
            n_lru_conv.append(buf)
            n_lru_state.append(st)
        h = h + out
        hn = rmsnorm(h, W['norm_mlp'][i])
        h = h + jnp.square(jax.nn.relu(hn @ W['mlp_w_up'][i])) @ W['mlp_w_down'][i]
        gate = jax.nn.sigmoid(rmsnorm(h, W['norm_ple'][i]) @ W['ple_w_gate'][i])
        h = h + (p[i] @ W['ple_w_proj'][i]) * gate
    y = rmsnorm(h, W['norm_final'])
    return (y, jnp.stack(n_ssd_conv), jnp.stack(n_ssd_state), jnp.stack(n_k), jnp.stack(n_v),
            jnp.stack(n_lru_conv), jnp.stack(n_lru_state))

def setup_inputs(seed: int = 0) -> dict:
    key = jax.random.key(seed)
    keys = list(jax.random.split(key, 48))

    def normal(shape, scale=1.0):
        return scale * jax.random.normal(keys.pop(), shape, jnp.float32)

    def gain(shape):
        return 1.0 + normal(shape, 0.02)

    def uniform(shape, lo, hi):
        return jax.random.uniform(keys.pop(), shape, jnp.float32, lo, hi)

    NS, NM, NL = N_SSD_LAYERS, N_MOBA_LAYERS, N_LRU_LAYERS
    perm = jax.random.permutation(keys.pop(), N_POOL_PAGES)
    page_table = perm[:DEC_BATCH * N_PAGES].reshape(DEC_BATCH, N_PAGES).astype(jnp.int32)
    dt0 = jnp.exp(uniform((NS, SSD_HEADS), math.log(1e-3), math.log(1e-1)))
    a_lru = uniform((NL, LRU_WIDTH), 0.9, 0.999) ** (1.0 / LRU_C)
    return {
        'x_prompt': normal((BATCH, SEQ, D_MODEL)),
        'x_sample': normal((DEC_BATCH, DEC_SEQ, D_MODEL)),
        'state_ssd_conv': normal((NS, DEC_BATCH, CONV_W - 1, SSD_CONV_DIM)),
        'state_ssd': normal((NS, DEC_BATCH, SSD_HEADS, SSD_HEAD_DIM, SSD_STATE), 0.1),
        'cache_k': normal((NM, N_POOL_PAGES, PAGE_SIZE, MOBA_HEADS, MOBA_HEAD_DIM)),
        'cache_v': normal((NM, N_POOL_PAGES, PAGE_SIZE, MOBA_HEADS, MOBA_HEAD_DIM)),
        'page_table': page_table,
        'state_lru_conv': normal((NL, DEC_BATCH, CONV_W - 1, LRU_WIDTH)),
        'state_lru': normal((NL, DEC_BATCH, LRU_WIDTH), 0.5),
        'p_prompt': normal((DEPTH, BATCH, SEQ, PLE_DIM)),
        'p_sample': normal((DEPTH, DEC_BATCH, DEC_SEQ, PLE_DIM)),
        'norm_mix': gain((DEPTH, D_MODEL)),
        'norm_mlp': gain((DEPTH, D_MODEL)),
        'norm_ple': gain((DEPTH, D_MODEL)),
        'norm_final': gain((D_MODEL,)),
        'ssd_w_in': normal((NS, D_MODEL, SSD_IN_DIM), D_MODEL ** -0.5),
        'ssd_conv_w': normal((NS, CONV_W, SSD_CONV_DIM), CONV_W ** -0.5),
        'ssd_conv_b': normal((NS, SSD_CONV_DIM), 0.02),
        'ssd_dt_bias': dt0 + jnp.log(-jnp.expm1(-dt0)),
        'ssd_a_log': jnp.log(uniform((NS, SSD_HEADS), 1.0, 16.0)),
        'ssd_d': gain((NS, SSD_HEADS)),
        'ssd_norm': gain((NS, SSD_D_INNER)),
        'ssd_w_out': normal((NS, SSD_D_INNER, D_MODEL), SSD_D_INNER ** -0.5),
        'moba_w_qkv': normal((NM, D_MODEL, 3 * MOBA_HEADS * MOBA_HEAD_DIM), D_MODEL ** -0.5),
        'moba_w_o': normal((NM, MOBA_HEADS * MOBA_HEAD_DIM, D_MODEL), (MOBA_HEADS * MOBA_HEAD_DIM) ** -0.5),
        'lru_w_in': normal((NL, D_MODEL, 2 * LRU_WIDTH), D_MODEL ** -0.5),
        'lru_conv_w': normal((NL, CONV_W, LRU_WIDTH), CONV_W ** -0.5),
        'lru_conv_b': normal((NL, LRU_WIDTH), 0.02),
        'lru_w_a': normal((NL, LRU_BLOCKS, LRU_BLOCK_W, LRU_BLOCK_W), LRU_BLOCK_W ** -0.5),
        'lru_b_a': normal((NL, LRU_BLOCKS, LRU_BLOCK_W), 0.02),
        'lru_w_x': normal((NL, LRU_BLOCKS, LRU_BLOCK_W, LRU_BLOCK_W), LRU_BLOCK_W ** -0.5),
        'lru_b_x': normal((NL, LRU_BLOCKS, LRU_BLOCK_W), 0.02),
        'lru_lambda': jnp.log(a_lru) - jnp.log1p(-a_lru),
        'lru_w_out': normal((NL, LRU_WIDTH, D_MODEL), LRU_WIDTH ** -0.5),
        'mlp_w_up': normal((DEPTH, D_MODEL, D_FF), D_MODEL ** -0.5),
        'mlp_w_down': normal((DEPTH, D_FF, D_MODEL), D_FF ** -0.5),
        'ple_w_proj': normal((DEPTH, PLE_DIM, D_MODEL), PLE_DIM ** -0.5),
        'ple_w_gate': normal((DEPTH, D_MODEL, D_MODEL), D_MODEL ** -0.5),
    }

def reference(x_prompt, x_sample, state_ssd_conv, state_ssd, cache_k, cache_v, page_table, state_lru_conv,
              state_lru, p_prompt, p_sample, norm_mix, norm_mlp, norm_ple, norm_final, ssd_w_in, ssd_conv_w,
              ssd_conv_b, ssd_dt_bias, ssd_a_log, ssd_d, ssd_norm, ssd_w_out, moba_w_qkv, moba_w_o, lru_w_in,
              lru_conv_w, lru_conv_b, lru_w_a, lru_b_a, lru_w_x, lru_b_x, lru_lambda, lru_w_out, mlp_w_up,
              mlp_w_down, ple_w_proj, ple_w_gate):
    W = {
        'norm_mix': norm_mix, 'norm_mlp': norm_mlp, 'norm_ple': norm_ple, 'norm_final': norm_final,
        'ssd_w_in': ssd_w_in, 'ssd_conv_w': ssd_conv_w, 'ssd_conv_b': ssd_conv_b, 'ssd_dt_bias': ssd_dt_bias,
        'ssd_a_log': ssd_a_log, 'ssd_d': ssd_d, 'ssd_norm': ssd_norm, 'ssd_w_out': ssd_w_out,
        'moba_w_qkv': moba_w_qkv, 'moba_w_o': moba_w_o,
        'lru_w_in': lru_w_in, 'lru_conv_w': lru_conv_w, 'lru_conv_b': lru_conv_b, 'lru_w_a': lru_w_a,
        'lru_b_a': lru_b_a, 'lru_w_x': lru_w_x, 'lru_b_x': lru_b_x, 'lru_lambda': lru_lambda,
        'lru_w_out': lru_w_out, 'mlp_w_up': mlp_w_up, 'mlp_w_down': mlp_w_down,
        'ple_w_proj': ple_w_proj, 'ple_w_gate': ple_w_gate,
    }
    (y_prompt, ssd_conv_p, ssd_state_p, k_p, v_p, lru_conv_p, lru_state_p) = trunk(
        x_prompt, p_prompt, 0, None, None, None, None, None, None, None, W)
    pos0 = page_table.shape[1] * PAGE_SIZE
    (y_sample, ssd_conv_s, ssd_state_s, k_s, v_s, lru_conv_s, lru_state_s) = trunk(
        x_sample, p_sample, pos0, state_ssd_conv, state_ssd, cache_k, cache_v, page_table,
        state_lru_conv, state_lru, W)
    return (y_prompt, y_sample, ssd_conv_p, ssd_state_p, k_p, v_p, lru_conv_p, lru_state_p,
            ssd_conv_s, ssd_state_s, k_s, v_s, lru_conv_s, lru_state_s)


_drawn_inputs = setup_inputs


def setup_inputs(seed=0):
    import zlib

    import numpy as np

    out = dict(_drawn_inputs(seed))
    spreads = {}
    factors = {'norm_ple': 50.591,
     'norm_final': 8.175,
     'ssd_d': 20.834,
     'ssd_norm': 3.026,
     'lru_b_a': 8.0,
     'lru_b_x': 6.273,
     'cache_k': 3.568,
     'cache_v': 2.881,
     'norm_mlp': 3.177}
    for name, (base, spread) in spreads.items():
        noise = np.random.default_rng([zlib.crc32(name.encode()), seed]).standard_normal(out[name].shape)
        drawn = base * np.exp(spread * noise) if base else spread * noise
        out[name] = jnp.asarray(drawn.astype(out[name].dtype))
    for name, factor in factors.items():
        out[name] = (out[name] * factor).astype(out[name].dtype)
    return out
```

```python
from contextlib import ExitStack

import concourse.bass as bass
from concourse import mybir

F32 = mybir.dt.float32
F32R = mybir.dt.float32r
I32 = mybir.dt.int32
ALU = mybir.AluOpType
ACT = mybir.ActivationFunctionType
AX = mybir.AxisListType.X
ds = bass.ds

P = 128
D = 1024
KT = D // P
SEQ = 256
NB = 8
T = SEQ + NB
DEPTH = 4
EPS = 1e-6
CW = 4
LAST = CW - 1 + NB
CHUNK = 256
CONVD = 4096
CT = CONVD // P
XT = 16
HEADS = 32
GROUPS = 8
PLE = 256
MH = 8
PAGES = 8
BLOCKS = 4
SCALE = float(P) ** -0.5
BIG = 1e30
TILE_B = T * 4
SSD_LAYERS = (0, 3)
GELU_A, GELU_B = 0.7978845608028654, 0.044715


def plan():
    stages, g, col = [], 0, 0
    for i in range(DEPTH):
        if i in SSD_LAYERS:
            mix = [("xbc", 16, 1), ("z", 8, 1), ("ssd_out", 8, 2)]
        elif i == 1:
            mix = [("qkv", 12, 1), ("wo", 4, 1)]
        else:
            mix = [("lru_in", 8, 1), ("lru_out", 4, 1)]
        for name, n, kq in mix + [("up", 16, 1), ("down", 16, 4), ("gate", 4, 1)]:
            stages.append(dict(name=name, layer=i, n=n, kq=kq, g0=g, c0=col))
            g += n
            col += n // kq
    return stages, g


def build_trunk(nc, t_in, t_out):
    stages, total = plan()
    stage = {(s["layer"], s["name"]): s for s in stages}
    ctx = ExitStack()
    with ctx:
        def sb(name, shape, dt=F32):
            return ctx.enter_context(nc.sbuf_tensor(name, shape, dt))

        def sem(name):
            return ctx.enter_context(nc.semaphore(name))

        raw = [sb(f"raw{u}", [P, KT, CHUNK]) for u in range(4)]
        whi = [sb(f"whi{u}", [P, KT, CHUNK], F32R) for u in range(2)]
        wlo = [sb(f"wlo{u}", [P, KT, CHUNK], F32R) for u in range(2)]
        h = sb("h", [P, KT, T])
        xg = sb("xg", [P, KT, T])
        xH = sb("xH", [P, KT, T], F32R)
        xL = sb("xL", [P, KT, T], F32R)
        rstd = sb("rstd", [P, T])
        rstd2 = sb("rstd2", [P, T])
        std = sb("std", [P, T])
        ssq = sb("ssq", [P, T])
        ident = sb("ident", [P, P])
        ones = sb("ones", [P, P])
        zeros = sb("zeros", [P, 64])
        tri = sb("tri", [P, 3 * P])
        amask = sb("amask", [P, 3 * P])
        colA = sb("colA", [P, 104])
        colB = sb("colB", [P, 96])
        colC = sb("colC", [P, 2, P])
        colE = sb("colE", [P, 64])
        hsm = sb("hsm", [HEADS, 6])
        evenodd = sb("evenodd", [HEADS, P])
        pairsel = sb("pairsel", [HEADS, XT])
        blockno = sb("blockno", [64, BLOCKS])
        epsc = sb("epsc", [P, 1])
        eo2 = sb("eo2", [HEADS, 2])
        ptab = sb("ptab", [1, NB * PAGES], I32)

        base = (nc.sbuf_base + 31) // 32 * 32
        arena_bytes = (nc.sbuf_usable_end - base) // 32 * 32
        ctx.enter_context(nc.sbuf_tensor("arena", [P, arena_bytes // 4 - 8], F32))

        def at(name, shape, off, dt=F32):
            n = 4
            for x in shape[1:]:
                n *= x
            assert off % 32 == 0 and off + n <= arena_bytes - 32, (name, off, n, arena_bytes)
            return nc.alloc_sbuf_tensor_at(name, shape, dt, offset=base + off)

        def row(off, items):
            got = {}
            for name, shape, *dt in items:
                got[name] = at(name, shape, off, *dt)
                n = 4
                for x in shape[1:]:
                    n *= x
                off += (n + 31) // 32 * 32
            return got, off

        A0, _ = row(0, [("xrow", [P, 2, D]), ("xrow8", [NB, D]), ("rowA", [104, P]), ("rowB", [96, P]),
                        ("rowC", [P, P]), ("rowD", [P, P]), ("rowE", [64, P])])
        Z, o1 = row(0, [("zs", [P, XT, T]), ("xbc", [P, CT, T])])
        grp, o2 = row(o1, [(f"{n}{b}", s) for b in range(2) for n, s in (
            ("stg", [P, 3, SEQ]), ("sel", [HEADS, 4, P]), ("cbm", [P, 3 * P]), ("xd", [P, 2, 4, 64]),
            ("xde", [P, 2, 4, 64]), ("btm", [P, 2, P]), ("seg", [P, 4, 3 * P]), ("stout", [P, 2, P]))])
        smp, o3 = row(o1, [(f"st{b}", [P, XT, P]) for b in range(4)])
        bcr, _ = row(2 * XT * TILE_B, [("bcrow", [NB, 2 * D]), ("scr", [P, XT, P])])
        cst, _ = row(o1, [("cst", [NB * 3, CONVD])])
        orow, _ = row(o1, [("orow", [LAST, CONVD])])
        cprod, _ = row(o1 + 16384, [("cprod", [P, CT, NB, 3])])
        ysp, o4 = row(o1, [("yH", [P, XT, T], F32R), ("yL", [P, XT, T], F32R)])
        ysq, _ = row(XT * TILE_B, [("ysq", [P, XT, T])])
        gnb, _ = row(2 * XT * TILE_B, [(f"{n}{b}", [P, T]) for b in range(2) for n in ("gstd", "grs")] +
                     [(f"yn{b}", [P, 2, T]) for b in range(2)])
        S, _ = row(max(o2, o3, o4), [("T0", [P, 2, 268]), ("T1", [P, 2, 268]), ("rawlast", [P, CT, LAST]),
                                     ("spre", [P, CT, NB])])
        o5 = max(o2, o3, o4) + 2 * 2144 + 1408 + 1024
        cstT, _ = row(o5, [("stT", [P, CT, NB * 3])])
        hv2, _ = row(o5, [("acum", [HEADS, SEQ]), ("vals", [HEADS, 17]), ("hv", [P, XT, 17]),
                          ("tm", [P, 6, HEADS]), ("xdts", [P, XT, NB]), ("ys", [P, XT, NB]),
                          ("ysb0", [P, XT]), ("ysb1", [P, XT]), ("selS0", [NB, P]), ("selS1", [NB, P]), ("bvec", [HEADS, 2])])
        hv_, _ = row(o1 + 33024, [("wdt", [P, KT, HEADS]), ("R", [HEADS, XT, 17]), ("dt", [HEADS, T]), ("dA", [HEADS, T])])
        dte_, _ = row(o1 + 22784, [("dte", [HEADS, SEQ])])
        xth, _ = row(o1 + 24576, [(f"xth{b}", [P, 4, T]) for b in range(2)])
        spl, _ = row(o1 + 16384, [(f"sp{k}", [HEADS, T]) for k in range(6)])
        M, m1 = row(0, [("qkv", [P, 3 * MH, T]), ("att", [P, KT, T]), ("rowS", [NB, 3, D])])
        pg, m2 = row(m1, [(f"pg{j}", [P, MH, P]) for j in range(PAGES)])
        mh, m3 = row(m2, [(f"{n}{b}", s) for b in range(2) for n, s in (
            ("stq", [P, 3, T]), ("kvt", [P, 4, P]), ("sc", [P, 3 * P]), ("pt", [P, 3 * P]),
            ("mx", [P, 2]), ("nm", [P, 2]), ("rs", [P, 2]), ("ri", [P, 2]))])
        ms, m4 = row(m2, [("sS", [P, PAGES, 64]), ("sR", [64, 1056]), ("pT8", [P, PAGES, 64]),
                          ("qk", [P, NB, MH]), ("gsum", [64, BLOCKS]), ("geq", [64, BLOCKS]),
                          ("gsc", [64, 8]), ("dg", [64, 64]), ("ov", [P, 64]), ("bco", [P, 64]),
                          ("qsel", [NB, P]), ("sq0", [P, PAGES, MH]), ("sq1", [P, PAGES, MH])])
        L, l1 = row(0, [("Gt", [P, KT, T]), ("XR", [P, KT, 268]), ("xc", [P, KT, T]), ("thr", [P, KT, T]),
                        ("thi", [P, KT, T]), ("la", [P, KT, T]), ("wax", [P, 16, P]),
                        ("hs", [P, KT, T]), ("lcst", [NB * 3, D]), ("lst", [NB, D]), ("lstT", [P, KT, NB * 3]),
                        ("lh0", [P, KT, NB]), ("lspre", [P, KT, NB]), ("ch", [P, KT]), ("bah", [P, KT]),
                        ("bxh", [P, KT]), ("lrow", [LAST, D]), ("hrow", [9, D]), 
                        ("lpr", [P, KT, NB, 3])])
        lsp, _ = row(l1, [(f"lp{k}", [P, KT]) for k in range(6)])
        ml, _ = row(0, [("aH", [P, 32, T], F32R), ("aL", [P, 32, T], F32R)] +
                    [(f"{n}{b}", [P, 2, T]) for b in range(2) for n in ("rl", "ac")] +
                    [("sq", [P, KT, T]), ("wp", [P, 2, D]), ("prow", [P, 2, PLE]), ("prow8", [NB, PLE]),
                     ("pT", [P, 2, T]), ("t1", [P, 2, T])])
        sq, aH, aL = ml["sq"], ml["aH"], ml["aL"]
        sq_mix, _ = row(0, [("sqm", [P, KT, T])])
        fin, _ = row(0, [("yfin", [P, KT, T]), ("yrow", [P, 2, D]), ("yrow8", [NB, D])])

        G = [ctx.enter_context(nc.psum_tensor(f"G{p}", [P, 2, 512], F32)) for p in range(2)]
        A = [ctx.enter_context(nc.psum_tensor(f"A{p}", [P, 2, 512], F32)) for p in range(2)]
        bank = [A[0][:, 0, :], A[0][:, 1, :], A[1][:, 0, :], A[1][:, 1, :],
                G[0][:, 0, :], G[0][:, 1, :], G[1][:, 0, :], G[1][:, 1, :]]

        s_raw = [sem(f"s_raw{u}") for u in range(4)]
        s_hi, s_lo = sem("s_hi"), sem("s_lo")
        s_mm = sem("s_mm")
        s_ev = sem("s_ev")
        s_xg, s_xh, s_xl = sem("s_xg"), sem("s_xh"), sem("s_xl")
        s_sq, s_ssq, s_var, s_std = sem("s_sq"), sem("s_ssq"), sem("s_var"), sem("s_std")
        s_bar = sem("s_bar")
        s_stored = sem("s_stored")
        s_const, s_load, s_load2, s_tp0 = sem("s_const"), sem("s_load"), sem("s_load2"), sem("s_tp0")
        s_init = sem("s_init")
        s_tap, s_conv = sem("s_tap"), sem("s_conv")
        s_last = sem("s_last")
        s_cst, s_cT, s_cE = sem("s_cst"), sem("s_cT"), sem("s_cE")
        s_zth, s_xth, s_th = sem("s_zth"), sem("s_xth"), sem("s_th")
        s_wdt, s_dtp, s_dt1, s_dt2, s_dt3 = sem("s_wdt"), sem("s_dtp"), sem("s_dt1"), sem("s_dt2"), sem("s_dt3")
        s_dt4, s_dt5, s_dt6 = sem("s_dt4"), sem("s_dt5"), sem("s_dt6")
        s_silu = sem("s_silu")
        s_orT, s_orE, s_orD = sem("s_orT"), sem("s_orE"), sem("s_orD")
        s_stg, s_sel, s_tp, s_ar = sem("s_stg"), sem("s_sel"), sem("s_tp"), sem("s_ar")
        s_xd, s_xde, s_seg, s_exp = sem("s_xd"), sem("s_xde"), sem("s_seg"), sem("s_exp")
        s_M, s_back, s_yev = sem("s_M"), sem("s_back"), sem("s_yev")
        s_sto = [sem(f"s_sto{b}") for b in range(2)]
        s_sin = [sem(f"s_sin{b}") for b in range(4)]
        s_sout = [sem(f"s_sout{b}") for b in range(4)]
        s_brT, s_brE, s_ssel = sem("s_brT"), sem("s_brE"), sem("s_ssel")
        s_bc, s_hd, s_hn, s_bcf = sem("s_bc"), sem("s_hd"), sem("s_hn"), sem("s_bcf")
        s_yz, s_ysq, s_gv, s_gs, s_yn, s_yh, s_mixh, s_mixl = (
            sem("s_yz"), sem("s_ysq"), sem("s_gv"), sem("s_gs"), sem("s_yn"), sem("s_yh"), sem("s_mixh"), sem("s_mixl"))
        s_out = sem("s_out")
        s_ac, s_aH, s_aL = sem("s_ac"), sem("s_aH"), sem("s_aL")
        s_ple, s_pT, s_pTe, s_pj, s_pje, s_tg = (sem("s_ple"), sem("s_pT"), sem("s_pTe"), sem("s_pj"),
                                                 sem("s_pje"), sem("s_tg"))
        s_fin, s_finT, s_finE = sem("s_fin"), sem("s_finT"), sem("s_finE")
        s_stq, s_mtp, s_msc, s_mex, s_mP = sem("s_stq"), sem("s_mtp"), sem("s_msc"), sem("s_mex"), sem("s_mP")
        s_mpT, s_mpt, s_mo, s_moe = sem("s_mpT"), sem("s_mpt"), sem("s_mo"), sem("s_moe")
        s_kst = [sem(f"s_kst{b}") for b in range(2)]
        s_tab = sem("s_tab")
        s_pg = [sem(f"s_pg{j}") for j in range(PAGES)]
        s_kd, s_vd = sem("s_kd"), sem("s_vd")
        s_qsel, s_qbc = sem("s_qsel"), sem("s_qbc")
        s_qk, s_sT, s_sR, s_sE, s_sP, s_sPT, s_sPTe = (sem("s_qk"), sem("s_sT"), sem("s_sR"), sem("s_sE"),
                                                       sem("s_sP"), sem("s_sPT"), sem("s_sPTe"))
        s_att, s_sown = sem("s_att"), sem("s_sown")
        s_lld, s_lT, s_lTe, s_lsp, s_lse = sem("s_lld"), sem("s_lT"), sem("s_lTe"), sem("s_lsp"), sem("s_lse")
        s_lt0, s_lc, s_lg, s_lth, s_lla = sem("s_lt0"), sem("s_lc"), sem("s_lg"), sem("s_lth"), sem("s_lla")
        s_la, s_lv, s_lsq, s_ly, s_lyH = sem("s_la"), sem("s_lv"), sem("s_lsq"), sem("s_ly"), sem("s_lyH")
        s_lgl, s_lgt, s_loT, s_loE = sem("s_lgl"), sem("s_lgt"), sem("s_loT"), sem("s_loE")

        block = ctx.enter_context(nc.Block())

        def weights(st):
            i, name = st["layer"], st["name"]
            q = i // 3
            return {
                "xbc": lambda: t_in["ssd_w_in"][q][:, 2048:2048 + CONVD],
                "z": lambda: t_in["ssd_w_in"][q][:, 0:2048],
                "ssd_out": lambda: t_in["ssd_w_out"][q],
                "qkv": lambda: t_in["moba_w_qkv"][0],
                "wo": lambda: t_in["moba_w_o"][0],
                "lru_in": lambda: t_in["lru_w_in"][0],
                "lru_out": lambda: t_in["lru_w_out"][0],
                "up": lambda: t_in["mlp_w_up"][i],
                "down": lambda: t_in["mlp_w_down"][i],
                "gate": lambda: t_in["ple_w_gate"][i],
            }[name]()

        def sweep(eng, st, body, first=0, last=None):
            unroll = 8 if st["kq"] == 4 else 4
            n = st["n"] // unroll if last is None else last
            if st["g0"] == 0 and first == 0:
                body(0)
                first = 1
            if n - first == 1:
                body(first)
            elif n > first:
                with eng.Fori(first, n) as it:
                    body(it)

        def unroll_of(st):
            return 8 if st["kq"] == 4 else 4

        def barrier(eng, k):
            eng.drain().then_inc(s_bar, 1)
            eng.wait_ge(s_bar, 4 * (k + 1))

        def skewed(eng, n, front, back, mid=lambda g, b: None):
            front(0, 0)
            mid(0, 0)
            front(1, 1)
            back(0, 0)
            mid(1, 1)
            with eng.Fori(1, n // 2) as it:
                front(it * 2, 0)
                back(it * 2 - 1, 1)
                mid(it * 2, 0)
                front(it * 2 + 1, 1)
                back(it * 2, 0)
                mid(it * 2 + 1, 1)
            back(n - 1, 1)

        def mix_count(i):
            return sum(GROUPS if k in SSD_LAYERS else 1 for k in range(i + 1))

        def gain_col(n):
            return 96 if n == 3 * DEPTH else 32 * (n % 3) + KT * (n // 3)

        @block.sync
        def _(sp):
            def loads(st, first=0, last=None):
                w = weights(st)

                def body(it):
                    for u in range(unroll_of(st)):
                        r = it * unroll_of(st) + u
                        g = r + st["g0"]
                        if not (isinstance(g, int) and g < 4):
                            sp.wait_ge(s_lo, g - 3)
                        if st["kq"] == 1:
                            cols, kq = r * CHUNK, 0
                        else:
                            cols, kq = (it * (unroll_of(st) // st["kq"]) + u // st["kq"]) * CHUNK, u % st["kq"]
                        src = w[kq * D:(kq + 1) * D, ds(cols, CHUNK)]
                        sp.dma_start(raw[u % 4][:], src.rearrange("(k p) n -> p k n", p=P)).then_inc(s_raw[u % 4], 16)
                sweep(sp, st, body, first, last)

            outs = [0]

            def store(dst, src):
                outs[0] += 1
                sp.dma_start(dst, src).then_inc(s_out, 16)

            def stored():
                sp.wait_ge(s_out, 16 * outs[0])

            for i in range(DEPTH):
                q = i // 3
                if i in SSD_LAYERS:
                    loads(stage[i, "xbc"])
                    loads(stage[i, "z"])
                    loads(stage[i, "ssd_out"], 0, 1)
                    conv_p, conv_s = t_out["ssd_conv_p"][q], t_out["ssd_conv_s"][q]
                    sp.wait_ge(s_orE, 8 * (q + 1))
                    sp.dma_start(conv_p[0], orow["orow"][0:3, :]).then_inc(s_orD, 16)
                    sp.dma_start(conv_s[:, 2, :], orow["orow"][3:LAST, :]).then_inc(s_orD, 16)
                    store(conv_s[:, 0:2, :], t_in["state_ssd_conv"][q][:, 1:3, :])
                    dst = t_out["ssd_state_p"][q][0].rearrange("(i e) p n -> (e p) i n", e=2)

                    def put(g, b):
                        sp.wait_ge(s_yev, g + 1 + GROUPS * q)
                        sp.dma_start(dst[:, ds(g * 2, 2), :], grp[f"stout{b}"][:]).then_inc(s_sto[b], 16)
                    with sp.Fori(0, GROUPS // 2) as it:
                        put(it * 2, 0)
                        put(it * 2 + 1, 1)
                    sdst = t_out["ssd_state_s"][q].rearrange("b (i e) p n -> b (e p) i n", e=2)
                    with sp.Fori(0, NB // 4) as it:
                        for u in range(4):
                            sp.wait_ge(s_hn, it * 4 + (u + 1 + NB * q))
                            sp.dma_start(sdst[ds(it * 4 + u, 1)].rearrange("o p i n -> p (o i) n"),
                                         smp[f"st{u}"][:]).then_inc(s_sout[u], 16)
                    loads(stage[i, "ssd_out"], 1)
                elif i == 1:
                    loads(stage[i, "qkv"])
                    loads(stage[i, "wo"])
                    kp = t_out["k_p"][0][0].rearrange("(c t) h d -> h t c d", c=2)
                    vp = t_out["v_p"][0][0].rearrange("(c t) h d -> h t c d", c=2)
                    with sp.Fori(0, MH // 2) as it:
                        for b in range(2):
                            sp.wait_ge(s_msc, it * 2 + (b + 1))
                            hd = ds(it * 2 + b, 1)
                            sp.dma_start(kp[hd].rearrange("o t c d -> t (o c) d"), mh[f"kvt{b}"][:, 0:2]).then_inc(s_kst[b], 16)
                            sp.dma_start(vp[hd].rearrange("o t c d -> t (o c) d"), mh[f"kvt{b}"][:, 2:4]).then_inc(s_kst[b], 16)
                    store(t_out["k_s"][0].rearrange("b s h d -> b (s h d)"), M["rowS"][:, 1, :])
                    store(t_out["v_s"][0].rearrange("b s h d -> b (s h d)"), M["rowS"][:, 2, :])
                else:
                    loads(stage[i, "lru_in"])
                    loads(stage[i, "lru_out"])
                    sp.wait_ge(s_loE, 2)
                    store(t_out["lru_conv_p"][0][0], L["lrow"][0:3, :])
                    store(t_out["lru_conv_s"][0][:, 2, :], L["lrow"][3:LAST, :])
                    store(t_out["lru_conv_s"][0][:, 0:2, :], t_in["state_lru_conv"][0][:, 1:3, :])
                    store(t_out["lru_state_p"][0], L["hrow"][0:1, :])
                    store(t_out["lru_state_s"][0], L["hrow"][1:9, :])
                stored()
                if i in SSD_LAYERS:
                    sp.wait_ge(s_orD, 32 * (q + 1))
                    for b in range(2):
                        sp.wait_ge(s_sto[b], 8 * GROUPS * (q + 1))
                    for u in range(4):
                        sp.wait_ge(s_sout[u], 32 * (q + 1))
                if i == 1:
                    for b in range(2):
                        sp.wait_ge(s_kst[b], 32 * MH // 2)
                sp.nop().then_inc(s_stored, 1)
                loads(stage[i, "up"])
                loads(stage[i, "down"])
                loads(stage[i, "gate"])
            sp.wait_ge(s_finE, 2)
            store(t_out["y_p"][0].rearrange("(c t) d -> t c d", c=2), fin["yrow"][:])
            store(t_out["y_s"].rearrange("b s d -> (b s) d"), fin["yrow8"][:])
            stored()

        @block.tensor
        def _(pe):
            mm = nc.tensor.matmul

            def tr(out, in_, k):
                return nc.tensor.transpose(out, in_, ident[0:k, 0:k])

            def norm_sum(n, sqt):
                pe.wait_ge(s_ssq, n + 1)
                mm(bank[0][:, 0:T], ones[:], ssq[:], start=True, stop=True).then_inc(s_var, 1)

            def project(st, act_h, act_l, ready=None, after=None):
                kq_n = st["kq"]
                U = unroll_of(st)

                def body(it):
                    for u in range(U):
                        g = it * U + (u + st["g0"])
                        col = it * (U // kq_n) + (u // kq_n + st["c0"])
                        p, kq = ((u // kq_n) + st["c0"]) % 2, u % kq_n
                        pe.wait_ge(s_lo, g + 1)
                        if kq == 0 and not (isinstance(col, int) and col < 2):
                            pe.wait_ge(s_ev, col - 1)
                        if ready:
                            ready(u)
                        for m in range(2):
                            for k in range(KT):
                                w = slice(m * P, m * P + P)
                                x = kq * KT + k
                                first, last = kq == 0 and k == 0, kq == kq_n - 1 and k == KT - 1
                                o = G[p][:, m, 0:T]
                                mm(o, whi[u % 2][:, k, w], act_h[:, x, :], start=first, stop=False)
                                mm(o, wlo[u % 2][:, k, w], act_h[:, x, :], start=False, stop=False)
                                done = mm(o, whi[u % 2][:, k, w], act_l[:, x, :], start=False, stop=last)
                        done.then_inc(s_mm, 1)
                        if after:
                            after(u)
                sweep(nc.tensor, st, body)

            bar = [0]

            def phase():
                barrier(pe, bar[0])
                bar[0] += 1

            pe.wait_ge(s_const, 1)
            pe.wait_ge(s_load, 16 * 5)
            pe.wait_ge(s_load2, 16 * 13)
            for c in range(2):
                for k in range(KT):
                    tr(G[c][:, k // 4, (k % 4) * P:(k % 4 + 1) * P], A0["xrow"][:, c, k * P:(k + 1) * P], P)
            for k in range(KT):
                tr(bank[0][:, k * NB:(k + 1) * NB], A0["xrow8"][:, k * P:(k + 1) * P], NB)
            tr(bank[1][:, 0:104], A0["rowA"][:], 104)
            tr(bank[1][:, 128:224], A0["rowB"][:], 96)
            tr(bank[2][:, 0:128], A0["rowC"][:], P)
            tr(bank[2][:, 128:256], A0["rowD"][:], P)
            tr(bank[2][:, 256:320], A0["rowE"][:], 64).then_inc(s_tp0, 1)
            pe.wait_ge(s_init, 1)

            def x_ready(n):
                pe.wait_ge(s_xl, 2 * (n + 1))

            def ssd(i, q):
                phase()
                pe.wait_ge(s_cst, 16 * (q + 1))
                for k in range(CT):
                    t_ = tr(bank[2 + k // 16][:, (k % 16) * 24:(k % 16 + 1) * 24],
                            cst["cst"][:, k * P:(k + 1) * P], 24)
                t_.then_inc(s_cT, 1)
                x_ready(3 * i)
                norm_sum(3 * i, sq_mix)
                project(stage[i, "xbc"], xH, xL)
                pe.wait_ge(s_wdt, 16 * (q + 1))
                pe.wait_ge(s_cE, q + 1)
                for k in range(KT):
                    t_ = mm(bank[1][0:HEADS, 0:T], hv_["wdt"][:, k, :], xg[:, k, :], start=(k == 0), stop=(k == KT - 1))
                t_.then_inc(s_dtp, 1)
                pe.wait_ge(s_dt5, q + 1)
                for c in range(2):
                    tr(bank[2][:, c * HEADS:(c + 1) * HEADS], hv_["dt"][:, c * P:(c + 1) * P], HEADS)
                    tr(bank[2][:, (2 + c) * HEADS:(3 + c) * HEADS], hv2["acum"][:, c * P:(c + 1) * P], HEADS)
                    tr(bank[2][:, (4 + c) * HEADS:(5 + c) * HEADS], dte_["dte"][:, c * P:(c + 1) * P], HEADS)
                mm(bank[3][:, 0:XT * 17], evenodd[:], hv_["R"][:].rearrange("h i v -> h (i v)"),
                   start=True, stop=True).then_inc(s_dt6, 1)
                project(stage[i, "z"], xH, xL)
                pe.wait_ge(s_last, 16 * (q + 1))
                pe.wait_ge(s_ev, stage[i, "z"]["c0"] + 8)
                pe.wait_ge(s_th, q + 1)
                for k in range(CT):
                    t_ = tr(bank[k // 4][0:LAST, (k % 4) * P:(k % 4 + 1) * P], S["rawlast"][:, k, :], P)
                    if k % 4 == 3:
                        t_.then_inc(s_orT, 1)
                pe.wait_ge(s_orE, 8 * (q + 1))

                def front(g, b):
                    pe.wait_ge(s_stg, g + 1 + GROUPS * q)
                    if not (isinstance(g, int) and g == 0):
                        pe.wait_ge(s_xd, g + GROUPS * q)
                    stg = grp[f"stg{b}"]
                    for c in range(2):
                        for t in range(2):
                            tr(bank[0][:, (2 * c + t) * P:(2 * c + t + 1) * P], stg[:, t, c * P:(c + 1) * P], P)
                        tr(bank[1][:, c * P:(c + 1) * P], stg[:, 2, c * P:(c + 1) * P], P)
                    xc = Z["xbc"]
                    cg = xc[:, ds(g + 24, 1), 0:SEQ].rearrange("p o t -> p (o t)")
                    mm(bank[2][:, 0:SEQ], stg[:, 2, 0:P], cg, start=True, stop=True)
                    mm(bank[2][:, SEQ:3 * P], stg[:, 2, P:SEQ],
                       xc[:, ds(g + 24, 1), P:SEQ].rearrange("p o t -> p (o t)"), start=True, stop=True).then_inc(s_tp, 1)
                    pe.wait_ge(s_sel, g + 1 + GROUPS * q)
                    if not (isinstance(g, int) and g == 0):
                        pe.wait_ge(s_seg, g + GROUPS * q)
                    for r in range(4):
                        t_ = mm(G[0][:, r // 2, (r % 2) * SEQ:(r % 2 + 1) * SEQ], grp[f"sel{b}"][:, r, :], hv2["acum"][:],
                                start=True, stop=True)
                    t_.then_inc(s_ar, 1)

                def back(g, b):
                    pe.wait_ge(s_M, g + 1 + GROUPS * q)
                    pe.wait_ge(s_xde, g + 1 + GROUPS * q)
                    if not (isinstance(g, int) and g == 0):
                        pe.wait_ge(s_yev, g + GROUPS * q)
                    w, xd, xde = grp[f"seg{b}"], grp[f"xd{b}"], grp[f"xde{b}"]
                    for r in range(4):
                        o = G[1][64 * (r % 2):64 * (r % 2) + 64, r // 2, 0:SEQ]
                        mm(o, xd[:, 0, r, :], w[:, r, 0:SEQ], start=True, stop=False)
                        mm(G[1][64 * (r % 2):64 * (r % 2) + 64, r // 2, P:SEQ], xd[:, 1, r, :], w[:, r, SEQ:3 * P],
                           start=False, stop=True)
                    for t in range(2):
                        for c in range(2):
                            t_ = mm(G[1][:, t, SEQ:3 * P], xde[:, c, 2 * t:2 * t + 2, :].rearrange("s r p -> s (r p)"),
                                    grp[f"btm{b}"][:, c, :], start=(c == 0), stop=(c == 1), skip_group_check=True)
                    t_.then_inc(s_back, 1)
                skewed(nc.tensor, GROUPS, front, back)

                pe.wait_ge(s_yev, GROUPS * (q + 1))
                for k in range(16):
                    t_ = tr(bank[k // 4][0:NB, (k % 4) * P:(k % 4 + 1) * P], Z["xbc"][:, XT + k, SEQ:T], P)
                t_.then_inc(s_brT, 1)
                pe.wait_ge(s_brE, q + 1)
                with nc.tensor.Fori(0, NB // 2) as it:
                    for b in range(2):
                        pe.wait_ge(s_ssel, it * 2 + (b + 1 + NB * q))
                        pe.wait_ge(s_bcf, it * 2 + (b + (NB + 2) * q + 1))
                        for c in range(4):
                            t_ = mm(bank[4 * b + c], hv2[f"selS{b}"][:], bcr["bcrow"][:, c * 512:(c + 1) * 512],
                                    start=True, stop=True)
                        t_.then_inc(s_bc, 1)
                pe.wait_ge(s_ysq, q + 1)
                with nc.tensor.Fori(0, GROUPS // 2) as it:
                    for b in range(2):
                        pe.wait_ge(s_gs, it * 2 + (b + (GROUPS + 2) * q + 1))
                        for t in range(2):
                            t_ = mm(bank[b][:, 0:T], ones[:],
                                    ysq["ysq"][:, ds(it * 4 + (2 * b + t), 1), :].rearrange("p o t -> p (o t)"),
                                    start=(t == 0), stop=(t == 1))
                        t_.then_inc(s_gv, 1)
                pe.wait_ge(s_mixl, mix_count(i))
                project(stage[i, "ssd_out"], ysp["yH"], ysp["yL"])

            def moba():
                phase()
                x_ready(3)
                norm_sum(3, sq_mix)
                project(stage[1, "qkv"], xH, xL)

                def front(hh, b):
                    pe.wait_ge(s_stq, hh + 1)
                    if not (isinstance(hh, int) and hh == 0):
                        pe.wait_ge(s_msc, hh)
                    stq = mh[f"stq{b}"]
                    for j in range(4):
                        tr(bank[0][:, j * P:(j + 1) * P], stq[:, 1 + j // 2, (j % 2) * P:(j % 2 + 1) * P], P)
                    for j in range(3):
                        tr(bank[1][0:NB, j * P:(j + 1) * P], stq[:, j, SEQ:T], P)
                    mm(bank[2][:, 0:P], stq[:, 0, 0:P], stq[:, 1, 0:P], start=True, stop=True)
                    mm(bank[2][:, P:3 * P], stq[:, 0, P:SEQ], stq[:, 1, 0:SEQ], start=True, stop=True).then_inc(s_mtp, 1)

                def back(hh, b):
                    pe.wait_ge(s_mP, hh + 1)
                    if not (isinstance(hh, int) and hh == 0):
                        pe.wait_ge(s_mpt, hh)
                    for j in range(3):
                        t_ = tr(bank[3][:, j * P:(j + 1) * P], mh[f"sc{b}"][:, j * P:(j + 1) * P], P)
                    t_.then_inc(s_mpT, 1)
                    pe.wait_ge(s_mpt, hh + 1)
                    if not (isinstance(hh, int) and hh == 0):
                        pe.wait_ge(s_moe, hh)
                    mm(bank[4][:, 0:SEQ], mh[f"kvt{b}"][:, 2, :], mh[f"pt{b}"][:, 0:SEQ], start=True, stop=False)
                    mm(bank[4][:, P:SEQ], mh[f"kvt{b}"][:, 3, :], mh[f"pt{b}"][:, SEQ:3 * P],
                       start=False, stop=True).then_inc(s_mo, 1)
                skewed(nc.tensor, MH, front, back)
                pe.wait_ge(s_moe, MH)
                pe.wait_ge(s_qk, 1)
                mm(bank[4][0:64, 0:1], ms["qk"][:].rearrange("p b h -> p (b h)"), ones[:, 0:1],
                   start=True, stop=True).then_inc(s_sown, 1)
                with nc.tensor.Fori(0, NB // 2) as it:
                    for b in range(2):
                        pe.wait_ge(s_qsel, it * 2 + (b + 1))
                        pe.wait_ge(s_kd, it * 16 + (8 * b + 8))
                        for c in range(2):
                            t_ = mm(A[b][:, c, :], ms["qsel"][:], M["rowS"][:, 0, c * 512:(c + 1) * 512],
                                    start=True, stop=True)
                        t_.then_inc(s_qbc, 1)
                pe.wait_ge(s_kd, 17 + NB * PAGES)
                for j in range(PAGES):
                    t_ = tr(A[0][0:64, j // 4, (j % 4) * P:(j % 4 + 1) * P], ms["sS"][:, j, :], P)
                t_.then_inc(s_sT, 1)
                pe.wait_ge(s_sP, 1)
                for j in range(PAGES):
                    tr(bank[2][:, j * 64:(j + 1) * 64], ms["sR"][:, j * P:(j + 1) * P], 64)
                mm(bank[5][:, 0:64], ones[0:64, :], ms["dg"][:], start=True, stop=True)
                mm(bank[6][:, 0:64], ident[:], zeros[:], start=True, stop=False, skip_group_check=True).then_inc(s_sPT, 1)
                pe.wait_ge(s_sPTe, 1)
                with nc.tensor.Fori(0, NB) as it:
                    for j in range(PAGES):
                        pe.wait_ge(s_pg[j], it * 16 + (16 + 16 * NB))
                        for hh in range(MH):
                            t_ = mm(bank[6][:, ds(it * 8 + hh, 1)], pg[f"pg{j}"][:, hh, :],
                                    ms["pT8"][:, j, ds(it * 8 + hh, 1)], start=False, stop=False, skip_group_check=True)
                        t_.then_inc(s_vd, 1)
                pe.wait_ge(s_mixl, mix_count(1))
                project(stage[1, "wo"], xH, xL)

            def lru():
                phase()
                pe.wait_ge(s_lld, 16 * 4)
                for k in range(KT):
                    tr(bank[2][:, k * 24:(k + 1) * 24], L["lcst"][:, k * P:(k + 1) * P], 24)
                for k in range(KT):
                    t_ = tr(bank[2][:, 192 + k * 8:200 + k * 8], L["lst"][:, k * P:(k + 1) * P], 8)
                t_.then_inc(s_lT, 1)
                x_ready(6)
                norm_sum(6, sq_mix)
                project(stage[2, "lru_in"], xH, xL)
                pe.wait_ge(s_lTe, 1)
                for n in range(KT):
                    pe.wait_ge(s_lc, n + 1)
                    if n >= 2:
                        pe.wait_ge(s_lth, n - 1)
                    mm(A[n % 2][:, 0, 0:T], L["wax"][:, n, :], L["xc"][:, n, :], start=True, stop=True)
                    mm(A[n % 2][:, 1, 0:T], L["wax"][:, 8 + n, :], L["xc"][:, n, :], start=True, stop=True).then_inc(s_lg, 1)
                pe.wait_ge(s_ly, 1)
                pe.wait_ge(s_lth, KT)
                for k in range(KT):
                    tr(A[0][0:LAST, k // 4, (k % 4) * P:(k % 4 + 1) * P], L["XR"][:, k, 256:256 + LAST], P)
                for k in range(KT):
                    t_ = tr(A[1][0:9, k // 4, (k % 4) * P:(k % 4 + 1) * P], L["hs"][:, k, 255:T], P)
                t_.then_inc(s_loT, 1)
                pe.wait_ge(s_mixl, mix_count(2))
                project(stage[2, "lru_out"], xH, xL)

            def mlp_ple(i):
                phase()
                x_ready(3 * i + 1)
                norm_sum(3 * i + 1, sq)
                project(stage[i, "up"], xH, xL)

                pe.wait_ge(s_ple, 48 * (i + 1))
                pe.wait_ge(s_std, 3 * i + 2)
                for k in range(2):
                    for c in range(2):
                        tr(A[0][:, k, c * P:(c + 1) * P], ml["prow"][:, c, k * P:(k + 1) * P], P)
                    t_ = tr(A[0][:, k, SEQ:T], ml["prow8"][:, k * P:(k + 1) * P], NB)
                t_.then_inc(s_pT, 1)

                def acts(u):
                    if u < 4:
                        pe.wait_ge(s_aL, 16 * i + 4 * (u + 1))
                project(stage[i, "down"], aH, aL, ready=acts)
                pe.wait_ge(s_pTe, i + 1)
                x_ready(3 * i + 2)
                norm_sum(3 * i + 2, sq)

                def proj(u):
                    if u == 0:
                        pe.wait_ge(s_std, 3 * i + 3)
                    if u >= 2:
                        pe.wait_ge(s_pje, 4 * i + u - 1)
                    for m in range(2):
                        for k in range(2):
                            t_ = mm(A[u % 2][:, m, 0:T], ml["wp"][:, k, (2 * u + m) * P:(2 * u + m + 1) * P],
                                    ml["pT"][:, k, :], start=(k == 0), stop=(k == 1))
                    t_.then_inc(s_pj, 1)
                project(stage[i, "gate"], xH, xL, after=proj)

            for i in range(DEPTH):
                if i in SSD_LAYERS:
                    ssd(i, i // 3)
                elif i == 1:
                    moba()
                else:
                    lru()
                mlp_ple(i)
            phase()
            pe.wait_ge(s_ssq, 13)
            norm_sum(12, None)
            pe.wait_ge(s_fin, 1)
            for c in range(2):
                for k in range(KT):
                    tr(G[c][:, k // 4, (k % 4) * P:(k % 4 + 1) * P], fin["yfin"][:, k, c * P:(c + 1) * P], P)
            for k in range(KT):
                t_ = tr(A[1][0:NB, k // 4, (k % 4) * P:(k % 4 + 1) * P], fin["yfin"][:, k, SEQ:T], P)
            t_.then_inc(s_finT, 1)

        @block.scalar
        def _(act):
            fn = nc.scalar.activation

            def split(st, it, u):
                U = unroll_of(st)
                g = it * U + (u + st["g0"])
                if isinstance(g, int) and g + 2 >= total:
                    return
                turn = it * (U // 4) + (st["g0"] // 4 + (u + 2) // 4)
                act.wait_ge(s_raw[(u + 2) % 4], turn * 16 + 16)
                act.wait_ge(s_mm, g + 1)
                fn(whi[u % 2][:], raw[(u + 2) % 4][:], ACT.Copy).then_inc(s_hi, 1)

            def splits(st, evac=None):
                def body(it):
                    for u in range(unroll_of(st)):
                        split(st, it, u)
                        if evac:
                            evac(it * unroll_of(st) + u, u)
                sweep(nc.scalar, st, body)

            def norm(n, sqt, gain=True):
                if gain:
                    for half in range(2):
                        act.wait_ge(s_xg, 2 * n + half + 1)
                        s4 = slice(4 * half, 4 * half + 4)
                        fn(xH[:, s4], xg[:, s4], ACT.Copy).then_inc(s_xh, 1)
                else:
                    act.wait_ge(s_xg, 2 * n + 1)
                fn(sqt[:], h[:], ACT.Square).then_inc(s_sq, 1)
                act.wait_ge(s_var, n + 1)
                fn(std[:], bank[0][:, 0:T], ACT.Sqrt, scale=1.0 / D, bias=epsc[:, 0:1]).then_inc(s_std, 1)

            bar = [0]

            def phase():
                barrier(act, bar[0])
                bar[0] += 1

            def stored(i):
                act.wait_ge(s_stored, i + 1)

            for dst, src in (
                (A0["xrow"][:], t_in["x_prompt"][0].rearrange("(c t) d -> t c d", c=2)),
                (A0["xrow8"][:], t_in["x_sample"].rearrange("b s d -> (b s) d")),
                (A0["rowC"][:], t_in["ssd_conv_w"][0].rearrange("k (j p) -> (k j) p", p=P)),
                (A0["rowD"][:], t_in["ssd_conv_w"][1].rearrange("k (j p) -> (k j) p", p=P)),
                (A0["rowE"][:], t_in["ssd_conv_b"].rearrange("q (j p) -> (q j) p", p=P)),
            ):
                act.dma_start(dst, src).then_inc(s_load, 16)
            at_row = 0
            for name in ("norm_mix", "norm_mlp", "norm_ple"):
                act.dma_start(A0["rowA"][at_row:at_row + 32, :], t_in[name].rearrange("i (k p) -> (i k) p", p=P)).then_inc(s_load2, 16)
                at_row += 32
            act.dma_start(A0["rowA"][96:104, :], t_in["norm_final"].rearrange("(k p) -> k p", p=P)).then_inc(s_load2, 16)
            act.dma_start(A0["rowB"][0:32, :], t_in["lru_conv_w"][0].rearrange("k (j p) -> (k j) p", p=P)).then_inc(s_load2, 16)
            act.dma_start(A0["rowB"][32:40, :], t_in["lru_conv_b"][0].rearrange("(k p) -> k p", p=P)).then_inc(s_load2, 16)
            act.dma_start(A0["rowB"][40:48, :], t_in["lru_lambda"][0].rearrange("(k p) -> k p", p=P)).then_inc(s_load2, 16)
            act.dma_start(A0["rowB"][48:56, :], t_in["lru_b_a"][0]).then_inc(s_load2, 16)
            act.dma_start(A0["rowB"][56:64, :], t_in["lru_b_x"][0]).then_inc(s_load2, 16)
            act.dma_start(A0["rowB"][64:96, :], t_in["ssd_norm"].rearrange("q (j p) -> (q j) p", p=P)).then_inc(s_load2, 16)
            for k, name in enumerate(("ssd_dt_bias", "ssd_a_log", "ssd_d")):
                act.dma_start(hsm[:, 2 * k:2 * k + 2], t_in[name].rearrange("q h -> h q"), allow_slow_non_contiguous=True).then_inc(s_load2, 16)
            for u in range(2):
                act.wait_ge(s_raw[u], 16)
                fn(whi[u][:], raw[u][:], ACT.Copy).then_inc(s_hi, 1)

            def ssd(i, q):
                phase()
                norm(3 * i, sq_mix["sqm"])
                xbc, zs, seq = Z["xbc"], Z["zs"], slice(0, SEQ)
                c0 = stage[i, "xbc"]["c0"]

                def tap(r, u):
                    act.wait_ge(s_ev, r + (c0 + 1))
                    for t in range(2):
                        tile = r * 2 + t
                        f = fn(xbc[:, ds(tile, 1), seq].rearrange("p o t -> p (o t)"), S[f"T{u % 2}"][:, t, seq], ACT.Identity,
                               bias=colE[:, ds(tile + CT * q, 1)], scale=colC[:, q, ds(tile, 1)])
                    f.then_inc(s_tap, 1)
                splits(stage[i, "xbc"], tap)
                act.wait_ge(s_dt1, q + 1)
                fn(spl["sp2"][:], spl["sp1"][:], ACT.Exp)
                fn(hv2["bvec"][:, 0:1], hsm[:, 2 + q:3 + q], ACT.Exp).then_inc(s_dt2, 1)
                act.wait_ge(s_dt3, q + 1)
                fn(hv2["vals"][:, 8:16], hv_["dA"][:, SEQ:T], ACT.Exp)
                fn(dte_["dte"][:], hv2["acum"][:], ACT.Exp, scale=-1.0, bias=hv2["acum"][:, SEQ - 1:SEQ]).then_inc(s_dt4, 1)
                act.wait_ge(s_conv, 16 * (q + 1))
                act.wait_ge(s_last, 16 * (q + 1))
                z0 = stage[i, "z"]["c0"]

                def silus(r, u):
                    b = u % 2
                    act.wait_ge(s_ev, r + (z0 + 1))
                    fn(S[f"T{b}"][:, :, 0:T], zs[:, ds(r * 2, 2), :], ACT.Tanh, scale=0.5).then_inc(s_zth, 1)
                    if not (isinstance(r, int) and r < 2 and q == 0):
                        act.wait_ge(s_silu, r + (8 * q - 1))
                    fn(xth[f"xth{b}"][:], xbc[:, ds(r * 4, 4), :], ACT.Tanh).then_inc(s_xth, 1)
                z = stage[i, "z"]
                def z_body(it):
                    for u in range(4):
                        split(z, it, u)
                        silus(it * 4 + u, u)
                z_body(0)
                z_body(1)
                for k in range(0, 8, 2):
                    act.wait_ge(s_orT, 8 * q + k + 1)
                    fn(orow["orow"][:, k * 512:(k + 1) * 512], bank[k][0:LAST, :], ACT.Copy).then_inc(s_orE, 1)

                act.wait_ge(s_orD, 32 * (q + 1))

                def group(g, b):
                    if not isinstance(g, int):
                        act.wait_ge(s_tp, g + (GROUPS * q - 1))
                    fn(grp[f"stg{b}"][:, 0:2, :], xbc[:, ds(g * 2, 2), seq], ACT.Copy)
                    fn(grp[f"stg{b}"][:, 2, :], xbc[:, ds(g + XT, 1), seq].rearrange("p o t -> p (o t)"), ACT.Copy).then_inc(s_stg, 1)
                    act.wait_ge(s_seg, g + (GROUPS * q + 1))
                    fn(grp[f"seg{b}"][:], grp[f"seg{b}"][:], ACT.Exp).then_inc(s_exp, 1)
                group(0, 0)
                group(1, 1)
                with nc.scalar.Fori(1, GROUPS // 2) as it:
                    group(it * 2, 0)
                    group(it * 2 + 1, 1)
                with nc.scalar.Fori(0, NB // 4) as it:
                    for u in range(4):
                        act.wait_ge(s_sin[u], it * 16 + (16 + 32 * q))
                        st_ = smp[f"st{u}"]
                        for t in range(XT):
                            f = fn(st_[:, t, :], st_[:, t, :], ACT.Copy, scale=hv2["hv"][:, t, ds(it * 4 + (8 + u), 1)])
                        f.then_inc(s_hd, 1)
                act.wait_ge(s_yz, q + 1)
                fn(ysq["ysq"][:], zs[:], ACT.Square).then_inc(s_ysq, 1)
                for u in range(4):
                    act.wait_ge(s_sout[u], 32 * (q + 1))

                with nc.scalar.Fori(0, GROUPS // 2) as it:
                    for b in range(2):
                        g = it * 2 + b
                        act.wait_ge(s_gv, g + (GROUPS * q + 1))
                        fn(gnb[f"gstd{b}"][:], bank[b][:, 0:T], ACT.Sqrt, scale=1.0 / 256, bias=epsc[:, 0:1]).then_inc(s_gs, 1)
                        act.wait_ge(s_yn, g + (GROUPS * q + 1))
                        fn(ysp["yH"][:, ds(g * 2, 2), :], gnb[f"yn{b}"][:], ACT.Copy).then_inc(s_yh, 1)
                splits(stage[i, "ssd_out"])

            def moba():
                phase()
                norm(3, sq_mix["sqm"])
                splits(stage[1, "qkv"])
                act.wait_ge(s_ev, stage[1, "qkv"]["c0"] + 12)
                heads = M["qkv"][:].rearrange("p (j t) x -> p j t x", j=3)

                def front(hh, b):
                    if not (isinstance(hh, int) and hh < 2):
                        act.wait_ge(s_mtp, hh - 1)
                    fn(mh[f"stq{b}"][:], heads[:, :, ds(hh, 1), :].rearrange("p j o x -> p (j o) x"), ACT.Copy).then_inc(s_stq, 1)

                def back(hh, b):
                    act.wait_ge(s_mpT, hh + 1)
                    if not (isinstance(hh, int) and hh < 2):
                        act.wait_ge(s_mo, hh - 1)
                    fn(mh[f"pt{b}"][:], bank[3][:, 0:3 * P], ACT.Copy).then_inc(s_mpt, 1)

                def mid(hh, b):
                    act.wait_ge(s_msc, hh + 1)
                    sc, nm, rs = mh[f"sc{b}"], mh[f"nm{b}"], mh[f"rs{b}"]
                    fn(sc[:, 0:P], sc[:, 0:P], ACT.Exp, scale=SCALE, bias=nm[:, 0:1], accum_out=rs[:, 0:1])
                    fn(sc[:, P:3 * P], sc[:, P:3 * P], ACT.Exp, scale=SCALE, bias=nm[:, 1:2], accum_out=rs[:, 1:2]).then_inc(s_mex, 1)
                skewed(nc.scalar, MH, front, back, mid)
                act.wait_ge(s_sR, 1)
                fn(ms["sR"][:, 0:1025], ms["sR"][:, 0:1025], ACT.Exp, scale=SCALE, bias=ms["gsc"][:, 2:3],
                   accum_out=ms["gsc"][:, 3:4]).then_inc(s_sE, 1)
                act.wait_ge(s_att, 1)
                fn(xH[:], M["att"][:], ACT.Copy).then_inc(s_mixh, 1)
                splits(stage[1, "wo"])

            def lru():
                phase()
                act.wait_ge(s_lsp, 1)
                fn(lsp["lp2"][:], lsp["lp1"][:], ACT.Exp).then_inc(s_lse, 1)
                norm(6, sq_mix["sqm"])
                st = stage[2, "lru_in"]
                for it in range(2):
                    for u in range(4):
                        split(st, it, u)
                act.wait_ge(s_ev, st["c0"] + 8)
                XR, xc = L["XR"], L["xc"]
                for k in range(KT):
                    f = fn(xc[:, k, 0:SEQ], XR[:, k, 0:SEQ], ACT.Identity, bias=colB[:, 32 + k:33 + k], scale=colB[:, k:k + 1])
                    f.then_inc(s_lt0, 1)
                for k in range(KT):
                    act.wait_ge(s_lg, k + 1)
                    fn(L["thr"][:, k, :], A[k % 2][:, 0, 0:T], ACT.Tanh, scale=0.5, bias=L["bah"][:, k:k + 1])
                    fn(L["thi"][:, k, :], A[k % 2][:, 1, 0:T], ACT.Tanh, scale=0.5, bias=L["bxh"][:, k:k + 1]).then_inc(s_lth, 1)
                act.wait_ge(s_lla, 1)
                fn(L["thr"][:], L["la"][:], ACT.Tanh, scale=-1.0).then_inc(s_la, 1)
                fn(L["la"][:], L["la"][:], ACT.Exp).then_inc(s_la, 1)
                act.wait_ge(s_lgl, 1)
                fn(L["xc"][:], L["xc"][:], ACT.Tanh, scale=GELU_A).then_inc(s_lgt, 1)
                act.wait_ge(s_lv, 1)
                fn(L["thr"][:], L["thr"][:], ACT.Sqrt, scale=2.0).then_inc(s_lsq, 1)
                act.wait_ge(s_ly, 1)
                fn(xH[:], L["xc"][:], ACT.Copy).then_inc(s_mixh, 1)
                splits(stage[2, "lru_out"])

            def mlp_ple(i):
                stored(i)
                phase()
                norm(3 * i + 1, sq)
                c0 = stage[i, "up"]["c0"]

                def square(r, u):
                    b = u % 2
                    act.wait_ge(s_mm, r + (stage[i, "up"]["g0"] + 1))
                    if not (isinstance(r, int) and r < 2 and i == 0):
                        act.wait_ge(s_ac, r + (16 * i - 1))
                    fn(ml[f"rl{b}"][:], G[b][:, :, 0:T], ACT.Relu).then_inc(s_ev, 1)
                    act.wait_ge(s_ev, r + (c0 + 1))
                    fn(aH[:, ds(r * 2, 2), :], ml[f"rl{b}"][:], ACT.Square).then_inc(s_aH, 1)

                def up_body(it):
                    for u in range(4):
                        split(stage[i, "up"], it, u)
                        square(it * 4 + u, u)
                up_body(0)
                with nc.scalar.Fori(1, 4) as it:
                    up_body(it)
                splits(stage[i, "down"])
                norm(3 * i + 2, sq)
                g0 = stage[i, "gate"]["c0"]
                for u in range(4):
                    split(stage[i, "gate"], 0, u)
                    act.wait_ge(s_ev, g0 + u + 1)
                    fn(ml["t1"][:], ml["t1"][:], ACT.Tanh, scale=0.5).then_inc(s_tg, 1)

            for i in range(DEPTH):
                if i in SSD_LAYERS:
                    ssd(i, i // 3)
                elif i == 1:
                    moba()
                else:
                    lru()
                mlp_ple(i)
            phase()
            norm(12, sq, gain=False)
            act.wait_ge(s_finT, 1)
            fn(fin["yrow"][:, 0, :], G[0][:].rearrange("p a b -> p (a b)"), ACT.Copy)
            fn(fin["yrow8"][:], A[1][0:NB].rearrange("p a b -> p (a b)"), ACT.Copy).then_inc(s_finE, 1)

        @block.gpsimd
        def _(pool):
            gp = nc.gpsimd
            gp.memset(ident[:], 0.0)
            gp.memset(ones[:], 1.0)
            gp.memset(zeros[:], 0.0)
            gp.memset(tri[:], 1.0)
            gp.memset(amask[:], 0.0)
            gp.memset(epsc[:], EPS)
            for n in range(BLOCKS):
                gp.memset(blockno[:, n:n + 1], float(n + 1))
            pool.drain()
            gp.affine_select(out=ident[:], in_=ident[:], compare_op=ALU.not_equal, fill=1.0, base=0,
                             pattern=[[-1, P]], channel_multiplier=1)
            for blk in (0, 2):
                c = slice(blk * P, blk * P + P)
                gp.affine_select(out=tri[:, c], in_=tri[:, c], compare_op=ALU.is_ge, fill=0.0, base=0,
                                 pattern=[[1, P]], channel_multiplier=-1)
                f = gp.affine_select(out=amask[:, c], in_=amask[:, c], compare_op=ALU.is_ge, fill=-BIG, base=0,
                                     pattern=[[-1, P]], channel_multiplier=1)
            f.then_inc(s_const, 1)

            bar = [0]

            def phase():
                barrier(pool, bar[0])
                bar[0] += 1

            def ssd(i, q):
                phase()
                pool.dma_start(cst["cst"][:], t_in["state_ssd_conv"][q].rearrange("b k c -> (b k) c")).then_inc(s_cst, 16)
                pool.wait_ge(s_cE, q + 1)
                pool.dma_start(hv_["wdt"][:], t_in["ssd_w_in"][q][:, 2048 + CONVD:].rearrange("(k p) n -> p k n", p=P)).then_inc(s_wdt, 16)
                c0 = stage[i, "xbc"]["c0"]

                def keep(r, b):
                    pool.wait_ge(s_ev, r + (c0 + 1))
                    gp.tensor_copy(S["rawlast"][:, ds(r * 2, 2), :], S[f"T{b}"][:, :, SEQ:SEQ + LAST]).then_inc(s_last, 1)
                with gp.Fori(0, 8) as it:
                    keep(it * 2, 0)
                    keep(it * 2 + 1, 1)
                pool.wait_ge(s_orD, 32 * (q + 1))

                def group(g, b):
                    if not isinstance(g, int):
                        pool.wait_ge(s_ar, g + (GROUPS * q - 1))
                    gp.tensor_copy(grp[f"sel{b}"][:], ident[0:HEADS, ds(g * 4, 4)].unsqueeze(2).to_broadcast([HEADS, 4, P])).then_inc(s_sel, 1)
                    pool.wait_ge(s_xd, g + (GROUPS * q + 1))
                    if not isinstance(g, int):
                        pool.wait_ge(s_back, g + (GROUPS * q - 1))
                    for c in range(2):
                        f = gp.tensor_tensor(grp[f"xde{b}"][:, c], grp[f"xd{b}"][:, c],
                                             hv2["tm"][:, 4 + c, ds(g * 4, 4)].unsqueeze(2).to_broadcast([P, 4, 64]), ALU.mult)
                    f.then_inc(s_xde, 1)
                group(0, 0)
                group(1, 1)
                with gp.Fori(1, GROUPS // 2) as it:
                    group(it * 2, 0)
                    group(it * 2 + 1, 1)
                pool.wait_ge(s_yev, GROUPS * (q + 1))
                for b in range(2):
                    pool.wait_ge(s_sto[b], 8 * GROUPS * (q + 1))
                src = t_in["state_ssd"][q].rearrange("b (i e) p n -> b (e p) i n", e=2)
                for turn in range(NB // 4):
                    for u in range(4):
                        b = 4 * turn + u
                        if turn:
                            pool.wait_ge(s_sout[u], 16 * turn + 32 * q)
                            pool.wait_ge(s_bcf, (NB + 2) * q + b - 1)
                        pool.dma_start(smp[f"st{u}"][:], src[b]).then_inc(s_sin[u], 16)
                    for u in range(4):
                        b = 4 * turn + u
                        if b >= 2:
                            pool.wait_ge(s_bc, NB * q + b - 1)
                        gp.tensor_copy(hv2[f"selS{b % 2}"][:], ident[0:NB, b:b + 1].to_broadcast([NB, P])).then_inc(s_ssel, 1)

            def moba():
                phase()
                pool.dma_start(ptab[:], t_in["page_table"].rearrange("b j -> (b j)").unsqueeze(0)).then_inc(s_tab, 16)
                pool.wait_ge(s_tab, 16)

                def page(pool_dram, n, j):
                    pid = pool.value_load(ptab[0:1, ds(n * PAGES + j, 1)], min_val=0, max_val=pool_dram.shape[1] - 1)
                    pool.dma_start(pg[f"pg{j}"][:], pool_dram[0][ds(pid, 1)].rearrange("o t h d -> t (o h) d")).then_inc(s_pg[j], 16)

                def selq(n):
                    gp.tensor_copy(ms["qsel"][:], ident[0:NB, ds(n, 1)].to_broadcast([NB, P])).then_inc(s_qsel, 1)
                for j in range(PAGES):
                    page(t_in["cache_k"], 0, j)
                pool.wait_ge(s_qk, 1)
                selq(0)
                with gp.Fori(1, NB) as it:
                    pool.wait_ge(s_qbc, it)
                    selq(it)
                    for j in range(PAGES):
                        pool.wait_ge(s_kd, it * 8 + (16 - 8 + j + 1))
                        page(t_in["cache_k"], it, j)
                for j in range(PAGES):
                    pool.wait_ge(s_kd, 16 + 8 * (NB - 1) + j + 1)
                    page(t_in["cache_v"], 0, j)
                with gp.Fori(1, NB) as it:
                    for j in range(PAGES):
                        pool.wait_ge(s_vd, it * 8 + (j - 7))
                        page(t_in["cache_v"], it, j)

            def lru():
                phase()
                pool.dma_start(L["lcst"][:], t_in["state_lru_conv"][0].rearrange("b k c -> (b k) c")).then_inc(s_lld, 16)
                pool.dma_start(L["lst"][:], t_in["state_lru"][0]).then_inc(s_lld, 16)
                pool.dma_start(L["wax"][:, 0:8, :], t_in["lru_w_a"][0].rearrange("n c d -> c n d")).then_inc(s_lld, 16)
                pool.dma_start(L["wax"][:, 8:16, :], t_in["lru_w_x"][0].rearrange("n c d -> c n d")).then_inc(s_lld, 16)

            def mlp_ple(i):
                phase()
                pool.dma_start(ml["wp"][:], t_in["ple_w_proj"][i].rearrange("(k p) n -> p k n", p=P)).then_inc(s_ple, 16)
                pool.dma_start(ml["prow"][:], t_in["p_prompt"][i][0].rearrange("(c t) d -> t c d", c=2)).then_inc(s_ple, 16)
                pool.dma_start(ml["prow8"][:], t_in["p_sample"][i].rearrange("b s d -> (b s) d")).then_inc(s_ple, 16)
                c0 = stage[i, "up"]["c0"]

                def square(r, b):
                    pool.wait_ge(s_ev, r + (c0 + 1))
                    if not (isinstance(r, int) and r < 2 and i == 0):
                        pool.wait_ge(s_aL, r + (16 * i - 1))
                    gp.tensor_tensor(ml[f"ac{b}"][:], ml[f"rl{b}"][:], ml[f"rl{b}"][:], ALU.mult).then_inc(s_ac, 1)
                square(0, 0)
                square(1, 1)
                with gp.Fori(1, 8) as it:
                    square(it * 2, 0)
                    square(it * 2 + 1, 1)

            for i in range(DEPTH):
                if i in SSD_LAYERS:
                    ssd(i, i // 3)
                elif i == 1:
                    moba()
                else:
                    lru()
                mlp_ple(i)
            phase()

        @block.vector
        def _(dve):
            V = nc.vector

            def split(st, it, u):
                g = it * unroll_of(st) + (u + st["g0"])
                if isinstance(g, int) and g + 2 >= total:
                    return
                dve.wait_ge(s_hi, g + 3)
                V.tensor_tensor(wlo[u % 2][:], raw[(u + 2) % 4][:], whi[u % 2][:].bitcast(F32), ALU.subtract).then_inc(s_lo, 1)

            def evacs(st, evac, first=None):
                kq_n, U = st["kq"], unroll_of(st)

                def body(it):
                    for u in range(U):
                        g = it * U + (u + st["g0"])
                        r = it * (U // kq_n) + u // kq_n
                        p = (u // kq_n + st["c0"]) % 2
                        whole = u % kq_n == kq_n - 1
                        if first and whole:
                            dve.wait_ge(s_mm, g + 1)
                            first(r, p)
                        split(st, it, u)
                        if whole:
                            if not first:
                                dve.wait_ge(s_mm, g + 1)
                            evac(r, p)
                sweep(V, st, body)

            def bc(ap, n):
                return ap.unsqueeze(1).to_broadcast([ap.shape[0], n, ap.shape[1]])

            def norm(n, sqt, gain=True):
                col = gain_col(n)
                if gain:
                    for half in range(2):
                        for k in range(4 * half, 4 * half + 4):
                            f = V.tensor_scalar(xg[:, k, :], h[:, k, :], colA[:, col + k:col + k + 1], None, ALU.mult)
                        f.then_inc(s_xg, 1)
                    for half in range(2):
                        dve.wait_ge(s_xh, 2 * n + half + 1)
                        s4 = slice(4 * half, 4 * half + 4)
                        V.tensor_tensor(xL[:, s4], xg[:, s4], xH[:, s4].bitcast(F32), ALU.subtract).then_inc(s_xl, 1)
                else:
                    dve.nop().then_inc(s_xg, 1)
                dve.wait_ge(s_sq, n + 1)
                V.tensor_reduce(ssq[:], sqt[:].rearrange("p k t -> p t k"), AX, ALU.add).then_inc(s_ssq, 1)
                dve.wait_ge(s_std, n + 1)
                V.reciprocal(rstd[:], std[:])
                dve.drain()
                if n % 3 == 1:
                    V.tensor_tensor(rstd2[:], rstd[:], rstd[:], ALU.mult)
                    dve.drain()

            bar = [0]

            def phase():
                barrier(dve, bar[0])
                bar[0] += 1

            def softplus(x, e, t, z, z2, out):
                V.tensor_scalar(t, e, 2.0, None, ALU.add)
                dve.drain()
                V.reciprocal(z, t)
                dve.drain()
                V.tensor_tensor(z, z, e, ALU.mult)
                dve.drain()
                V.tensor_tensor(z2, z, z, ALU.mult)
                V.tensor_scalar(x, x, 0.0, None, ALU.max)
                dve.drain()
                V.tensor_scalar(t, z2, 1.0 / 17, None, ALU.mult)
                for k in (15, 13, 11, 9, 7, 5, 3):
                    dve.drain()
                    V.scalar_tensor_tensor(t, t, 1.0 / k, z2, ALU.add, ALU.mult)
                dve.drain()
                V.scalar_tensor_tensor(t, t, 1.0, z, ALU.add, ALU.mult)
                dve.drain()
                V.scalar_tensor_tensor(out, t, 2.0, x, ALU.mult, ALU.add)
                dve.drain()

            dve.wait_ge(s_const, 1)
            V.tensor_reduce(pairsel[:], ident[0:HEADS, 0:HEADS].rearrange("h (i e) -> h i e", e=2), AX, ALU.add)
            eo = ident[0:HEADS, 0:HEADS].rearrange("h (i e) -> h e i", e=2)
            V.tensor_reduce(eo2[:], eo, AX, ALU.add)
            dve.drain()
            V.tensor_copy(evenodd[:].rearrange("h (e p) -> h e p", e=2), eo2[:].unsqueeze(2).to_broadcast([HEADS, 2, 64]))
            for u in range(2):
                dve.wait_ge(s_hi, u + 1)
                V.tensor_tensor(wlo[u][:], raw[u][:], whi[u][:].bitcast(F32), ALU.subtract).then_inc(s_lo, 1)
            dve.wait_ge(s_tp0, 1)
            for c in range(2):
                V.tensor_copy(h[:, :, c * P:(c + 1) * P], G[c][:].rearrange("p a (k t) -> p (a k) t", t=P))
            V.tensor_copy(h[:, :, SEQ:T], bank[0][:, 0:KT * NB].rearrange("p (k b) -> p k b", b=NB))
            V.tensor_copy(colA[:], bank[1][:, 0:104])
            V.tensor_copy(colB[:], bank[1][:, 128:224])
            V.tensor_scalar(colC[:], bank[2][:, 0:256].rearrange("p (q c) -> p q c", q=2), 0.5, None, ALU.mult)
            V.tensor_scalar(colE[:], bank[2][:, 256:320], 0.5, None, ALU.mult).then_inc(s_init, 1)
            dve.drain()

            def add_h(r, p):
                hr = h[:, ds(r * 2, 2), :]
                V.tensor_tensor(hr, hr, G[p][:, :, 0:T], ALU.add).then_inc(s_ev, 1)

            def ssd(i, q):
                phase()
                xbc, zs, seq, smpl = Z["xbc"], Z["zs"], slice(0, SEQ), slice(SEQ, T)
                for b in range(2):
                    V.memset(S[f"T{b}"][:, :, 0:3], 0.0)
                norm(3 * i, sq_mix["sqm"])
                dve.wait_ge(s_cT, q + 1)
                stT, cp = cstT["stT"], cprod["cprod"]
                for a in range(2):
                    V.tensor_copy(stT[:, 16 * a:16 * a + 16, :], bank[2 + a][:, 0:384].rearrange("p (t s) -> p t s", s=24))
                dve.drain()
                for k in range(3):
                    V.tensor_tensor(cp[:, :, :, k], stT[:].rearrange("p t (b k) -> p t b k", k=3)[:, :, :, k],
                                    colC[:, q, k * CT:(k + 1) * CT].unsqueeze(2).to_broadcast([P, CT, NB]), ALU.mult)
                dve.drain()
                V.tensor_reduce(S["spre"][:], cp[:], AX, ALU.add)
                dve.drain()
                V.tensor_tensor(S["spre"][:], S["spre"][:], colE[:, q * CT:(q + 1) * CT].unsqueeze(2).to_broadcast([P, CT, NB]), ALU.add).then_inc(s_cE, 1)
                dve.drain()

                def raw_out(r, p):
                    if not (isinstance(r, int) and r < 2 and q == 0):
                        dve.wait_ge(s_tap, r + (16 * q - 1))
                        dve.wait_ge(s_last, r + (16 * q - 1))
                    V.tensor_tensor(S[f"T{p}"][:, :, 3:3 + T], G[p][:, :, 0:T], bc(rstd[:], 2), ALU.mult).then_inc(s_ev, 1)

                def taps(r, p):
                    dve.wait_ge(s_tap, r + (16 * q + 1))
                    T_ = S[f"T{p}"]
                    for k in range(1, CW):
                        for t in range(2):
                            tile = r * 2 + t
                            o = xbc[:, ds(tile, 1), seq].rearrange("p o t -> p (o t)")
                            V.scalar_tensor_tensor(o, T_[:, t, k:k + SEQ], colC[:, q, ds(tile + k * CT, 1)], o, ALU.mult, ALU.add)
                        dve.drain()
                    for t in range(2):
                        tile = r * 2 + t
                        f = V.scalar_tensor_tensor(xbc[:, ds(tile, 1), smpl].rearrange("p o t -> p (o t)"), T_[:, t, 3 + SEQ:3 + T],
                                                   colC[:, q, ds(tile + 3 * CT, 1)],
                                                   S["spre"][:, ds(tile, 1), :].rearrange("p o b -> p (o b)"), ALU.mult, ALU.add)
                    f.then_inc(s_conv, 1)
                evacs(stage[i, "xbc"], taps, raw_out)
                sp = [spl[f"sp{k}"][:] for k in range(6)]
                dve.wait_ge(s_dtp, q + 1)
                V.tensor_tensor(sp[0], bank[1][0:HEADS, 0:T], rstd[0:HEADS, :], ALU.mult)
                dve.drain()
                V.tensor_scalar(sp[0], sp[0], hsm[:, q:q + 1], None, ALU.add)
                dve.drain()
                V.scalar_tensor_tensor(sp[1], sp[0], -1.0, sp[0], ALU.mult, ALU.min).then_inc(s_dt1, 1)
                dve.wait_ge(s_dt2, q + 1)
                dt, dA, acum, vals = hv_["dt"], hv_["dA"], hv2["acum"], hv2["vals"]
                softplus(sp[0], sp[2], sp[3], sp[4], sp[5], dt[:])
                V.tensor_scalar(dA[:], dt[:], hv2["bvec"][:, 0:1], -1.0, ALU.mult, ALU.mult)
                dve.drain()
                V.tensor_tensor_scan(acum[:], ones[0:HEADS, 0:1].to_broadcast([HEADS, SEQ]), dA[:, seq], 0.0, ALU.mult, ALU.add).then_inc(s_dt3, 1)
                V.tensor_copy(vals[:, 0:8], dt[:, smpl])
                V.tensor_copy(vals[:, 16:17], hsm[:, 4 + q:5 + q])
                dve.wait_ge(s_dt4, q + 1)
                dve.drain()
                V.tensor_tensor(hv_["R"][:], vals[:].unsqueeze(1).to_broadcast([HEADS, XT, 17]),
                                pairsel[:].unsqueeze(2).to_broadcast([HEADS, XT, 17]), ALU.mult).then_inc(s_dt5, 1)
                dve.wait_ge(s_dt6, q + 1)
                tm, hv = hv2["tm"], hv2["hv"]
                V.tensor_copy(tm[:], bank[2][:, 0:6 * HEADS].rearrange("p (j h) -> p j h", h=HEADS))
                V.tensor_copy(hv[:], bank[3][:, 0:XT * 17].rearrange("p (i v) -> p i v", v=17))
                dve.drain()

                def z_out(r, p):
                    V.tensor_tensor(zs[:, ds(r * 2, 2), :], G[p][:, :, 0:T], bc(rstd[:], 2), ALU.mult).then_inc(s_ev, 1)

                def silus(r, p):
                    b = r % 2
                    dve.wait_ge(s_zth, 8 * q + r + 1)
                    V.scalar_tensor_tensor(zs[:, 2 * r:2 * r + 2, :], S[f"T{b}"][:, :, 0:T], 1.0, zs[:, 2 * r:2 * r + 2, :], ALU.add, ALU.mult)
                    dve.wait_ge(s_xth, 8 * q + r + 1)
                    V.scalar_tensor_tensor(xbc[:, 4 * r:4 * r + 4, :], xth[f"xth{b}"][:], 1.0, xbc[:, 4 * r:4 * r + 4, :], ALU.add, ALU.mult).then_inc(s_silu, 1)
                z = stage[i, "z"]
                for r in range(8):
                    dve.wait_ge(s_mm, z["g0"] + r + 1)
                    z_out(r, (r + z["c0"]) % 2)
                    split(z, r // 4, r % 4)
                    silus(r, r % 2)
                dve.drain().then_inc(s_th, 1)
                for k in range(1, 8, 2):
                    dve.wait_ge(s_orT, 8 * q + k + 1)
                    V.tensor_copy(orow["orow"][:, k * 512:(k + 1) * 512], bank[k][0:LAST, :]).then_inc(s_orE, 1)
                dve.wait_ge(s_orD, 32 * (q + 1))

                def front(g, b):
                    dve.wait_ge(s_tp, g + (GROUPS * q + 1))
                    if not (isinstance(g, int) and g < 2):
                        dve.wait_ge(s_back, g + (GROUPS * q - 1))
                    xd, btm, cbm, seg = (grp[f"{n}{b}"] for n in ("xd", "btm", "cbm", "seg"))
                    for c in range(2):
                        V.tensor_tensor(xd[:, c], bank[0][:, c * SEQ:(c + 1) * SEQ].rearrange("s (r p) -> s r p", p=64),
                                        tm[:, c, ds(g * 4, 4)].unsqueeze(2).to_broadcast([P, 4, 64]), ALU.mult)
                    if not (isinstance(g, int) and g < 2):
                        dve.wait_ge(s_xde, g + (GROUPS * q - 1))
                    V.tensor_copy(btm[:], bank[1][:, 0:SEQ].rearrange("s (c n) -> s c n", c=2))
                    V.tensor_tensor(cbm[:], bank[2][:, 0:3 * P], tri[:], ALU.mult).then_inc(s_xd, 1)
                    dve.wait_ge(s_ar, g + (GROUPS * q + 1))
                    for r in range(4):
                        at_ = G[0][:, r // 2, (r % 2) * SEQ:(r % 2 + 1) * SEQ]
                        V.tensor_scalar(seg[:, r, 0:SEQ], at_, tm[:, 2, ds(g * 4 + r, 1)], 0.0, ALU.subtract, ALU.min)
                        f = V.tensor_scalar(seg[:, r, SEQ:3 * P], at_[:, P:SEQ], tm[:, 3, ds(g * 4 + r, 1)], 0.0, ALU.subtract, ALU.min)
                    f.then_inc(s_seg, 1)

                def mid(g, b):
                    dve.wait_ge(s_exp, g + (GROUPS * q + 1))
                    seg = grp[f"seg{b}"]
                    V.tensor_tensor(seg[:], seg[:], bc(grp[f"cbm{b}"][:], 4), ALU.mult).then_inc(s_M, 1)

                def back(g, b):
                    dve.wait_ge(s_back, g + (GROUPS * q + 1))
                    y = S[f"T{b}"]
                    for t in range(2):
                        V.scalar_tensor_tensor(y[:, t, seq], xbc[:, ds(g * 2 + t, 1), seq].rearrange("p o t -> p (o t)"),
                                               hv[:, ds(g * 2 + t, 1), 16:17].rearrange("p o v -> p (o v)"), G[1][:, t, seq], ALU.mult, ALU.add)
                    dve.drain()
                    if not (isinstance(g, int) and g < 2):
                        dve.wait_ge(s_sto[b], g * 8 + (8 * GROUPS * q - 8 * b))
                    zz = zs[:, ds(g * 2, 2), seq]
                    V.scalar_tensor_tensor(zz, y[:, :, seq], 0.5, zz, ALU.mult, ALU.mult)
                    V.tensor_copy(grp[f"stout{b}"][:], G[1][:, :, SEQ:3 * P]).then_inc(s_yev, 1)
                skewed(V, GROUPS, front, back, mid)
                for b in range(2):
                    dve.wait_ge(s_sto[b], 8 * GROUPS * (q + 1))
                dve.wait_ge(s_brT, q + 1)
                V.tensor_copy(bcr["bcrow"][:, 0:D], A[0][0:NB].rearrange("b a n -> b (a n)"))
                V.tensor_copy(bcr["bcrow"][:, D:2 * D], A[1][0:NB].rearrange("b a n -> b (a n)")).then_inc(s_brE, 1)
                xdts, ys = hv2["xdts"], hv2["ys"]
                V.tensor_tensor(xdts[:], xbc[:, 0:XT, smpl], hv[:, :, 0:8], ALU.mult)
                dve.drain().then_inc(s_bcf, 2)
                with V.Fori(0, NB // 4) as it:
                    for u in range(4):
                        n = it * 4 + u
                        bb, cc = (A[0], A[1]) if u % 2 == 0 else (G[0], G[1])
                        st_ = smp[f"st{u}"]
                        dve.wait_ge(s_bc, n + (NB * q + 1))
                        dve.wait_ge(s_hd, n + (NB * q + 1))
                        for t in range(XT):
                            w = slice((t // 2 % 4) * P, (t // 2 % 4) * P + P)
                            f = V.scalar_tensor_tensor(st_[:, t, :], bb[:, t // 8, w], xdts[:, t, ds(n, 1)], st_[:, t, :], ALU.mult, ALU.add)
                        f.then_inc(s_hn, 1)
                        dve.drain()
                        for t in range(XT):
                            w = slice((t // 2 % 4) * P, (t // 2 % 4) * P + P)
                            f = V.tensor_tensor_reduce(bcr["scr"][:, t, :], st_[:, t, :], cc[:, t // 8, w], 1.0, 0.0,
                                                       ALU.mult, ALU.add, hv2[f"ysb{u % 2}"][:, t:t + 1])
                        f.then_inc(s_bcf, 1)
                        dve.drain()
                        V.tensor_copy(ys[:, :, ds(n, 1)].rearrange("p t o -> p (t o)"), hv2[f"ysb{u % 2}"][:])
                dve.drain()
                xs = xbc[:, 0:XT, smpl]
                V.tensor_tensor(xdts[:], xs, hv[:, :, 16:17].to_broadcast([P, XT, NB]), ALU.mult)
                dve.drain()
                V.tensor_tensor(xdts[:], xdts[:], ys[:], ALU.add)
                dve.drain()
                V.scalar_tensor_tensor(zs[:, :, smpl], xdts[:], 0.5, zs[:, :, smpl], ALU.mult, ALU.mult)
                dve.drain().then_inc(s_yz, 1)
                dve.nop().then_inc(s_gs, 2)
                with V.Fori(0, GROUPS // 2) as it:
                    for b in range(2):
                        g = it * 2 + b
                        yn = gnb[f"yn{b}"]
                        dve.wait_ge(s_gs, g + ((GROUPS + 2) * q + 3))
                        V.reciprocal(gnb[f"grs{b}"][:], gnb[f"gstd{b}"][:])
                        dve.drain()
                        for t in range(2):
                            f = V.scalar_tensor_tensor(yn[:, t, :], zs[:, ds(g * 2 + t, 1), :].rearrange("p o t -> p (o t)"),
                                                       colB[:, ds(g * 2 + (64 + XT * q + t), 1)], gnb[f"grs{b}"][:], ALU.mult, ALU.mult)
                        f.then_inc(s_yn, 1)
                        dve.wait_ge(s_yh, g + (GROUPS * q + 1))
                        V.tensor_tensor(ysp["yL"][:, ds(g * 2, 2), :], yn[:], ysp["yH"][:, ds(g * 2, 2), :].bitcast(F32), ALU.subtract).then_inc(s_mixl, 1)
                evacs(stage[i, "ssd_out"], add_h)

            def moba():
                phase()
                norm(3, sq_mix["sqm"])
                qkv, att = M["qkv"], M["att"]

                def qkv_out(r, p):
                    V.tensor_tensor(qkv[:, ds(r * 2, 2), :], G[p][:, :, 0:T], bc(rstd[:], 2), ALU.mult).then_inc(s_ev, 1)
                evacs(stage[1, "qkv"], qkv_out)

                def front(hh, b):
                    dve.wait_ge(s_mtp, hh + 1)
                    if not (isinstance(hh, int) and hh < 2):
                        dve.wait_ge(s_mo, hh - 1)
                        dve.wait_ge(s_kst[b], hh * 16 - 16 * b)
                    sc, mx, nm = mh[f"sc{b}"], mh[f"mx{b}"], mh[f"nm{b}"]
                    V.tensor_copy(mh[f"kvt{b}"][:], bank[0].rearrange("p (j d) -> p j d", j=4))
                    V.tensor_copy(M["rowS"][:, :, ds(hh * P, P)], bank[1][0:NB, 0:3 * P].rearrange("p (j d) -> p j d", j=3))
                    V.tensor_tensor(sc[:], bank[2][:, 0:3 * P], amask[:], ALU.add)
                    dve.drain()
                    V.tensor_reduce(mx[:, 0:1], sc[:, 0:P], AX, ALU.max)
                    V.tensor_reduce(mx[:, 1:2], sc[:, P:3 * P], AX, ALU.max)
                    dve.drain()
                    V.tensor_scalar(nm[:], mx[:], -SCALE, None, ALU.mult).then_inc(s_msc, 1)

                def mid(hh, b):
                    dve.wait_ge(s_mex, hh + 1)
                    sc, rs, ri = mh[f"sc{b}"], mh[f"rs{b}"], mh[f"ri{b}"]
                    V.reciprocal(ri[:], rs[:])
                    dve.drain()
                    V.tensor_scalar(sc[:, 0:P], sc[:, 0:P], ri[:, 0:1], None, ALU.mult)
                    V.tensor_scalar(sc[:, P:3 * P], sc[:, P:3 * P], ri[:, 1:2], None, ALU.mult).then_inc(s_mP, 1)

                def back(hh, b):
                    dve.wait_ge(s_mo, hh + 1)
                    V.tensor_copy(att[:, ds(hh, 1), 0:SEQ].rearrange("p o t -> p (o t)"), bank[4][:, 0:SEQ]).then_inc(s_moe, 1)
                skewed(V, MH, front, back, mid)
                for b in range(2):
                    dve.wait_ge(s_kst[b], 16 * MH)
                S_ = slice(SEQ, T)
                V.tensor_tensor(ms["qk"][:], qkv[:, 0:8, S_].rearrange("p h b -> p b h"), qkv[:, 8:16, S_].rearrange("p h b -> p b h"), ALU.mult).then_inc(s_qk, 1)
                dve.nop().then_inc(s_kd, 16)
                with V.Fori(0, NB // 2) as it:
                    for b in range(2):
                        n = it * 2 + b
                        dve.wait_ge(s_qbc, n + 1)
                        for j in range(PAGES):
                            dve.wait_ge(s_pg[j], n * 16 + 16)
                            for hh in range(MH):
                                f = V.tensor_tensor_reduce(pg[f"pg{j}"][:, hh, :], pg[f"pg{j}"][:, hh, :], A[b][:, hh // 4, (hh % 4) * P:(hh % 4 + 1) * P],
                                                           1.0, 0.0, ALU.mult, ALU.add, ms[f"sq{b}"][:, j, hh:hh + 1])
                            f.then_inc(s_kd, 1)
                        dve.drain()
                        V.tensor_copy(ms["sS"][:, :, ds(n * 8, 8)], ms[f"sq{b}"][:])
                dve.drain().then_inc(s_kd, 1)
                sR, gs, geq, gsc = ms["sR"], ms["gsum"], ms["geq"], ms["gsc"]
                dve.wait_ge(s_sT, 1)
                V.tensor_copy(sR[:, 0:1024], A[0][0:64].rearrange("p a n -> p (a n)"))
                V.tensor_copy(sR[:, 1024:1025], bank[4][0:64, 0:1])
                dve.drain()
                blocks = sR[:, 0:1024].rearrange("p (n k) -> p n k", n=BLOCKS)
                V.tensor_reduce(gs[:], blocks, AX, ALU.add)
                dve.drain()
                V.tensor_reduce(gsc[:, 0:1], gs[:], AX, ALU.min)
                dve.drain()
                V.scalar_tensor_tensor(geq[:], gs[:], gsc[:, 0:1], blockno[:], ALU.is_equal, ALU.mult)
                dve.drain()
                V.tensor_reduce(gsc[:, 1:2], geq[:], AX, ALU.max)
                dve.drain()
                V.tensor_scalar(geq[:], geq[:], gsc[:, 1:2], -BIG, ALU.is_equal, ALU.mult)
                dve.drain()
                V.tensor_tensor(blocks, blocks, geq[:].unsqueeze(2).to_broadcast([64, BLOCKS, 256]), ALU.add)
                dve.drain()
                V.tensor_reduce(gsc[:, 4:5], sR[:, 0:1025], AX, ALU.max)
                dve.drain()
                V.tensor_scalar(gsc[:, 2:3], gsc[:, 4:5], -SCALE, None, ALU.mult).then_inc(s_sR, 1)
                dve.wait_ge(s_sE, 1)
                V.reciprocal(gsc[:, 5:6], gsc[:, 3:4])
                dve.drain()
                V.tensor_scalar(sR[:, 0:1025], sR[:, 0:1025], gsc[:, 5:6], None, ALU.mult)
                dve.drain()
                V.tensor_scalar(ms["dg"][:], ident[0:64, 0:64], sR[:, 1024:1025], None, ALU.mult).then_inc(s_sP, 1)
                dve.wait_ge(s_sPT, 1)
                V.tensor_copy(ms["pT8"][:], bank[2].rearrange("p (j c) -> p j c", j=PAGES)).then_inc(s_sPTe, 1)
                V.tensor_copy(ms["bco"][:], bank[5][:, 0:64])
                dve.drain()
                ov = ms["ov"][:].rearrange("p (b h) -> p b h", h=MH)
                V.tensor_tensor(ov, qkv[:, 16:24, S_].rearrange("p h b -> p b h"), ms["bco"][:].rearrange("p (b h) -> p b h", h=MH), ALU.mult)
                dve.drain()
                dve.wait_ge(s_vd, NB * PAGES)
                V.tensor_tensor(att[:, :, S_].rearrange("p h b -> p b h"), bank[6][:, 0:64].rearrange("p (b h) -> p b h", h=MH), ov, ALU.add).then_inc(s_att, 1)
                dve.wait_ge(s_mixh, 1)
                V.tensor_tensor(xL[:], att[:], xH[:].bitcast(F32), ALU.subtract).then_inc(s_mixl, 1)
                evacs(stage[1, "wo"], add_h)

            def lru():
                phase()
                lp = [lsp[f"lp{k}"][:] for k in range(6)]
                lam = colB[:, 40:48]
                V.tensor_scalar(lp[0], lam, -1.0, None, ALU.mult)
                dve.drain()
                V.tensor_tensor(lp[1], lp[0], lam, ALU.min).then_inc(s_lsp, 1)
                dve.wait_ge(s_lse, 1)
                softplus(lp[0], lp[2], lp[3], lp[4], lp[5], L["ch"][:])
                V.tensor_scalar(L["ch"][:], L["ch"][:], -4.0, None, ALU.mult)
                V.tensor_scalar(L["bah"][:], colB[:, 48:56], 0.5, None, ALU.mult)
                V.tensor_scalar(L["bxh"][:], colB[:, 56:64], 0.5, None, ALU.mult)
                V.memset(L["XR"][:, :, 0:3], 0.0)
                norm(6, sq_mix["sqm"])
                st = stage[2, "lru_in"]
                for it in range(2):
                    for u in range(4):
                        split(st, it, u)
                        dve.wait_ge(s_mm, st["g0"] + 4 * it + u + 1)
                        o = L["Gt"][:, 2 * u:2 * u + 2, :] if it == 0 else L["XR"][:, 2 * u:2 * u + 2, 3:3 + T]
                        V.tensor_tensor(o, G[(u + st["c0"]) % 2][:, :, 0:T], bc(rstd[:], 2), ALU.mult).then_inc(s_ev, 1)
                XR, xc, la = L["XR"], L["xc"], L["la"]
                dve.wait_ge(s_lT, 1)
                V.tensor_copy(L["lstT"][:], bank[2][:, 0:192].rearrange("p (k s) -> p k s", s=24))
                V.tensor_copy(L["lh0"][:], bank[2][:, 192:256].rearrange("p (k b) -> p k b", b=8)).then_inc(s_lTe, 1)
                dve.drain()
                for k in range(3):
                    V.tensor_tensor(L["lpr"][:, :, :, k], L["lstT"][:].rearrange("p t (b k) -> p t b k", k=3)[:, :, :, k],
                                    colB[:, k * KT:(k + 1) * KT].unsqueeze(2).to_broadcast([P, KT, NB]), ALU.mult)
                dve.drain()
                V.tensor_reduce(L["lspre"][:], L["lpr"][:], AX, ALU.add)
                dve.drain()
                V.tensor_tensor(L["lspre"][:], L["lspre"][:], colB[:, 32:40].unsqueeze(2).to_broadcast([P, KT, NB]), ALU.add)
                dve.drain()
                for k in range(KT):
                    dve.wait_ge(s_lt0, k + 1)
                    for w in range(1, CW):
                        V.scalar_tensor_tensor(xc[:, k, 0:SEQ], XR[:, k, w:w + SEQ], colB[:, w * KT + k:w * KT + k + 1], xc[:, k, 0:SEQ], ALU.mult, ALU.add)
                        dve.drain()
                    V.scalar_tensor_tensor(xc[:, k, SEQ:T], XR[:, k, 3 + SEQ:3 + T], colB[:, 3 * KT + k:3 * KT + k + 1], L["lspre"][:, k, :],
                                           ALU.mult, ALU.add).then_inc(s_lc, 1)
                for k in range(KT):
                    dve.wait_ge(s_lth, k + 1)
                    f = V.tensor_scalar(la[:, k, :], L["thr"][:, k, :], 1.0, L["ch"][:, k:k + 1], ALU.add, ALU.mult)
                f.then_inc(s_lla, 1)
                V.scalar_tensor_tensor(L["thi"][:], L["thi"][:], 1.0, xc[:], ALU.add, ALU.mult)
                dve.drain()
                V.tensor_tensor(xc[:], L["Gt"][:], L["Gt"][:], ALU.mult)
                dve.drain()
                V.tensor_scalar(xc[:], xc[:], GELU_B, 1.0, ALU.mult, ALU.add)
                dve.drain()
                V.tensor_tensor(xc[:], xc[:], L["Gt"][:], ALU.mult).then_inc(s_lgl, 1)
                dve.wait_ge(s_la, 1)
                V.tensor_scalar(L["hs"][:], L["thr"][:], 1.0, None, ALU.add)
                dve.drain()
                V.reciprocal(L["hs"][:], L["hs"][:])
                dve.drain()
                V.tensor_tensor(L["thr"][:], L["thr"][:], L["hs"][:], ALU.mult).then_inc(s_lv, 1)
                dve.wait_ge(s_lgt, 1)
                V.scalar_tensor_tensor(xc[:], xc[:], 1.0, L["Gt"][:], ALU.add, ALU.mult)
                dve.wait_ge(s_lsq, 1)
                V.scalar_tensor_tensor(L["thi"][:], L["thi"][:], 0.5, L["thr"][:], ALU.mult, ALU.mult)
                dve.wait_ge(s_la, 2)
                dve.drain()
                for k in range(KT):
                    V.tensor_tensor_scan(L["hs"][:, k, 0:SEQ], la[:, k, 0:SEQ], L["thi"][:, k, 0:SEQ], 0.0, ALU.mult, ALU.add)
                V.tensor_tensor(L["lh0"][:], L["lh0"][:], la[:, :, SEQ:T], ALU.mult)
                dve.drain()
                V.tensor_tensor(L["hs"][:, :, SEQ:T], L["lh0"][:], L["thi"][:, :, SEQ:T], ALU.add)
                dve.drain()
                V.scalar_tensor_tensor(xc[:], xc[:], 0.5, L["hs"][:], ALU.mult, ALU.mult).then_inc(s_ly, 1)
                dve.wait_ge(s_mixh, 2)
                V.tensor_tensor(xL[:], xc[:], xH[:].bitcast(F32), ALU.subtract).then_inc(s_mixl, 1)
                dve.wait_ge(s_loT, 1)
                V.tensor_copy(L["lrow"][:], A[0][0:LAST].rearrange("p a n -> p (a n)")).then_inc(s_loE, 1)
                V.tensor_copy(L["hrow"][:], A[1][0:9].rearrange("p a n -> p (a n)")).then_inc(s_loE, 1)
                evacs(stage[2, "lru_out"], add_h)

            def mlp_ple(i):
                phase()
                norm(3 * i + 1, sq)

                def low(r, b):
                    dve.wait_ge(s_ac, r + (16 * i + 1))
                    dve.wait_ge(s_aH, r + (16 * i + 1))
                    V.tensor_tensor(aL[:, ds(r * 2, 2), :], ml[f"ac{b}"][:], aH[:, ds(r * 2, 2), :].bitcast(F32), ALU.subtract).then_inc(s_aL, 1)
                evacs(stage[i, "up"], low)
                dve.wait_ge(s_pT, i + 1)
                V.tensor_copy(ml["pT"][:], A[0][:, :, 0:T]).then_inc(s_pTe, 1)

                def down(r, p):
                    V.tensor_tensor(ml["t1"][:], G[p][:, :, 0:T], bc(rstd2[:], 2), ALU.mult).then_inc(s_ev, 1)
                    dve.drain()
                    hr = h[:, ds(r * 2, 2), :]
                    V.tensor_tensor(hr, hr, ml["t1"][:], ALU.add)
                evacs(stage[i, "down"], down)
                dve.drain()
                norm(3 * i + 2, sq)
                st = stage[i, "gate"]
                t1 = ml["t1"]
                for r in range(4):
                    split(st, 0, r)
                    dve.wait_ge(s_mm, st["g0"] + r + 1)
                    V.tensor_tensor(t1[:], G[(r + st["c0"]) % 2][:, :, 0:T], bc(rstd[:], 2), ALU.mult).then_inc(s_ev, 1)
                    dve.wait_ge(s_tg, 4 * i + r + 1)
                    dve.wait_ge(s_pj, 4 * i + r + 1)
                    V.scalar_tensor_tensor(t1[:], t1[:], 1.0, A[r % 2][:, :, 0:T], ALU.add, ALU.mult).then_inc(s_pje, 1)
                    dve.drain()
                    hr = h[:, 2 * r:2 * r + 2, :]
                    V.scalar_tensor_tensor(hr, t1[:], 0.5, hr, ALU.mult, ALU.add)
                    dve.drain()

            for i in range(DEPTH):
                if i in SSD_LAYERS:
                    ssd(i, i // 3)
                elif i == 1:
                    moba()
                else:
                    lru()
                mlp_ple(i)
            phase()
            norm(12, sq, gain=False)
            for k in range(KT):
                f = V.scalar_tensor_tensor(fin["yfin"][:, k, :], h[:, k, :], colA[:, 96 + k:97 + k], rstd[:], ALU.mult, ALU.mult)
            f.then_inc(s_fin, 1)
            dve.wait_ge(s_finT, 1)
            V.tensor_copy(fin["yrow"][:, 1, :], G[1][:].rearrange("p a b -> p (a b)")).then_inc(s_finE, 1)


INPUTS = ["x_prompt", "x_sample", "state_ssd_conv", "state_ssd", "cache_k", "cache_v", "page_table", "state_lru_conv",
          "state_lru", "p_prompt", "p_sample", "norm_mix", "norm_mlp", "norm_ple", "norm_final", "ssd_w_in",
          "ssd_conv_w", "ssd_conv_b", "ssd_dt_bias", "ssd_a_log", "ssd_d", "ssd_norm", "ssd_w_out", "moba_w_qkv",
          "moba_w_o", "lru_w_in", "lru_conv_w", "lru_conv_b", "lru_w_a", "lru_b_a", "lru_w_x", "lru_b_x",
          "lru_lambda", "lru_w_out", "mlp_w_up", "mlp_w_down", "ple_w_proj", "ple_w_gate"]
OUTPUTS = [("y_p", (1, 256, 1024)), ("y_s", (8, 1, 1024)),
           ("ssd_conv_p", (2, 1, 3, 4096)), ("ssd_state_p", (2, 1, 32, 64, 128)),
           ("k_p", (1, 1, 256, 8, 128)), ("v_p", (1, 1, 256, 8, 128)),
           ("lru_conv_p", (1, 1, 3, 1024)), ("lru_state_p", (1, 1, 1024)),
           ("ssd_conv_s", (2, 8, 3, 4096)), ("ssd_state_s", (2, 8, 32, 64, 128)),
           ("k_s", (1, 8, 1, 8, 128)), ("v_s", (1, 8, 1, 8, 128)),
           ("lru_conv_s", (1, 8, 3, 1024)), ("lru_state_s", (1, 8, 1024))]


def kernel(**inputs):
    import numpy as np
    import concourse.bacc as bacc
    from concourse.bass_utils import run_bass_kernel_spmd

    nc = bacc.Bacc("TRN2", target_bir_lowering=False, num_devices=1)
    arrays, t_in, t_out = {}, {}, {}
    for name in INPUTS:
        a = np.ascontiguousarray(inputs[name])
        arrays[f"in_{name}"] = a
        t_in[name] = nc.dram_tensor(f"in_{name}", a.shape, mybir.dt.from_np(a.dtype), kind="ExternalInput").ap()
    for name, shape in OUTPUTS:
        t_out[name] = nc.dram_tensor(f"out_{name}", shape, F32, kind="ExternalOutput").ap()
    build_trunk(nc, t_in, t_out)
    r = run_bass_kernel_spmd(nc, [arrays], core_ids=[0])
    return tuple(r.results[0][f"out_{name}"] for name, _ in OUTPUTS)
```

```python
from contextlib import ExitStack

import concourse.bass as bass
from concourse import mybir

F32 = mybir.dt.float32
F32R = mybir.dt.float32r
I32 = mybir.dt.int32
ALU = mybir.AluOpType
ACT = mybir.ActivationFunctionType
AX = mybir.AxisListType.X
ds = bass.ds

P = 128
D = 1024
KT = D // P
SEQ = 256
NB = 8
T = SEQ + NB
DEPTH = 4
EPS = 1e-6
CW = 4
LAST = CW - 1 + NB
CHUNK = 256
CONVD = 4096
CT = CONVD // P
XT = 16
HEADS = 32
GROUPS = 8
PLE = 256
MH = 8
PAGES = 8
BLOCKS = 4
SCALE = float(P) ** -0.5
BIG = 1e30
TILE_B = T * 4
SSD_LAYERS = (0, 3)
DH = 2
GELU_A, GELU_B = 0.7978845608028654, 0.044715


def plan():
    stages, g, col = [], 0, 0
    for i in range(DEPTH):
        if i in SSD_LAYERS:
            mix = [("xbc", 16, 1), ("z", 8, 1), ("ssd_out", 8, 2)]
        elif i == 1:
            mix = [("qkv", 12, 1), ("wo", 4, 1)]
        else:
            mix = [("lru_in", 8, 1), ("lru_out", 4, 1)]
        for name, n, kq in mix + [("up", 16, 1), ("down", 16, 4), ("gate", 4, 1)]:
            stages.append(dict(name=name, layer=i, n=n, kq=kq, g0=g, c0=col))
            g += n
            col += n // kq
    return stages, g


def build_trunk(nc, t_in, t_out):
    stages, total = plan()
    stage = {(s["layer"], s["name"]): s for s in stages}
    ctx = ExitStack()
    with ctx:
        def sb(name, shape, dt=F32):
            return ctx.enter_context(nc.sbuf_tensor(name, shape, dt))

        def sem(name):
            return ctx.enter_context(nc.semaphore(name))

        raw = [sb(f"raw{u}", [P, KT, CHUNK]) for u in range(4)]
        whi = [sb(f"whi{u}", [P, KT, CHUNK], F32R) for u in range(2)]
        wlo = [sb(f"wlo{u}", [P, KT, CHUNK], F32R) for u in range(2)]
        h = sb("h", [P, KT, T])
        rstd = sb("rstd", [P, T])
        sums = sb("sums", [P, 4, T])
        ssq, hh2 = sums[:, 0:2, :], sums[:, 2:4, :]
        eo2 = sums[0:HEADS, 2, 0:2]
        grow = sums[0:GROUPS].rearrange("p a t -> p (a t)")[:, 0:GROUPS * P]
        ident = sb("ident", [P, P])
        ones = sb("ones", [P, P])
        zeros = sb("zeros", [P, 64])
        tri = sb("tri", [P, 3 * P])
        amask = sb("amask", [P, 3 * P])
        colA = sb("colA", [P, 104])
        colB = sb("colB", [P, 96])
        colC = sb("colC", [P, 2, P])
        colE = sb("colE", [P, 64])
        hsm = sb("hsm", [HEADS, 6])
        evenodd = sb("evenodd", [HEADS, P])
        pairsel = sb("pairsel", [HEADS, XT])
        blockno = sb("blockno", [64, BLOCKS])
        epsc = sb("epsc", [P, 1])
        lsp = {n: sb(n, [P, KT]) for n in ("ch", "bah", "bxh")}
        lsp.update({f"lp{k}": sums[:, 3, k * KT:(k + 1) * KT] for k in range(6)})
        gsel = sb("gsel", [P, GROUPS, GROUPS])
        ptab = sb("ptab", [1, NB * PAGES], I32)

        base = (nc.sbuf_base + 31) // 32 * 32
        arena_bytes = (nc.sbuf_usable_end - base) // 32 * 32
        ctx.enter_context(nc.sbuf_tensor("arena", [P, arena_bytes // 4 - 8], F32))

        def at(name, shape, off, dt=F32):
            n = 4
            for x in shape[1:]:
                n *= x
            assert off % 32 == 0 and off + n <= arena_bytes - 32, (name, off, n, arena_bytes)
            return nc.alloc_sbuf_tensor_at(name, shape, dt, offset=base + off)

        x0 = 2 * XT * TILE_B + XT * TILE_B + 2 * 18944 + 2 * 2144
        x1 = x0 + 3 * KT * TILE_B

        def row(off, items):
            got = {}
            for name, shape, *dt in items:
                n = 4
                for x in shape[1:]:
                    n *= x
                n = (n + 31) // 32 * 32
                if off < x1 and off + n > x0:
                    off = x1
                got[name] = at(name, shape, off, *dt)
                off += n
            return got, off

        xg = at("xg", [P, KT, T], x0)
        xH = at("xH", [P, KT, T], x0 + KT * TILE_B, F32R)
        xL = at("xL", [P, KT, T], x0 + 2 * KT * TILE_B, F32R)

        A0, _ = row(0, [("xrow", [P, 2, D]), ("xrow8", [NB, D]), ("rowA", [104, P]), ("rowB", [96, P]),
                        ("rowC", [P, P]), ("rowD", [P, P]), ("rowE", [64, P])])
        Z, o1 = row(0, [("zs", [P, XT, T]), ("xbc", [P, CT, T])])
        grp, o2 = row(o1, [(f"{n}{b}", s) for b in range(2) for n, s in (
            ("stg", [P, 3, SEQ]), ("sel", [HEADS, 4, P]), ("cbm", [P, 3 * P]), ("xd", [P, 2, 4, 64]),
            ("xde", [P, 2, 4, 64]), ("btm", [P, 2, P]), ("seg", [P, 4, 3 * P]), ("stout", [P, 2, P]))])
        assert o2 + 2 * 2144 == x0
        stt = at("stt", [P, NB, XT * P], x1 - NB * XT * P * 4)
        stx = [stt[:, NB - 1 - n, :].rearrange("p (i c) -> p i c", i=XT) for n in range(NB)]
        bcr, _ = row(2 * XT * TILE_B, [("bcH", [NB, 2 * D], F32R), ("bcL", [NB, 2 * D], F32R)])
        otm, _ = row(XT * TILE_B, [(f"out{b}", [P, XT, P]) for b in range(2)])
        cst, _ = row(o1, [("cst", [NB * 3, CONVD])])
        orow, _ = row(0, [("orow", [LAST, CONVD])])
        cprod, _ = row(o1 + 16384, [("cprod", [P, CT, NB, 3])])
        ysp, o4 = row(o1, [("yH", [P, XT, T], F32R), ("yL", [P, XT, T], F32R)])
        ysq, _ = row(XT * TILE_B, [("ysq", [P, XT, T])])
        gnb, _ = row(2 * XT * TILE_B, [("grs", [GROUPS, T])])
        S, o5 = row(max(o2, o4), [("T0", [P, 2, 268]), ("T1", [P, 2, 268]), ("rawlast", [P, CT, LAST]),
                                     ("spre", [P, CT, NB])])
        cstT, _ = row(o5, [("stT", [P, CT, NB * 3])])
        hv2, _ = row(o5, [("acum", [HEADS, SEQ]), ("vals", [HEADS, 17]), ("hv", [P, XT, 17]),
                          ("tm", [P, 6, HEADS]), ("xdts", [P, XT, NB]), ("ys", [P, XT, NB]),
                          ("ysb0", [P, XT]), ("ysb1", [P, XT]), ("selS0", [NB, P], F32R), ("selS1", [NB, P], F32R), ("bvec", [HEADS, 2])])
        hv3, _ = row(o5 - 4 * CT * NB, [("dx", [P, XT, NB])])
        hv_, _ = row(o1 + 33024, [("wdt", [P, KT, HEADS]), ("R", [HEADS, XT, 17]), ("dt", [HEADS, T]), ("dA", [HEADS, T])])
        dte_, _ = row(o1 + 22784, [("dte", [HEADS, SEQ])])
        xth, _ = row(o1 + 24576, [(f"xth{b}", [P, 4, T]) for b in range(2)])
        spl, _ = row(o1 + 16384, [(f"sp{k}", [HEADS, T]) for k in range(6)])
        M, m1 = row(0, [("qkv", [P, 3 * MH, T]), ("att", [P, KT, T]), ("rowS", [NB, 3, D])])
        pg, m2 = row(m1, [(f"pg{j}", [P, MH, P]) for j in range(PAGES)])
        mh, m3 = row(m2, [(f"{n}{b}", s) for b in range(2) for n, s in (
            ("stq", [P, 3, T]), ("kvt", [P, 4, P]), ("sc", [P, 3 * P]), ("pt", [P, 3 * P]),
            ("mx", [P, 2]), ("nm", [P, 2]), ("rs", [P, 2]), ("ri", [P, 2]))])
        ms, m4 = row(m2, [("sS", [P, PAGES, 64]), ("sR", [64, 1056]), ("pT8", [P, PAGES, 64]),
                          ("qk", [P, NB, MH]), ("gsum", [64, BLOCKS]), ("geq", [64, BLOCKS]),
                          ("gsc", [64, 8]), ("dg", [64, 64]), ("ov", [P, 64]), ("bco", [P, 64]), ("pH8", [P, PAGES, 64], F32R), ("pL8", [P, PAGES, 64], F32R),
                          ("qsel", [NB, P]), ("sq0", [P, PAGES, MH]), ("sq1", [P, PAGES, MH])])
        L, l1 = row(0, [("Gt", [P, KT, T]), ("XR", [P, KT, 268]), ("xc", [P, KT, T]), ("thr", [P, KT, T]),
                        ("thi", [P, KT, T]), ("la", [P, KT, T]), ("wax", [P, 16, P]),
                        ("hs", [P, KT, T]), ("a2", [P, KT, T]), ("lcst", [NB * 3, D]), ("lst", [NB, D]), ("lstT", [P, KT, NB * 3]),
                        ("lh0", [P, KT, NB]), ("lspre", [P, KT, NB]), ("lrow", [LAST, D]), ("hrow", [9, D]), 
                        ("lpr", [P, KT, NB, 3])])
        ml, m0 = row(0, [("aH", [P, 32, T], F32R), ("aL", [P, 32, T], F32R)])
        pin, m0b = row(m0, [("pH", [P, KT, T], F32R), ("pL", [P, KT, T], F32R)])
        mrl, _ = row(m0, [(f"{n}{b}", [P, 2, T]) for b in range(2) for n in ("rl", "ac")])
        mpl, _ = row(m0b, [("wp", [P, 2, D]), ("prow", [P, 2, PLE]), ("prow8", [NB, PLE]),
                     ("pT", [P, 2, T]), ("t1", [P, 2, T])])
        ml.update(mrl)
        ml.update(mpl)
        aH, aL = ml["aH"], ml["aL"]
        vH, vL = ([at(f"{n}{u}", [P, 2, D // 2], off + 4 * D * (u % 2), F32R)
                   for u, off in enumerate((a_, a_, b_, b_))]
                  for n, a_, b_ in (("vH", x0 + KT * TILE_B, 0), ("vL", x0 + 2 * KT * TILE_B, 8 * D)))
        pn = at("pn", [P, 2, 2, PAGES, NB * MH], x0, F32R)
        ao, _ = row(0, [("oH", [P, KT, T], F32R), ("oL", [P, KT, T], F32R)])
        lo_, _ = row(2 * KT * TILE_B + KT * 268 * 4, [("oH", [P, KT, T], F32R)])
        lo2, _ = row(4 * KT * TILE_B + KT * 268 * 4, [("oL", [P, KT, T], F32R)])
        fin, _ = row(0, [("yfin", [P, KT, T]), ("yrow", [P, 2, D]), ("yrow8", [NB, D])])

        G = [ctx.enter_context(nc.psum_tensor(f"G{p}", [P, 2, 512], F32)) for p in range(2)]
        A = [ctx.enter_context(nc.psum_tensor(f"A{p}", [P, 2, 512], F32)) for p in range(2)]
        bank = [A[0][:, 0, :], A[0][:, 1, :], A[1][:, 0, :], A[1][:, 1, :],
                G[0][:, 0, :], G[0][:, 1, :], G[1][:, 0, :], G[1][:, 1, :]]

        head_banks = (bank[0:3], bank[5:8])

        s_raw = [sem(f"s_raw{u}") for u in range(4)]
        s_hi, s_lo = sem("s_hi"), sem("s_lo")
        s_mm = sem("s_mm")
        s_ev = sem("s_ev")
        s_xg, s_xh, s_xl = sem("s_xg"), sem("s_xh"), sem("s_xl")
        s_ssq, s_var, s_std = sem("s_ssq"), sem("s_var"), sem("s_std")
        s_stored = sem("s_stored")
        s_const, s_load, s_load2, s_tp0 = sem("s_const"), sem("s_load"), sem("s_load2"), sem("s_tp0")
        s_init = sem("s_init")
        s_tap, s_conv = sem("s_tap"), sem("s_conv")
        s_last = sem("s_last")
        s_cst, s_cT = sem("s_cst"), sem("s_cT")
        s_zth, s_xth, s_th = sem("s_zth"), sem("s_xth"), sem("s_th")
        s_wdt, s_dtp, s_dt1, s_dt2, s_dt3 = sem("s_wdt"), sem("s_dtp"), sem("s_dt1"), sem("s_dt2"), sem("s_dt3")
        s_dt4, s_dt5, s_dt6 = sem("s_dt4"), sem("s_dt5"), sem("s_dt6")
        s_silu = sem("s_silu")
        s_orT, s_orE = sem("s_orT"), sem("s_orE")
        s_stg, s_sel, s_tp, s_ar = sem("s_stg"), sem("s_sel"), sem("s_tp"), sem("s_ar")
        s_xd, s_xde, s_seg, s_exp = sem("s_xd"), sem("s_xde"), sem("s_seg"), sem("s_exp")
        s_M, s_back, s_yev = sem("s_M"), sem("s_back"), sem("s_yev")
        s_sto = [sem(f"s_sto{b}") for b in range(2)]
        s_sinA, s_sinB = sem("s_sinA"), sem("s_sinB")
        s_sout = sem("s_sout")
        s_brH, s_ot = sem("s_brH"), sem("s_ot")
        s_brT, s_brE, s_ssel = sem("s_brT"), sem("s_brE"), sem("s_ssel")
        s_bc, s_hd, s_hn, s_bcf = sem("s_bc"), sem("s_hd"), sem("s_hn"), sem("s_bcf")
        s_M2 = sem("s_M2")
        s_yss, s_bb = sem("s_yss"), sem("s_bb")
        s_dt7 = sem("s_dt7")
        s_dtr, s_dtd, s_gr, s_gb, s_grow = sem("s_dtr"), sem("s_dtd"), sem("s_gr"), sem("s_gb"), sem("s_grow")
        s_yz, s_ysq, s_gv, s_gs, s_yn, s_yh, s_mixh, s_mixl = (
            sem("s_yz"), sem("s_ysq"), sem("s_gv"), sem("s_gs"), sem("s_yn"), sem("s_yh"), sem("s_mixh"), sem("s_mixl"))
        s_out = sem("s_out")
        s_ac, s_aH, s_aL = sem("s_ac"), sem("s_aH"), sem("s_aL")
        s_ple, s_pT, s_pTe, s_pj, s_pje, s_tg = (sem("s_ple"), sem("s_pT"), sem("s_pTe"), sem("s_pj"),
                                                 sem("s_pje"), sem("s_tg"))
        s_fin, s_finT, s_finE = sem("s_fin"), sem("s_finT"), sem("s_finE")
        s_stq, s_mtp, s_msc, s_mex, s_mP = sem("s_stq"), sem("s_mtp"), sem("s_msc"), sem("s_mex"), sem("s_mP")
        s_mpT, s_mpt, s_mo, s_moe = sem("s_mpT"), sem("s_mpt"), sem("s_mo"), sem("s_moe")
        s_kst = [sem(f"s_kst{b}") for b in range(2)]
        s_tab = sem("s_tab")
        s_pg = [sem(f"s_pg{j}") for j in range(PAGES)]
        s_km, s_ka = sem("s_km"), sem("s_ka")
        s_kd, s_vd = sem("s_kd"), sem("s_vd")
        s_qsel, s_qbc = sem("s_qsel"), sem("s_qbc")
        s_qk, s_sT, s_sR, s_sE, s_sP, s_sPT = sem("s_qk"), sem("s_sT"), sem("s_sR"), sem("s_sE"), sem("s_sP"), sem("s_sPT")
        s_att, s_sown, s_ptn = sem("s_att"), sem("s_sown"), sem("s_ptn")
        s_vh, s_vl, s_vo, s_vt = sem("s_vh"), sem("s_vl"), sem("s_vo"), sem("s_vt")
        s_lld, s_lT, s_lTe, s_lsp, s_lse = sem("s_lld"), sem("s_lT"), sem("s_lTe"), sem("s_lsp"), sem("s_lse")
        s_lt0, s_lc, s_lg, s_lth, s_lla = sem("s_lt0"), sem("s_lc"), sem("s_lg"), sem("s_lth"), sem("s_lla")
        s_la, s_lv, s_lsq, s_ly = sem("s_la"), sem("s_lv"), sem("s_lsq"), sem("s_ly")
        s_lb = sem("s_lb")
        s_lgl, s_lgt, s_loT, s_loE = sem("s_lgl"), sem("s_lgt"), sem("s_loT"), sem("s_loE")

        block = ctx.enter_context(nc.Block())

        def weights(st):
            i, name = st["layer"], st["name"]
            q = i // 3
            return {
                "xbc": lambda: t_in["ssd_w_in"][q][:, 2048:2048 + CONVD],
                "z": lambda: t_in["ssd_w_in"][q][:, 0:2048],
                "ssd_out": lambda: t_in["ssd_w_out"][q],
                "qkv": lambda: t_in["moba_w_qkv"][0],
                "wo": lambda: t_in["moba_w_o"][0],
                "lru_in": lambda: t_in["lru_w_in"][0],
                "lru_out": lambda: t_in["lru_w_out"][0],
                "up": lambda: t_in["mlp_w_up"][i],
                "down": lambda: t_in["mlp_w_down"][i],
                "gate": lambda: t_in["ple_w_gate"][i],
            }[name]()

        def sweep(eng, st, body, first=0, last=None, peel=False):
            unroll = 8 if st["kq"] == 4 else 4
            n = st["n"] // unroll if last is None else last
            if (peel or st["g0"] == 0) and first == 0:
                body(0)
                first = 1
            if n - first == 1:
                body(first)
            elif n > first:
                with eng.Fori(first, n) as it:
                    body(it)

        def unroll_of(st):
            return 8 if st["kq"] == 4 else 4

        def skewed(eng, n, front, back, mid=lambda g, b: None):
            front(0, 0)
            mid(0, 0)
            front(1, 1)
            back(0, 0)
            mid(1, 1)
            with eng.Fori(1, n // 2) as it:
                front(it * 2, 0)
                back(it * 2 - 1, 1)
                mid(it * 2, 0)
                front(it * 2 + 1, 1)
                back(it * 2, 0)
                mid(it * 2 + 1, 1)
            back(n - 1, 1)

        def mix_count(i):
            return sum(GROUPS if k in SSD_LAYERS else 1 for k in range(i + 1))

        def split_input(n):
            return (pin["pH"], pin["pL"]) if n % 3 == 2 else (xH, xL)

        def is_first(it):
            return isinstance(it, int) and it == 0

        def gain_col(n):
            return 96 if n == 3 * DEPTH else 32 * (n % 3) + KT * (n // 3)

        @block.sync
        def _(sp):
            def loads(st, first=0, last=None):
                w = weights(st)

                def body(it):
                    for u in range(unroll_of(st)):
                        r = it * unroll_of(st) + u
                        g = r + st["g0"]
                        if not (isinstance(g, int) and g < 4):
                            sp.wait_ge(s_lo, g - 3)
                        if st["kq"] == 1:
                            cols, kq = r * CHUNK, 0
                        else:
                            cols, kq = (it * (unroll_of(st) // st["kq"]) + u // st["kq"]) * CHUNK, u % st["kq"]
                        src = w[kq * D:(kq + 1) * D, ds(cols, CHUNK)]
                        sp.dma_start(raw[u % 4][:], src.rearrange("(k p) n -> p k n", p=P)).then_inc(s_raw[u % 4], 16)
                sweep(sp, st, body, first, last)

            outs = [0]

            def store(dst, src):
                outs[0] += 1
                sp.dma_start(dst, src).then_inc(s_out, 16)

            def stored():
                sp.wait_ge(s_out, 16 * outs[0])

            sp.wait_ge(s_load, 16 * 5)
            for i in range(DEPTH):
                q = i // 3
                if i in SSD_LAYERS:
                    loads(stage[i, "xbc"])
                    loads(stage[i, "z"])
                    loads(stage[i, "ssd_out"], 0, 1)
                    conv_p, conv_s = t_out["ssd_conv_p"][q], t_out["ssd_conv_s"][q]
                    store(conv_s[:, 0:2, :], t_in["state_ssd_conv"][q][:, 1:3, :])
                    src = t_in["state_ssd"][q].rearrange("b (i e) p n -> b (e p) i n", e=2)
                    sp.wait_ge(s_th, q + 1)
                    for n in range(3):
                        sp.dma_start(stx[n], src[n]).then_inc(s_sinA, 16)
                    dst = t_out["ssd_state_p"][q][0].rearrange("(i e) p n -> (e p) i n", e=2)

                    def put(g, b):
                        sp.wait_ge(s_yev, g + 1 + GROUPS * q)
                        sp.dma_start(dst[:, ds(g * 2, 2), :], grp[f"stout{b}"][:]).then_inc(s_sto[b], 16)
                    with sp.Fori(0, GROUPS // 2) as it:
                        put(it * 2, 0)
                        put(it * 2 + 1, 1)
                    for b in range(2):
                        sp.wait_ge(s_sto[b], 8 * GROUPS * (q + 1))
                    for n in range(3, NB):
                        sp.dma_start(stx[n], src[n]).then_inc(s_sinB, 16)
                    sdst = t_out["ssd_state_s"][q].rearrange("b (i e) p n -> b (e p) i n", e=2)
                    for n in range(NB):
                        sp.wait_ge(s_hn, n + 1 + NB * q)
                        sp.dma_start(sdst[n], stx[n]).then_inc(s_sout, 16)
                    loads(stage[i, "ssd_out"], 1)
                    sp.wait_ge(s_orE, 8 * (q + 1))
                    store(conv_p[0], orow["orow"][0:3, :])
                    store(conv_s[:, 2, :], orow["orow"][3:LAST, :])
                elif i == 1:
                    loads(stage[i, "qkv"])
                    loads(stage[i, "wo"])
                    kp = t_out["k_p"][0][0].rearrange("(c t) h d -> h t c d", c=2)
                    vp = t_out["v_p"][0][0].rearrange("(c t) h d -> h t c d", c=2)
                    with sp.Fori(0, MH // 2) as it:
                        for b in range(2):
                            sp.wait_ge(s_msc, it * 2 + (b + 1))
                            hd = ds(it * 2 + b, 1)
                            sp.dma_start(kp[hd].rearrange("o t c d -> t (o c) d"), mh[f"kvt{b}"][:, 0:2]).then_inc(s_kst[b], 16)
                            sp.dma_start(vp[hd].rearrange("o t c d -> t (o c) d"), mh[f"kvt{b}"][:, 2:4]).then_inc(s_kst[b], 16)
                    store(t_out["k_s"][0].rearrange("b s h d -> b (s h d)"), M["rowS"][:, 1, :])
                    store(t_out["v_s"][0].rearrange("b s h d -> b (s h d)"), M["rowS"][:, 2, :])
                else:
                    loads(stage[i, "lru_in"])
                    loads(stage[i, "lru_out"])
                    sp.wait_ge(s_loE, 2)
                    store(t_out["lru_conv_p"][0][0], L["lrow"][0:3, :])
                    store(t_out["lru_conv_s"][0][:, 2, :], L["lrow"][3:LAST, :])
                    store(t_out["lru_conv_s"][0][:, 0:2, :], t_in["state_lru_conv"][0][:, 1:3, :])
                    store(t_out["lru_state_p"][0], L["hrow"][0:1, :])
                    store(t_out["lru_state_s"][0], L["hrow"][1:9, :])
                stored()
                if i in SSD_LAYERS:
                    for b in range(2):
                        sp.wait_ge(s_sto[b], 8 * GROUPS * (q + 1))
                    sp.wait_ge(s_sout, 16 * NB * (q + 1))
                if i == 1:
                    for b in range(2):
                        sp.wait_ge(s_kst[b], 32 * MH // 2)
                sp.nop().then_inc(s_stored, 1)
                loads(stage[i, "up"])
                loads(stage[i, "down"])
                loads(stage[i, "gate"])
            sp.wait_ge(s_finE, 2)
            store(t_out["y_p"][0].rearrange("(c t) d -> t c d", c=2), fin["yrow"][:])
            store(t_out["y_s"].rearrange("b s d -> (b s) d"), fin["yrow8"][:])
            stored()

        @block.tensor
        def _(pe):
            mm = nc.tensor.matmul

            def tr(out, in_, k):
                return nc.tensor.transpose(out, in_, ident[0:k, 0:k])

            def norm_sum(n):
                pe.wait_ge(s_ssq, n + 1)
                mm(bank[0][:, 0:T], ones[:], ssq[:, 0, :], start=True, stop=False)
                mm(bank[0][:, 0:T], ones[:], ssq[:, 1, :], start=False, stop=True).then_inc(s_var, 1)

            def project(st, act_h, act_l, norm=None, ready=None, after=None, pairs=None):
                kq_n = st["kq"]
                U = unroll_of(st)

                def body(it):
                    for u in range(U):
                        g = it * U + (u + st["g0"])
                        col = it * (U // kq_n) + (u // kq_n + st["c0"])
                        p, kq = ((u // kq_n) + st["c0"]) % 2, u % kq_n
                        pe.wait_ge(s_lo, g + 1)
                        if kq == 0 and not (isinstance(col, int) and col < 2):
                            pe.wait_ge(s_ev, col - 1)
                        if ready:
                            ready(u)
                        for m in range(2):
                            for k in range(KT):
                                x = kq * KT + k
                                if pairs is not None and is_first(it) and u < 2 and m == 0 and k % 2 == 0:
                                    pe.wait_ge(s_mixl, pairs + x // 2 + 1)
                                if norm is not None and is_first(it) and u == 0 and m == 0 and k % 2 == 0:
                                    pe.wait_ge(s_xl, 4 * norm + k // 2 + 1)
                                w = slice(m * P, m * P + P)
                                first, last = kq == 0 and k == 0, kq == kq_n - 1 and k == KT - 1
                                o = G[p][:, m, 0:T]
                                mm(o, whi[u % 2][:, k, w], act_h[:, x, :], start=first, stop=False)
                                mm(o, wlo[u % 2][:, k, w], act_h[:, x, :], start=False, stop=False)
                                done = mm(o, whi[u % 2][:, k, w], act_l[:, x, :], start=False, stop=last)
                        done.then_inc(s_mm, 1)
                        if norm is not None and is_first(it) and u == 0:
                            norm_sum(norm)
                        if after:
                            after(it, u)
                sweep(nc.tensor, st, body, peel=norm is not None or pairs is not None)

            pe.wait_ge(s_const, 1)
            pe.wait_ge(s_load, 16 * 5)
            pe.wait_ge(s_load2, 16 * 13)
            for c in range(2):
                for k in range(KT):
                    tr(G[c][:, k // 4, (k % 4) * P:(k % 4 + 1) * P], A0["xrow"][:, c, k * P:(k + 1) * P], P)
            for k in range(KT):
                tr(bank[0][:, k * NB:(k + 1) * NB], A0["xrow8"][:, k * P:(k + 1) * P], NB)
            tr(bank[1][:, 0:104], A0["rowA"][:], 104)
            tr(bank[1][:, 128:224], A0["rowB"][:], 96)
            tr(bank[2][:, 0:128], A0["rowC"][:], P)
            tr(bank[2][:, 128:256], A0["rowD"][:], P)
            tr(bank[2][:, 256:320], A0["rowE"][:], 64).then_inc(s_tp0, 1)
            pe.wait_ge(s_init, 1)

            def ssd(i, q):
                def conv_state(it, u):
                    if is_first(it) and u == 1:
                        pe.wait_ge(s_wdt, 16 * (q + 1))
                        for k in range(KT):
                            t_ = mm(bank[1][0:HEADS, 0:T], hv_["wdt"][:, k, :], xg[:, k, :], start=(k == 0), stop=(k == KT - 1))
                        t_.then_inc(s_dtp, 1)
                    if not (is_first(it) and u == 0):
                        return
                    pe.wait_ge(s_cst, 16 * (q + 1))
                    for k in range(CT):
                        t_ = tr(bank[2 + k // 16][:, (k % 16) * 24:(k % 16 + 1) * 24],
                                cst["cst"][:, k * P:(k + 1) * P], 24)
                    t_.then_inc(s_cT, 1)
                project(stage[i, "xbc"], xH, xL, norm=3 * i, after=conv_state)
                project(stage[i, "z"], xH, xL)
                pe.wait_ge(s_dt5, q + 1)
                for c in range(2):
                    tr(bank[2][:, c * HEADS:(c + 1) * HEADS], hv_["dt"][:, c * P:(c + 1) * P], HEADS)
                    tr(bank[2][:, (2 + c) * HEADS:(3 + c) * HEADS], hv2["acum"][:, c * P:(c + 1) * P], HEADS)
                    tr(bank[2][:, (4 + c) * HEADS:(5 + c) * HEADS], dte_["dte"][:, c * P:(c + 1) * P], HEADS)
                mm(bank[3][:, 0:XT * 17], evenodd[:], hv_["R"][:].rearrange("h i v -> h (i v)"),
                   start=True, stop=True).then_inc(s_dt6, 1)
                pe.wait_ge(s_th, q + 1)

                def front(g, b):
                    pe.wait_ge(s_stg, g + 1 + GROUPS * q)
                    if not (isinstance(g, int) and g == 0):
                        pe.wait_ge(s_xd, g + GROUPS * q)
                    else:
                        pe.wait_ge(s_dt7, q + 1)
                    stg = grp[f"stg{b}"]
                    for c in range(2):
                        for t in range(2):
                            tr(bank[0][:, (2 * c + t) * P:(2 * c + t + 1) * P], stg[:, t, c * P:(c + 1) * P], P)
                        tr(bank[1][:, c * P:(c + 1) * P], stg[:, 2, c * P:(c + 1) * P], P)
                    xc = Z["xbc"]
                    cg = xc[:, ds(g + 24, 1), 0:SEQ].rearrange("p o t -> p (o t)")
                    mm(bank[2][:, 0:SEQ], stg[:, 2, 0:P], cg, start=True, stop=True)
                    mm(bank[2][:, SEQ:3 * P], stg[:, 2, P:SEQ],
                       xc[:, ds(g + 24, 1), P:SEQ].rearrange("p o t -> p (o t)"), start=True, stop=True).then_inc(s_tp, 1)
                    pe.wait_ge(s_sel, g + 1 + GROUPS * q)
                    if not (isinstance(g, int) and g == 0):
                        pe.wait_ge(s_seg, g + GROUPS * q)
                    for r in range(4):
                        t_ = mm(G[0][:, r // 2, (r % 2) * SEQ:(r % 2 + 1) * SEQ], grp[f"sel{b}"][:, r, :], hv2["acum"][:],
                                start=True, stop=True)
                    t_.then_inc(s_ar, 1)

                def back(g, b):
                    pe.wait_ge(s_M, g + 1 + GROUPS * q)
                    pe.wait_ge(s_M2, g + 1 + GROUPS * q)
                    pe.wait_ge(s_xde, g + 1 + GROUPS * q)
                    if not (isinstance(g, int) and g == 0):
                        pe.wait_ge(s_yev, g + GROUPS * q)
                    w, xd, xde = grp[f"seg{b}"], grp[f"xd{b}"], grp[f"xde{b}"]
                    for r in range(4):
                        o = G[1][64 * (r % 2):64 * (r % 2) + 64, r // 2, 0:SEQ]
                        mm(o, xd[:, 0, r, :], w[:, r, 0:SEQ], start=True, stop=False)
                        mm(G[1][64 * (r % 2):64 * (r % 2) + 64, r // 2, P:SEQ], xd[:, 1, r, :], w[:, r, SEQ:3 * P],
                           start=False, stop=True)
                    for t in range(2):
                        for c in range(2):
                            t_ = mm(G[1][:, t, SEQ:3 * P], xde[:, c, 2 * t:2 * t + 2, :].rearrange("s r p -> s (r p)"),
                                    grp[f"btm{b}"][:, c, :], start=(c == 0), stop=(c == 1), skip_group_check=True)
                    t_.then_inc(s_back, 1)
                skewed(nc.tensor, GROUPS, front, back)

                pe.wait_ge(s_yev, GROUPS * (q + 1))
                for k in range(16):
                    t_ = tr(bank[k // 4][0:NB, (k % 4) * P:(k % 4 + 1) * P], Z["xbc"][:, XT + k, SEQ:T], P)
                t_.then_inc(s_brT, 1)
                pe.wait_ge(s_brE, q + 1)
                with nc.tensor.Fori(0, NB // 2) as it:
                    for b in range(2):
                        pe.wait_ge(s_ssel, it * 2 + (b + 1 + NB * q))
                        pe.wait_ge(s_ot, it * 2 + (b + (NB + 2) * q + 1))
                        for c in range(4):
                            if c == 2:
                                pe.wait_ge(s_bcf, it * 2 + (b + (NB + 2) * q + 1))
                            mm(bank[4 * b + c], hv2[f"selS{b}"][:], bcr["bcH"][:, c * 512:(c + 1) * 512], start=True, stop=False)
                            t_ = mm(bank[4 * b + c], hv2[f"selS{b}"][:], bcr["bcL"][:, c * 512:(c + 1) * 512],
                                    start=False, stop=True)
                            if c == 1:
                                t_.then_inc(s_bb, 1)
                        t_.then_inc(s_bc, 1)
                for g in range(GROUPS):
                    pe.wait_ge(s_yss, GROUPS * q + g + 1)
                    t_ = mm(bank[0][0:GROUPS, 0:T], gsel[:, g, :], ysq["ysq"][:, 2 * g, :], start=(g == 0), stop=(g == GROUPS - 1))
                t_.then_inc(s_gv, 1)
                pe.wait_ge(s_grow, q + 1)
                pe.wait_ge(s_gs, q + 1)
                for g in range(GROUPS):
                    if g >= 4:
                        pe.wait_ge(s_yn, GROUPS * q + g - 3)
                    mm(bank[g % 4][:, 0:T], grow[:, g * P:(g + 1) * P], gnb["grs"][:], start=True, stop=True).then_inc(s_gb, 1)

                def conv_rows(it, u):
                    if not (is_first(it) and u in (1, 2)):
                        return
                    if u == 2:
                        pe.wait_ge(s_orE, 8 * q + 4)
                    for k in range(16):
                        t_ = tr(bank[k // 4][0:LAST, (k % 4) * P:(k % 4 + 1) * P], S["rawlast"][:, 16 * (u - 1) + k, :], P)
                        if k % 4 == 3:
                            t_.then_inc(s_orT, 1)
                project(stage[i, "ssd_out"], ysp["yH"], ysp["yL"], after=conv_rows, pairs=mix_count(i) - GROUPS)

            def moba():
                project(stage[1, "qkv"], xH, xL, norm=3)

                def front(hh, b):
                    pe.wait_ge(s_stq, hh + 1)
                    if not (isinstance(hh, int) and hh < 2):
                        pe.wait_ge(s_msc, hh - 1)
                    stq = mh[f"stq{b}"]
                    b0, b1, b2 = head_banks[b]
                    for j in range(4):
                        tr(b0[:, j * P:(j + 1) * P], stq[:, 1 + j // 2, (j % 2) * P:(j % 2 + 1) * P], P)
                    for j in range(3):
                        tr(b1[0:NB, j * P:(j + 1) * P], stq[:, j, SEQ:T], P)
                    mm(b2[:, 0:P], stq[:, 0, 0:P], stq[:, 1, 0:P], start=True, stop=True)
                    mm(b2[:, P:3 * P], stq[:, 0, P:SEQ], stq[:, 1, 0:SEQ], start=True, stop=True).then_inc(s_mtp, 1)

                def back(hh, b):
                    pe.wait_ge(s_mP, hh + 1)
                    if not (isinstance(hh, int) and hh == 0):
                        pe.wait_ge(s_mpt, hh)
                    for j in range(3):
                        t_ = tr(bank[3][:, j * P:(j + 1) * P], mh[f"sc{b}"][:, j * P:(j + 1) * P], P)
                    t_.then_inc(s_mpT, 1)
                    pe.wait_ge(s_mpt, hh + 1)
                    if not (isinstance(hh, int) and hh == 0):
                        pe.wait_ge(s_moe, hh)
                    mm(bank[4][:, 0:SEQ], mh[f"kvt{b}"][:, 2, :], mh[f"pt{b}"][:, 0:SEQ], start=True, stop=False)
                    mm(bank[4][:, P:SEQ], mh[f"kvt{b}"][:, 3, :], mh[f"pt{b}"][:, SEQ:3 * P],
                       start=False, stop=True).then_inc(s_mo, 1)
                skewed(nc.tensor, MH, front, back)
                pe.wait_ge(s_moe, MH)
                pe.wait_ge(s_qk, 1)
                mm(bank[4][0:64, 0:1], ms["qk"][:].rearrange("p b h -> p (b h)"), ones[:, 0:1],
                   start=True, stop=True).then_inc(s_sown, 1)
                with nc.tensor.Fori(0, NB // 2) as it:
                    for b in range(2):
                        pe.wait_ge(s_qsel, it * 2 + (b + 1))
                        pe.wait_ge(s_kd, it * 16 + (8 * b + 8))
                        for c in range(2):
                            t_ = mm(A[b][:, c, :], ms["qsel"][:], M["rowS"][:, 0, c * 512:(c + 1) * 512],
                                    start=True, stop=True)
                        t_.then_inc(s_qbc, 1)
                pe.wait_ge(s_kd, 17 + NB * PAGES)
                for j in range(PAGES):
                    t_ = tr(A[0][0:64, j // 4, (j % 4) * P:(j % 4 + 1) * P], ms["sS"][:, j, :], P)
                t_.then_inc(s_sT, 1)
                pe.wait_ge(s_sP, 1)
                for j in range(PAGES):
                    tr(bank[2][:, j * 64:(j + 1) * 64], ms["sR"][:, j * P:(j + 1) * P], 64)
                mm(bank[5][:, 0:64], ones[0:64, :], ms["dg"][:], start=True, stop=True).then_inc(s_sPT, 1)
                pe.wait_ge(s_ptn, 1)
                for c in range(2):
                    mm(G[1][0:64, c, :], zeros[:], ms["pT8"][:].rearrange("p j c -> p (j c)"),
                       start=True, stop=False, skip_group_check=True)
                with nc.tensor.Fori(0, NB // 2) as it:
                    for b in range(2):
                        pe.wait_ge(s_ptn, it * 2 + (b + 1))
                        pb = pn[:, b]
                        for j in range(PAGES):
                            pe.wait_ge(s_vl, it * 16 + (8 * b + j + 1))
                            for c in range(2):
                                o = G[1][0:64, c, :]
                                mm(o, pb[:, 0, j, :], vH[j % 4][:, c, :], start=False, stop=False, skip_group_check=True)
                                mm(o, pb[:, 1, j, :], vH[j % 4][:, c, :], start=False, stop=False, skip_group_check=True)
                                t_ = mm(o, pb[:, 0, j, :], vL[j % 4][:, c, :], start=False, stop=False, skip_group_check=True)
                            t_.then_inc(s_vd, 1)
                pe.wait_ge(s_vo, 2)
                for hh in range(MH):
                    t_ = tr(bank[2][:, hh * 64:(hh + 1) * 64], ms["sR"][:, hh * P:(hh + 1) * P], 64)
                t_.then_inc(s_vt, 1)
                pe.wait_ge(s_mixl, mix_count(1))
                project(stage[1, "wo"], ao["oH"], ao["oL"])

            def lru():
                def states(it, u):
                    if not (is_first(it) and u == 3):
                        return
                    pe.wait_ge(s_lld, 16 * 4)
                    for k in range(KT):
                        tr(bank[2][:, k * 24:(k + 1) * 24], L["lcst"][:, k * P:(k + 1) * P], 24)
                    for k in range(KT):
                        t_ = tr(bank[2][:, 192 + k * 8:200 + k * 8], L["lst"][:, k * P:(k + 1) * P], 8)
                    t_.then_inc(s_lT, 1)
                def gates(n):
                    pe.wait_ge(s_lc, n + 1)
                    if n == 0:
                        pe.wait_ge(s_lTe, 1)
                    if n >= 2:
                        pe.wait_ge(s_lth, n - 1)
                    mm(A[n % 2][:, 0, 0:T], L["wax"][:, n, :], L["xc"][:, n, :], start=True, stop=True)
                    mm(A[n % 2][:, 1, 0:T], L["wax"][:, 8 + n, :], L["xc"][:, n, :], start=True, stop=True).then_inc(s_lg, 1)

                def after_in(it, u):
                    states(it, u)
                    if not is_first(it) and u:
                        gates(2 * u - 2)
                        gates(2 * u - 1)
                project(stage[2, "lru_in"], xH, xL, norm=6, after=after_in)
                gates(KT - 2)
                gates(KT - 1)

                def rows(it, u):
                    if u:
                        return
                    pe.wait_ge(s_lth, KT)
                    for k in range(KT):
                        tr(A[0][0:LAST, k // 4, (k % 4) * P:(k % 4 + 1) * P], L["XR"][:, k, 256:256 + LAST], P)
                    for k in range(KT):
                        t_ = tr(A[1][0:9, k // 4, (k % 4) * P:(k % 4 + 1) * P], L["hs"][:, k, 255:T], P)
                    t_.then_inc(s_loT, 1)
                pe.wait_ge(s_mixl, mix_count(2))
                project(stage[2, "lru_out"], lo_["oH"], lo2["oL"], after=rows)

            def mlp_ple(i):
                project(stage[i, "up"], xH, xL, norm=3 * i + 1)

                pe.wait_ge(s_ple, 48 * (i + 1))
                pe.wait_ge(s_std, 3 * i + 2)
                for k in range(2):
                    for c in range(2):
                        tr(A[0][:, k, c * P:(c + 1) * P], ml["prow"][:, c, k * P:(k + 1) * P], P)
                    t_ = tr(A[0][:, k, SEQ:T], ml["prow8"][:, k * P:(k + 1) * P], NB)
                t_.then_inc(s_pT, 1)

                def acts(u):
                    if u < 4:
                        pe.wait_ge(s_aL, 16 * i + 4 * (u + 1))
                project(stage[i, "down"], aH, aL, ready=acts)
                pe.wait_ge(s_pTe, i + 1)

                def proj(u):
                    if u == 1:
                        pe.wait_ge(s_std, 3 * i + 3)
                    if u >= 2:
                        pe.wait_ge(s_pje, 4 * i + u - 1)
                    for m in range(2):
                        for k in range(2):
                            t_ = mm(A[(u + 1) % 2][:, m, 0:T], ml["wp"][:, k, (2 * u + m) * P:(2 * u + m + 1) * P],
                                    ml["pT"][:, k, :], start=(k == 0), stop=(k == 1))
                    t_.then_inc(s_pj, 1)

                def before(u):
                    if u in (0, 3):
                        proj(u)

                def after(it, u):
                    if u in (1, 2):
                        proj(u)
                project(stage[i, "gate"], pin["pH"], pin["pL"], norm=3 * i + 2, ready=before, after=after)

            for i in range(DEPTH):
                if i in SSD_LAYERS:
                    ssd(i, i // 3)
                elif i == 1:
                    moba()
                else:
                    lru()
                mlp_ple(i)
            norm_sum(12)
            pe.wait_ge(s_std, 13)
            for k in range(KT):
                pe.wait_ge(s_fin, k + 1)
                for c in range(2):
                    tr(G[c][:, k // 4, (k % 4) * P:(k % 4 + 1) * P], fin["yfin"][:, k, c * P:(c + 1) * P], P)
                t_ = tr(A[1][0:NB, k // 4, (k % 4) * P:(k % 4 + 1) * P], fin["yfin"][:, k, SEQ:T], P)
            t_.then_inc(s_finT, 1)

        @block.scalar
        def _(act):
            fn = nc.scalar.activation

            def split(st, it, u):
                U = unroll_of(st)
                g = it * U + (u + st["g0"])
                if isinstance(g, int) and g + 2 >= total:
                    return
                turn = it * (U // 4) + (st["g0"] // 4 + (u + 2) // 4)
                act.wait_ge(s_raw[(u + 2) % 4], turn * 16 + 16)
                act.wait_ge(s_mm, g + 1)
                fn(whi[u % 2][:], raw[(u + 2) % 4][:], ACT.Copy).then_inc(s_hi, 1)

            def root(n):
                act.wait_ge(s_var, n + 1)
                fn(rstd[:], bank[0][:, 0:T], ACT.Sqrt, scale=1.0 / D, bias=epsc[:, 0:1]).then_inc(s_std, 1)

            def splits(st, evac=None, norm=None, extra=None):
                def body(it):
                    for u in range(unroll_of(st)):
                        split(st, it, u)
                        if norm is not None and is_first(it) and u == 0:
                            root(norm)
                            if extra:
                                extra()
                        if evac:
                            evac(it * unroll_of(st) + u, u)
                sweep(nc.scalar, st, body, peel=norm is not None)

            def high(n, r):
                if n == 3 * DEPTH:
                    return
                act.wait_ge(s_xg, r + (4 * n + 1))
                fn(split_input(n)[0][:, ds(r * 2, 2), :], xg[:, ds(r * 2, 2), :], ACT.Copy).then_inc(s_xh, 1)

            def splits_out(st, n, after=None):
                def body(it):
                    U, kq_n = unroll_of(st), st["kq"]
                    for u in range(U):
                        whole, r = u % kq_n == kq_n - 1, it * (U // kq_n) + u // kq_n
                        if u == U - 1:
                            high(n, r)
                        split(st, it, u)
                        if whole and u < U - 1:
                            high(n, r)
                        if after:
                            after(it, u)
                sweep(nc.scalar, st, body, peel=after is not None)

            def stored(i):
                act.wait_ge(s_stored, i + 1)

            for dst, src in (
                (A0["xrow"][:], t_in["x_prompt"][0].rearrange("(c t) d -> t c d", c=2)),
                (A0["xrow8"][:], t_in["x_sample"].rearrange("b s d -> (b s) d")),
                (A0["rowC"][:], t_in["ssd_conv_w"][0].rearrange("k (j p) -> (k j) p", p=P)),
                (A0["rowD"][:], t_in["ssd_conv_w"][1].rearrange("k (j p) -> (k j) p", p=P)),
                (A0["rowE"][:], t_in["ssd_conv_b"].rearrange("q (j p) -> (q j) p", p=P)),
            ):
                act.dma_start(dst, src).then_inc(s_load, 16)
            at_row = 0
            for name in ("norm_mix", "norm_mlp", "norm_ple"):
                act.dma_start(A0["rowA"][at_row:at_row + 32, :], t_in[name].rearrange("i (k p) -> (i k) p", p=P)).then_inc(s_load2, 16)
                at_row += 32
            act.dma_start(A0["rowA"][96:104, :], t_in["norm_final"].rearrange("(k p) -> k p", p=P)).then_inc(s_load2, 16)
            act.dma_start(A0["rowB"][0:32, :], t_in["lru_conv_w"][0].rearrange("k (j p) -> (k j) p", p=P)).then_inc(s_load2, 16)
            act.dma_start(A0["rowB"][32:40, :], t_in["lru_conv_b"][0].rearrange("(k p) -> k p", p=P)).then_inc(s_load2, 16)
            act.dma_start(A0["rowB"][40:48, :], t_in["lru_lambda"][0].rearrange("(k p) -> k p", p=P)).then_inc(s_load2, 16)
            act.dma_start(A0["rowB"][48:56, :], t_in["lru_b_a"][0]).then_inc(s_load2, 16)
            act.dma_start(A0["rowB"][56:64, :], t_in["lru_b_x"][0]).then_inc(s_load2, 16)
            act.dma_start(A0["rowB"][64:96, :], t_in["ssd_norm"].rearrange("q (j p) -> (q j) p", p=P)).then_inc(s_load2, 16)
            for k, name in enumerate(("ssd_dt_bias", "ssd_a_log", "ssd_d")):
                act.dma_start(hsm[:, 2 * k:2 * k + 2], t_in[name].rearrange("q h -> h q"), allow_slow_non_contiguous=True).then_inc(s_load2, 16)
            for u in range(2):
                act.wait_ge(s_raw[u], 16)
                fn(whi[u][:], raw[u][:], ACT.Copy).then_inc(s_hi, 1)
            for r in range(4):
                high(0, r)

            def ssd(i, q):
                xbc, zs, seq = Z["xbc"], Z["zs"], slice(0, SEQ)
                c0 = stage[i, "xbc"]["c0"]

                def tap(r, u):
                    act.wait_ge(s_ev, r + (c0 + 1))
                    for t in range(2):
                        tile = r * 2 + t
                        f = fn(xbc[:, ds(tile, 1), seq].rearrange("p o t -> p (o t)"), S[f"T{u % 2}"][:, t, seq], ACT.Identity,
                               bias=colE[:, ds(tile + CT * q, 1)], scale=colC[:, q, ds(tile, 1)])
                    f.then_inc(s_tap, 1)
                    fn(S["rawlast"][:, ds(r * 2, 2), :], S[f"T{u % 2}"][:, :, SEQ:SEQ + LAST], ACT.Copy).then_inc(s_last, 1)
                    if isinstance(r, int) and r == 1:
                        act.wait_ge(s_dt1, q + 1)
                        fn(spl["sp2"][:], spl["sp1"][:], ACT.Exp)
                        fn(hv2["bvec"][:, 0:1], hsm[:, 2 + q:3 + q], ACT.Exp).then_inc(s_dt2, 1)
                splits(stage[i, "xbc"], tap, norm=3 * i)
                act.wait_ge(s_dt3, q + 1)
                fn(hv2["vals"][:, 8:16], hv_["dA"][:, SEQ:T], ACT.Exp)
                fn(dte_["dte"][:], hv2["acum"][:], ACT.Exp, scale=-1.0, bias=hv2["acum"][:, SEQ - 1:SEQ]).then_inc(s_dt4, 1)
                act.wait_ge(s_conv, 17 * (q + 1))
                act.wait_ge(s_last, 16 * (q + 1))
                z0 = stage[i, "z"]["c0"]

                def silus(r, u):
                    b = u % 2
                    act.wait_ge(s_ev, r + (z0 + 1))
                    fn(S[f"T{b}"][:, :, 0:T], zs[:, ds(r * 2, 2), :], ACT.Tanh, scale=0.5).then_inc(s_zth, 1)
                    if not (isinstance(r, int) and r < 2 and q == 0):
                        act.wait_ge(s_silu, r + (8 * q - 1))
                    fn(xth[f"xth{b}"][:], xbc[:, ds(r * 4, 4), :], ACT.Tanh).then_inc(s_xth, 1)
                z = stage[i, "z"]
                def z_body(it):
                    for u in range(4):
                        last = it * 4 + u == 7
                        if not last:
                            split(z, it, u)
                        silus(it * 4 + u, u)
                        if last:
                            split(z, it, u)
                z_body(0)
                z_body(1)
                act.wait_ge(s_dt7, q + 1)

                def stage_in(g, b):
                    if not (isinstance(g, int) and g < 2):
                        act.wait_ge(s_tp, g + (GROUPS * q - 1))
                        act.wait_ge(s_ar, g + (GROUPS * q - 1))
                    fn(grp[f"stg{b}"][:, 0:2, :], xbc[:, ds(g * 2, 2), seq], ACT.Copy)
                    fn(grp[f"stg{b}"][:, 2, :], xbc[:, ds(g + XT, 1), seq].rearrange("p o t -> p (o t)"), ACT.Copy).then_inc(s_stg, 1)
                    fn(grp[f"sel{b}"][:], ident[0:HEADS, ds(g * 4, 4)].unsqueeze(2).to_broadcast([HEADS, 4, P]), ACT.Copy).then_inc(s_sel, 1)

                def decays(g, b):
                    act.wait_ge(s_seg, g + (GROUPS * q + 1))
                    fn(grp[f"seg{b}"][:], grp[f"seg{b}"][:], ACT.Exp).then_inc(s_exp, 1)
                def two_groups(it):
                    stage_in(it * 2 + 1, 1)
                    decays(it * 2, 0)
                    stage_in(it * 2 + 2, 0)
                    decays(it * 2 + 1, 1)
                stage_in(0, 0)
                two_groups(0)
                with nc.scalar.Fori(1, GROUPS // 2 - 1) as it:
                    two_groups(it)
                stage_in(GROUPS - 1, 1)
                decays(GROUPS - 2, 0)
                decays(GROUPS - 1, 1)
                act.wait_ge(s_brT, q + 1)
                for a in range(2):
                    fn(bcr["bcH"][:, a * D:(a + 1) * D], A[a][0:NB].rearrange("b a n -> b (a n)"), ACT.Copy).then_inc(s_brH, 1)
                def decayed(n):
                    for t in range(XT):
                        blk = stt[:, ds(n * -1 + (NB - 1), 1), t * P:(t + 1) * P].rearrange("p o n -> p (o n)")
                        f = fn(blk, blk, ACT.Copy, scale=hv2["hv"][:, t, ds(n + 8, 1)])
                    f.then_inc(s_hd, 1)
                act.wait_ge(s_sinA, 16 * 3 * (q + 1))
                with nc.scalar.Fori(0, 3) as n:
                    decayed(n)
                act.wait_ge(s_sinB, 16 * (NB - 3) * (q + 1))
                with nc.scalar.Fori(3, NB) as n:
                    decayed(n)
                act.wait_ge(s_yz, q + 1)
                for g in range(GROUPS):
                    fn(ysq["ysq"][:, 2 * g:2 * g + 2, :], zs[:, 2 * g:2 * g + 2, :], ACT.Square).then_inc(s_ysq, 1)
                act.wait_ge(s_gv, q + 1)
                fn(gnb["grs"][:], bank[0][0:GROUPS, 0:T], ACT.Sqrt, scale=1.0 / 256, bias=epsc[0:GROUPS, 0:1]).then_inc(s_gr, 1)
                act.wait_ge(s_sout, 16 * NB * (q + 1))
                with nc.scalar.Fori(0, GROUPS) as g:
                    act.wait_ge(s_yn, g + (GROUPS * q + 1))
                    fn(ysp["yH"][:, ds(g * 2, 2), :], zs[:, ds(g * 2, 2), :], ACT.Copy).then_inc(s_yh, 1)

                def conv_rows(it, u):
                    if is_first(it) and u in (1, 2):
                        for k in range(4):
                            act.wait_ge(s_orT, 8 * q + 4 * (u - 1) + k + 1)
                            half = slice((4 * u + k - 4) * 512, (4 * u + k - 3) * 512)
                            fn(orow["orow"][:, half], bank[k][0:LAST, :], ACT.Copy).then_inc(s_orE, 1)
                splits_out(stage[i, "ssd_out"], 3 * i + 1, after=conv_rows)

            def moba():
                splits(stage[1, "qkv"], norm=3)
                act.wait_ge(s_ev, stage[1, "qkv"]["c0"] + 12)
                heads = M["qkv"][:].rearrange("p (j t) x -> p j t x", j=3)

                def stage_head(hh, b):
                    if not (isinstance(hh, int) and hh < 2):
                        act.wait_ge(s_mtp, hh - 1)
                    fn(mh[f"stq{b}"][:], heads[:, :, ds(hh, 1), :].rearrange("p j o x -> p (j o) x"), ACT.Copy).then_inc(s_stq, 1)

                def back(hh, b):
                    act.wait_ge(s_mpT, hh + 1)
                    if not (isinstance(hh, int) and hh < 2):
                        act.wait_ge(s_mo, hh - 1)
                    fn(mh[f"pt{b}"][:], bank[3][:, 0:3 * P], ACT.Copy).then_inc(s_mpt, 1)

                def mid(hh, b):
                    act.wait_ge(s_msc, hh + 1)
                    sc, nm, rs = mh[f"sc{b}"], mh[f"nm{b}"], mh[f"rs{b}"]
                    fn(sc[:, 0:P], sc[:, 0:P], ACT.Exp, scale=SCALE, bias=nm[:, 0:1], accum_out=rs[:, 0:1])
                    fn(sc[:, P:3 * P], sc[:, P:3 * P], ACT.Exp, scale=SCALE, bias=nm[:, 1:2], accum_out=rs[:, 1:2]).then_inc(s_mex, 1)
                def turn(hh, b):
                    stage_head(hh + 1, 1 - b)
                    back(hh - 1, 1 - b)
                    mid(hh, b)
                stage_head(0, 0)
                stage_head(1, 1)
                mid(0, 0)
                turn(1, 1)
                turn(2, 0)
                with nc.scalar.Fori(1, MH // 2 - 1) as it:
                    turn(it * 2 + 1, 1)
                    turn(it * 2 + 2, 0)
                back(MH - 2, 0)
                mid(MH - 1, 1)
                back(MH - 1, 1)
                with nc.scalar.Fori(0, NB // 2) as it:
                    for b in range(2):
                        for j in range(PAGES):
                            act.wait_ge(s_km, it * 16 + (8 * b + j + 1))
                            for hh in range(4):
                                f = fn(pg[f"pg{j}"][:, hh, :], pg[f"pg{j}"][:, hh, :], ACT.Copy, accum_out=ms[f"sq{b}"][:, j, hh:hh + 1])
                            f.then_inc(s_ka, 1)
                act.wait_ge(s_sR, 1)
                fn(ms["sR"][:, 0:1025], ms["sR"][:, 0:1025], ACT.Exp, scale=SCALE, bias=ms["gsc"][:, 2:3],
                   accum_out=ms["gsc"][:, 3:4]).then_inc(s_sE, 1)
                def value_high(n, j, seen):
                    act.wait_ge(s_pg[j], n * 16 + (16 + 16 * NB))
                    if seen:
                        act.wait_ge(s_vd, n * PAGES + (j - 3))
                    fn(vH[j % 4][:], pg[f"pg{j}"][:].rearrange("p (c h) d -> p c (h d)", c=2), ACT.Copy).then_inc(s_vh, 1)
                for j in range(PAGES):
                    value_high(0, j, j >= 4)
                with nc.scalar.Fori(1, NB) as it:
                    for j in range(PAGES):
                        value_high(it, j, True)
                act.wait_ge(s_vd, NB * PAGES)
                fn(ms["sR"][:, 0:512], G[1][0:64, 0, :], ACT.Copy).then_inc(s_vo, 1)
                for part, cols in enumerate((slice(0, SEQ), slice(SEQ, T))):
                    act.wait_ge(s_att, part + 1)
                    fn(ao["oH"][:, :, cols], M["att"][:, :, cols], ACT.Copy).then_inc(s_mixh, 1)
                splits_out(stage[1, "wo"], 4)

            def lru():
                st = stage[2, "lru_in"]
                XR, xc, thr, la = L["XR"], L["xc"], L["thr"], L["la"]

                def gate_tanh(k):
                    act.wait_ge(s_lg, k + 1)
                    fn(thr[:, k, :], A[k % 2][:, 0, 0:T], ACT.Tanh, scale=0.5, bias=lsp["bah"][:, k:k + 1])
                    fn(L["thi"][:, k, :], A[k % 2][:, 1, 0:T], ACT.Tanh, scale=0.5, bias=lsp["bxh"][:, k:k + 1]).then_inc(s_lth, 1)
                for u in range(4):
                    split(st, 0, u)
                    if u == 0:
                        root(6)
                    if u:
                        act.wait_ge(s_lgl, u)
                        fn(L["a2"][:, 2 * u - 2:2 * u, :], L["a2"][:, 2 * u - 2:2 * u, :], ACT.Tanh, scale=GELU_A).then_inc(s_lgt, 1)
                halves = (slice(0, 4), slice(4, 8))

                def decay_parts(n):
                    s4 = halves[n]
                    act.wait_ge(s_lla, n + 1)
                    fn(thr[:, s4], la[:, s4], ACT.Tanh, scale=-1.0)
                    fn(L["a2"][:, s4], la[:, s4], ACT.Exp, scale=2.0).then_inc(s_la, 1)
                    fn(la[:, s4], la[:, s4], ACT.Exp).then_inc(s_lb, 1)
                for u in range(4):
                    if u < 3:
                        split(st, 1, u)
                    if u == 0:
                        act.wait_ge(s_lgl, 4)
                        fn(L["a2"][:, 6:8, :], L["a2"][:, 6:8, :], ACT.Tanh, scale=GELU_A).then_inc(s_lgt, 1)
                    act.wait_ge(s_ev, st["c0"] + 4 + u + 1)
                    for k in (2 * u, 2 * u + 1):
                        fn(xc[:, k, 0:SEQ], XR[:, k, 0:SEQ], ACT.Identity, bias=colB[:, 32 + k:33 + k], scale=colB[:, k:k + 1]).then_inc(s_lt0, 1)
                    if u:
                        gate_tanh(2 * u - 2)
                        gate_tanh(2 * u - 1)
                decay_parts(0)
                gate_tanh(KT - 2)
                gate_tanh(KT - 1)
                decay_parts(1)
                for n, s4 in enumerate(halves):
                    act.wait_ge(s_lv, n + 1)
                    fn(thr[:, s4], thr[:, s4], ACT.Sqrt).then_inc(s_lsq, 1)
                for n, s4 in enumerate(halves):
                    act.wait_ge(s_ly, n + 1)
                    fn(lo_["oH"][:, s4], xc[:, s4], ACT.Copy).then_inc(s_mixh, 1)
                split(st, 1, 3)

                def rows(it, u):
                    if u:
                        return
                    act.wait_ge(s_loT, 1)
                    fn(L["lrow"][:], A[0][0:LAST].rearrange("p a n -> p (a n)"), ACT.Copy).then_inc(s_loE, 1)
                    fn(L["hrow"][:], A[1][0:9].rearrange("p a n -> p (a n)"), ACT.Copy).then_inc(s_loE, 1)
                splits_out(stage[2, "lru_out"], 7, after=rows)

            def mlp_ple(i):
                stored(i)
                c0 = stage[i, "up"]["c0"]

                def square(r, u):
                    b = u % 2
                    act.wait_ge(s_mm, r + (stage[i, "up"]["g0"] + 1))
                    if not (isinstance(r, int) and r < 2 and i == 0):
                        act.wait_ge(s_ac, r + (16 * i - 1))
                    fn(ml[f"rl{b}"][:], G[b][:, :, 0:T], ACT.Relu).then_inc(s_ev, 1)
                    act.wait_ge(s_ev, r + (c0 + 1))
                    fn(aH[:, ds(r * 2, 2), :], ml[f"rl{b}"][:], ACT.Square).then_inc(s_aH, 1)

                def up_body(it):
                    for u in range(4):
                        split(stage[i, "up"], it, u)
                        square(it * 4 + u, u)
                        if is_first(it) and u == 0:
                            root(3 * i + 1)
                up_body(0)
                with nc.scalar.Fori(1, 4) as it:
                    up_body(it)
                if i == 1:
                    act.wait_ge(s_lsp, 1)
                    fn(lsp["lp2"], lsp["lp1"], ACT.Exp).then_inc(s_lse, 1)
                splits_out(stage[i, "down"], 3 * i + 2)
                g0 = stage[i, "gate"]["c0"]
                for u in range(4):
                    if u == 0:
                        split(stage[i, "gate"], 0, u)
                        root(3 * i + 2)
                    act.wait_ge(s_ev, g0 + u + 1)
                    fn(ml["t1"][:], ml["t1"][:], ACT.Tanh, scale=0.5).then_inc(s_tg, 1)
                    if u in (1, 2):
                        split(stage[i, "gate"], 0, u)
                    high(3 * i + 3, u)
                    if u == 3:
                        split(stage[i, "gate"], 0, u)

            for i in range(DEPTH):
                if i in SSD_LAYERS:
                    ssd(i, i // 3)
                elif i == 1:
                    moba()
                else:
                    lru()
                mlp_ple(i)
            root(12)
            act.wait_ge(s_finT, 1)
            fn(fin["yrow"][:, 0, :], G[0][:].rearrange("p a b -> p (a b)"), ACT.Copy)
            fn(fin["yrow8"][:], A[1][0:NB].rearrange("p a b -> p (a b)"), ACT.Copy).then_inc(s_finE, 1)

        @block.gpsimd
        def _(pool):
            gp = nc.gpsimd
            gp.memset(ident[:], 0.0)
            gp.memset(ones[:], 1.0)
            gp.memset(zeros[:], 0.0)
            gp.memset(tri[:], 1.0)
            gp.memset(amask[:], 0.0)
            gp.memset(epsc[:], EPS)
            gp.memset(gsel[:], 0.0)
            for n in range(BLOCKS):
                gp.memset(blockno[:, n:n + 1], float(n + 1))
            pool.drain()
            gp.memset(gsel[:].rearrange("p g c -> p (g c)")[:, ::GROUPS + 1], 1.0)
            gp.affine_select(out=ident[:], in_=ident[:], compare_op=ALU.not_equal, fill=1.0, base=0,
                             pattern=[[-1, P]], channel_multiplier=1)
            for blk in (0, 2):
                c = slice(blk * P, blk * P + P)
                gp.affine_select(out=tri[:, c], in_=tri[:, c], compare_op=ALU.is_ge, fill=0.0, base=0,
                                 pattern=[[1, P]], channel_multiplier=-1)
                f = gp.affine_select(out=amask[:, c], in_=amask[:, c], compare_op=ALU.is_ge, fill=-BIG, base=0,
                                     pattern=[[-1, P]], channel_multiplier=1)
            f.then_inc(s_const, 1)

            def squares(n):
                for r in range(4):
                    pool.wait_ge(s_xg, 4 * n + r + 1)
                    hr = h[:, 2 * r:2 * r + 2, :]
                    if r == 0:
                        gp.tensor_tensor(ssq, hr, hr, ALU.mult)
                        continue
                    gp.tensor_tensor(hh2, hr, hr, ALU.mult)
                    pool.drain()
                    f = gp.tensor_tensor(ssq, ssq, hh2, ALU.add)
                    if r < 3:
                        pool.drain()
                f.then_inc(s_ssq, 1)

            def ssd(i, q):
                if i:
                    pool.wait_ge(s_mm, stage[i - 1, "gate"]["g0"])
                pool.dma_start(cst["cst"][:], t_in["state_ssd_conv"][q].rearrange("b k c -> (b k) c")).then_inc(s_cst, 16)
                pool.dma_start(hv_["wdt"][:], t_in["ssd_w_in"][q][:, 2048 + CONVD:].rearrange("(k p) n -> p k n", p=P)).then_inc(s_wdt, 16)
                pool.wait_ge(s_dtr, q + 1)
                x, e, t, z, z2, dt = spl["sp0"][:], spl["sp2"][:], spl["sp3"][:], spl["sp4"][:], spl["sp5"][:], hv_["dt"][:]
                gp.tensor_tensor(z, z, e, ALU.mult)
                gp.tensor_scalar(x, x, 0.0, None, ALU.max)
                pool.drain()
                gp.tensor_tensor(z2, z, z, ALU.mult)
                pool.drain()
                gp.tensor_scalar(t, z2, 1.0 / 17, 1.0 / 15, ALU.mult, ALU.add)
                for k in (13, 11, 9, 7, 5, 3, 1):
                    pool.drain()
                    gp.tensor_tensor(t, t, z2, ALU.mult)
                    pool.drain()
                    gp.tensor_scalar(t, t, 1.0 / k, None, ALU.add)
                pool.drain()
                gp.tensor_tensor(t, t, z, ALU.mult)
                pool.drain()
                gp.tensor_scalar(t, t, 2.0, None, ALU.mult)
                pool.drain()
                gp.tensor_tensor(dt, t, x, ALU.add).then_inc(s_dtd, 1)
                pool.wait_ge(s_dt7, q + 1)

                def group(g, b):
                    pool.wait_ge(s_xd, g + (GROUPS * q + 1))
                    if not (isinstance(g, int) and g < 2):
                        pool.wait_ge(s_back, g + (GROUPS * q - 1))
                    for c in range(2):
                        f = gp.tensor_tensor(grp[f"xde{b}"][:, c], grp[f"xd{b}"][:, c],
                                             hv2["tm"][:, 4 + c, ds(g * 4, 4)].unsqueeze(2).to_broadcast([P, 4, 64]), ALU.mult)
                    f.then_inc(s_xde, 1)
                    pool.wait_ge(s_exp, g + (GROUPS * q + 1))
                    seg = grp[f"seg{b}"][:, DH:4, :]
                    gp.tensor_tensor(seg, seg, grp[f"cbm{b}"][:].unsqueeze(1).to_broadcast([P, 4 - DH, 3 * P]), ALU.mult).then_inc(s_M2, 1)
                group(0, 0)
                group(1, 1)
                with gp.Fori(1, GROUPS // 2) as it:
                    group(it * 2, 0)
                    group(it * 2 + 1, 1)
                def selector(n, b):
                    if not (isinstance(n, int) and n < 2):
                        pool.wait_ge(s_bc, n + (NB * q - 1))
                    gp.tensor_copy(hv2[f"selS{b}"][:], ident[0:NB, ds(n, 1)].to_broadcast([NB, P])).then_inc(s_ssel, 1)
                selector(0, 0)
                selector(1, 1)

                def complete(n, b):
                    pool.wait_ge(s_ot, n + ((NB + 2) * q + 3))
                    pool.wait_ge(s_hd, n + (NB * q + 1))
                    st_ = stt[:, ds(n * -1 + (NB - 1), 1), :].rearrange("p o n -> p (o n)")
                    gp.tensor_tensor(st_, st_, otm[f"out{b}"][:].rearrange("p t n -> p (t n)"), ALU.add).then_inc(s_hn, 1)
                with gp.Fori(0, NB // 2 - 1) as it:
                    for b in range(2):
                        complete(it * 2 + b, b)
                        selector(it * 2 + (b + 2), b)
                for b in range(2):
                    complete(NB - 2 + b, b)
                gp.tensor_copy(grow.rearrange("p (g c) -> p g c", g=GROUPS),
                               ident[0:GROUPS, 0:GROUPS].unsqueeze(2).to_broadcast([GROUPS, GROUPS, P])).then_inc(s_grow, 1)

            def moba():
                pool.wait_ge(s_ev, stage[1, "qkv"]["c0"])
                pool.dma_start(ptab[:], t_in["page_table"].rearrange("b j -> (b j)").unsqueeze(0)).then_inc(s_tab, 16)
                pool.wait_ge(s_tab, 16)

                def page(pool_dram, n, j):
                    pid = pool.value_load(ptab[0:1, ds(n * PAGES + j, 1)], min_val=0, max_val=pool_dram.shape[1] - 1)
                    pool.dma_start(pg[f"pg{j}"][:], pool_dram[0][ds(pid, 1)].rearrange("o t h d -> t (o h) d")).then_inc(s_pg[j], 16)

                def selq(n):
                    gp.tensor_copy(ms["qsel"][:], ident[0:NB, ds(n, 1)].to_broadcast([NB, P])).then_inc(s_qsel, 1)
                for j in range(PAGES):
                    page(t_in["cache_k"], 0, j)
                pool.wait_ge(s_qk, 1)
                selq(0)
                with gp.Fori(1, NB) as it:
                    pool.wait_ge(s_qbc, it)
                    selq(it)
                    for j in range(PAGES):
                        pool.wait_ge(s_kd, it * 8 + (16 - 8 + j + 1))
                        pool.wait_ge(s_ka, it * 8 + (j - 7))
                        page(t_in["cache_k"], it, j)
                for j in range(PAGES):
                    pool.wait_ge(s_kd, 16 + 8 * (NB - 1) + j + 1)
                    pool.wait_ge(s_ka, 8 * (NB - 1) + j + 1)
                    page(t_in["cache_v"], 0, j)
                with gp.Fori(1, NB) as it:
                    for j in range(PAGES):
                        pool.wait_ge(s_vl, it * 8 + (j - 7))
                        page(t_in["cache_v"], it, j)

            def lru():
                pool.wait_ge(s_ev, stage[2, "lru_in"]["c0"])
                pool.dma_start(L["lcst"][:], t_in["state_lru_conv"][0].rearrange("b k c -> (b k) c")).then_inc(s_lld, 16)
                pool.dma_start(L["lst"][:], t_in["state_lru"][0]).then_inc(s_lld, 16)
                pool.dma_start(L["wax"][:, 0:8, :], t_in["lru_w_a"][0].rearrange("n c d -> c n d")).then_inc(s_lld, 16)
                pool.dma_start(L["wax"][:, 8:16, :], t_in["lru_w_x"][0].rearrange("n c d -> c n d")).then_inc(s_lld, 16)

            def mlp_ple(i):
                pool.wait_ge(s_stored, i + 1)
                pool.wait_ge(s_ev, stage[i, "up"]["c0"])
                pool.dma_start(ml["wp"][:], t_in["ple_w_proj"][i].rearrange("(k p) n -> p k n", p=P)).then_inc(s_ple, 16)
                pool.dma_start(ml["prow"][:], t_in["p_prompt"][i][0].rearrange("(c t) d -> t c d", c=2)).then_inc(s_ple, 16)
                pool.dma_start(ml["prow8"][:], t_in["p_sample"][i].rearrange("b s d -> (b s) d")).then_inc(s_ple, 16)
                c0 = stage[i, "up"]["c0"]

                def square(r, b):
                    pool.wait_ge(s_ev, r + (c0 + 1))
                    if not (isinstance(r, int) and r < 2 and i == 0):
                        pool.wait_ge(s_aL, r + (16 * i - 1))
                    gp.tensor_tensor(ml[f"ac{b}"][:], ml[f"rl{b}"][:], ml[f"rl{b}"][:], ALU.mult).then_inc(s_ac, 1)
                square(0, 0)
                square(1, 1)
                with gp.Fori(1, 8) as it:
                    square(it * 2, 0)
                    square(it * 2 + 1, 1)
                squares(3 * i + 2)
                squares(3 * i + 3)

            squares(0)
            for i in range(DEPTH):
                if i in SSD_LAYERS:
                    ssd(i, i // 3)
                elif i == 1:
                    moba()
                else:
                    lru()
                squares(3 * i + 1)
                mlp_ple(i)

        @block.vector
        def _(dve):
            V = nc.vector

            def split(st, it, u):
                g = it * unroll_of(st) + (u + st["g0"])
                if isinstance(g, int) and g + 2 >= total:
                    return
                dve.wait_ge(s_hi, g + 3)
                V.tensor_tensor(wlo[u % 2][:], raw[(u + 2) % 4][:], whi[u % 2][:].bitcast(F32), ALU.subtract).then_inc(s_lo, 1)

            def rms(n):
                dve.wait_ge(s_std, n + 1)
                V.reciprocal(rstd[:], rstd[:])
                dve.drain()
                if n % 3 == 1:
                    V.tensor_tensor(rstd[:], rstd[:], rstd[:], ALU.mult)
                    dve.drain()

            def evacs(st, evac, first=None, norm=None, extra=None, after=None):
                kq_n, U = st["kq"], unroll_of(st)

                def body(it):
                    for u in range(U):
                        g = it * U + (u + st["g0"])
                        r = it * (U // kq_n) + u // kq_n
                        p = (u // kq_n + st["c0"]) % 2
                        whole = u % kq_n == kq_n - 1
                        begin = norm is not None and is_first(it) and u == 0
                        if first and whole and not begin:
                            dve.wait_ge(s_mm, g + 1)
                            first(r, p)
                        split(st, it, u)
                        if begin:
                            rms(norm)
                            if extra:
                                extra()
                            if first:
                                dve.wait_ge(s_mm, g + 1)
                                first(r, p)
                        if whole:
                            if not first:
                                dve.wait_ge(s_mm, g + 1)
                            if evac:
                                evac(r, p)
                        if after:
                            after(it, u)
                sweep(V, st, body, peel=norm is not None)

            def gained(n, r):
                if n == 3 * DEPTH:
                    dve.drain().then_inc(s_xg, 1)
                    return
                dve.drain()
                col = gain_col(n)
                for t in range(2):
                    tile = r * 2 + t
                    f = V.tensor_scalar(xg[:, ds(tile, 1), :].rearrange("p o t -> p (o t)"), h[:, ds(tile, 1), :].rearrange("p o t -> p (o t)"),
                                        colA[:, ds(tile + col, 1)], None, ALU.mult)
                f.then_inc(s_xg, 1)

            def low(n, r):
                if n == 3 * DEPTH:
                    return
                hi_, lo = split_input(n)
                dve.wait_ge(s_xh, r + (4 * n + 1))
                V.tensor_tensor(lo[:, ds(r * 2, 2), :], xg[:, ds(r * 2, 2), :], hi_[:, ds(r * 2, 2), :].bitcast(F32), ALU.subtract).then_inc(s_xl, 1)

            def evacs_out(st, add, n):
                kq_n, U = st["kq"], unroll_of(st)

                def body(it):
                    for u in range(U):
                        g = it * U + (u + st["g0"])
                        r = it * (U // kq_n) + u // kq_n
                        whole = u % kq_n == kq_n - 1
                        if whole:
                            dve.wait_ge(s_mm, g + 1)
                            add(r, (u // kq_n + st["c0"]) % 2)
                            gained(n, r)
                        if u == U - 1:
                            low(n, r)
                        split(st, it, u)
                        if whole and u < U - 1:
                            low(n, r)
                sweep(V, st, body)

            def bc(ap, n):
                return ap.unsqueeze(1).to_broadcast([ap.shape[0], n, ap.shape[1]])

            def softplus(x, e, t, z, z2, out):
                V.tensor_scalar(t, e, 2.0, None, ALU.add)
                dve.drain()
                V.reciprocal(z, t)
                dve.drain()
                V.tensor_tensor(z, z, e, ALU.mult)
                dve.drain()
                V.tensor_tensor(z2, z, z, ALU.mult)
                V.tensor_scalar(x, x, 0.0, None, ALU.max)
                dve.drain()
                V.tensor_scalar(t, z2, 1.0 / 17, None, ALU.mult)
                for k in (15, 13, 11, 9, 7, 5, 3):
                    dve.drain()
                    V.scalar_tensor_tensor(t, t, 1.0 / k, z2, ALU.add, ALU.mult)
                dve.drain()
                V.scalar_tensor_tensor(t, t, 1.0, z, ALU.add, ALU.mult)
                dve.drain()
                V.scalar_tensor_tensor(out, t, 2.0, x, ALU.mult, ALU.add)
                dve.drain()

            dve.wait_ge(s_const, 1)
            V.tensor_reduce(pairsel[:], ident[0:HEADS, 0:HEADS].rearrange("h (i e) -> h i e", e=2), AX, ALU.add)
            eo = ident[0:HEADS, 0:HEADS].rearrange("h (i e) -> h e i", e=2)
            V.tensor_reduce(eo2, eo, AX, ALU.add)
            dve.drain()
            V.tensor_copy(evenodd[:].rearrange("h (e p) -> h e p", e=2), eo2.unsqueeze(2).to_broadcast([HEADS, 2, 64]))
            for u in range(2):
                dve.wait_ge(s_hi, u + 1)
                V.tensor_tensor(wlo[u][:], raw[u][:], whi[u][:].bitcast(F32), ALU.subtract).then_inc(s_lo, 1)
            dve.wait_ge(s_tp0, 1)
            for c in range(2):
                V.tensor_copy(h[:, :, c * P:(c + 1) * P], G[c][:].rearrange("p a (k t) -> p (a k) t", t=P))
            V.tensor_copy(h[:, :, SEQ:T], bank[0][:, 0:KT * NB].rearrange("p (k b) -> p k b", b=NB))
            V.tensor_copy(colA[:], bank[1][:, 0:104])
            V.tensor_copy(colB[:], bank[1][:, 128:224])
            V.tensor_scalar(colC[:], bank[2][:, 0:256].rearrange("p (q c) -> p q c", q=2), 0.5, None, ALU.mult)
            V.tensor_scalar(colE[:], bank[2][:, 256:320], 0.5, None, ALU.mult).then_inc(s_init, 1)
            for r in range(4):
                gained(0, r)
            for r in range(4):
                low(0, r)

            def add_h(r, p):
                hr = h[:, ds(r * 2, 2), :]
                V.tensor_tensor(hr, hr, G[p][:, :, 0:T], ALU.add).then_inc(s_ev, 1)

            def ssd(i, q):
                xbc, zs, seq, smpl = Z["xbc"], Z["zs"], slice(0, SEQ), slice(SEQ, T)
                for b in range(2):
                    V.memset(S[f"T{b}"][:, :, 0:3], 0.0)

                def sample_conv():
                    dve.wait_ge(s_cT, q + 1)
                    stT, cp = cstT["stT"], cprod["cprod"]
                    for a in range(2):
                        V.tensor_copy(stT[:, 16 * a:16 * a + 16, :], bank[2 + a][:, 0:384].rearrange("p (t s) -> p t s", s=24))
                    dve.drain()
                    for k in range(3):
                        V.tensor_tensor(cp[:, :, :, k], stT[:].rearrange("p t (b k) -> p t b k", k=3)[:, :, :, k],
                                        colC[:, q, k * CT:(k + 1) * CT].unsqueeze(2).to_broadcast([P, CT, NB]), ALU.mult)
                    dve.drain()
                    V.tensor_reduce(S["spre"][:], cp[:], AX, ALU.add)
                    dve.drain()
                    V.tensor_tensor(S["spre"][:], S["spre"][:], colE[:, q * CT:(q + 1) * CT].unsqueeze(2).to_broadcast([P, CT, NB]), ALU.add)
                    dve.drain()

                def raw_out(r, p):
                    if not (isinstance(r, int) and r < 2 and q == 0):
                        dve.wait_ge(s_tap, r + (16 * q - 1))
                        dve.wait_ge(s_last, r + (16 * q - 1))
                    V.tensor_tensor(S[f"T{p}"][:, :, 3:3 + T], G[p][:, :, 0:T], bc(rstd[:], 2), ALU.mult).then_inc(s_ev, 1)

                def taps(r, p):
                    dve.wait_ge(s_tap, r + (16 * q + 1))
                    T_ = S[f"T{p}"]
                    for k in range(1, CW):
                        for t in range(2):
                            tile = r * 2 + t
                            o = xbc[:, ds(tile, 1), seq].rearrange("p o t -> p (o t)")
                            f = V.scalar_tensor_tensor(o, T_[:, t, k:k + SEQ], colC[:, q, ds(tile + k * CT, 1)], o, ALU.mult, ALU.add)
                        if k < CW - 1:
                            dve.drain()
                        else:
                            f.then_inc(s_conv, 1)

                def dt_head(it, u):
                    if is_first(it) and u == 1:
                        dve.wait_ge(s_dtp, q + 1)
                        V.tensor_tensor(sp[0], bank[1][0:HEADS, 0:T], rstd[0:HEADS, :], ALU.mult)
                        dve.drain()
                        V.tensor_scalar(sp[0], sp[0], hsm[:, q:q + 1], None, ALU.add)
                        dve.drain()
                        V.scalar_tensor_tensor(sp[1], sp[0], -1.0, sp[0], ALU.mult, ALU.min).then_inc(s_dt1, 1)
                    if is_first(it) and u == 2:
                        dve.wait_ge(s_dt2, q + 1)
                        V.tensor_scalar(sp[3], sp[2], 2.0, None, ALU.add)
                        dve.drain()
                        V.reciprocal(sp[4], sp[3]).then_inc(s_dtr, 1)
                sp = [spl[f"sp{k}"][:] for k in range(6)]
                evacs(stage[i, "xbc"], taps, raw_out, norm=3 * i, extra=sample_conv, after=dt_head)
                dve.wait_ge(s_last, 16 * (q + 1))
                V.tensor_tensor(xbc[:, :, smpl], S["rawlast"][:, :, 3:LAST],
                                colC[:, q, 3 * CT:4 * CT].unsqueeze(2).to_broadcast([P, CT, NB]), ALU.mult)
                dve.drain()
                V.tensor_tensor(xbc[:, :, smpl], xbc[:, :, smpl], S["spre"][:], ALU.add).then_inc(s_conv, 1)
                dt, dA, acum, vals = hv_["dt"], hv_["dA"], hv2["acum"], hv2["vals"]
                dve.wait_ge(s_dtd, q + 1)
                V.tensor_scalar(dA[:], dt[:], hv2["bvec"][:, 0:1], -1.0, ALU.mult, ALU.mult)
                dve.drain()
                V.tensor_tensor_scan(acum[:], ones[0:HEADS, 0:1].to_broadcast([HEADS, SEQ]), dA[:, seq], 0.0, ALU.mult, ALU.add).then_inc(s_dt3, 1)
                V.tensor_copy(vals[:, 0:8], dt[:, smpl])
                V.tensor_copy(vals[:, 16:17], hsm[:, 4 + q:5 + q])
                dve.wait_ge(s_dt4, q + 1)
                dve.drain()
                V.tensor_tensor(hv_["R"][:], vals[:].unsqueeze(1).to_broadcast([HEADS, XT, 17]),
                                pairsel[:].unsqueeze(2).to_broadcast([HEADS, XT, 17]), ALU.mult).then_inc(s_dt5, 1)

                def z_out(r, p):
                    V.tensor_tensor(zs[:, ds(r * 2, 2), :], G[p][:, :, 0:T], bc(rstd[:], 2), ALU.mult).then_inc(s_ev, 1)

                def silus(r, p):
                    b = r % 2
                    dve.wait_ge(s_zth, 8 * q + r + 1)
                    V.scalar_tensor_tensor(zs[:, 2 * r:2 * r + 2, :], S[f"T{b}"][:, :, 0:T], 1.0, zs[:, 2 * r:2 * r + 2, :], ALU.add, ALU.mult)
                    dve.wait_ge(s_xth, 8 * q + r + 1)
                    V.scalar_tensor_tensor(xbc[:, 4 * r:4 * r + 4, :], xth[f"xth{b}"][:], 1.0, xbc[:, 4 * r:4 * r + 4, :], ALU.add, ALU.mult).then_inc(s_silu, 1)
                z = stage[i, "z"]
                for r in range(8):
                    dve.wait_ge(s_mm, z["g0"] + r + 1)
                    z_out(r, (r + z["c0"]) % 2)
                    if r < 7:
                        split(z, r // 4, r % 4)
                    silus(r, r % 2)
                dve.drain().then_inc(s_th, 1)
                dve.wait_ge(s_dt6, q + 1)
                tm, hv = hv2["tm"], hv2["hv"]
                V.tensor_copy(tm[:], bank[2][:, 0:6 * HEADS].rearrange("p (j h) -> p j h", h=HEADS))
                V.tensor_copy(hv[:], bank[3][:, 0:XT * 17].rearrange("p (i v) -> p i v", v=17)).then_inc(s_dt7, 1)
                split(z, 1, 3)
                dve.drain()
                def front(g, b):
                    dve.wait_ge(s_tp, g + (GROUPS * q + 1))
                    if not (isinstance(g, int) and g < 2):
                        dve.wait_ge(s_back, g + (GROUPS * q - 1))
                    xd, btm, cbm, seg = (grp[f"{n}{b}"] for n in ("xd", "btm", "cbm", "seg"))
                    for c in range(2):
                        V.tensor_tensor(xd[:, c], bank[0][:, c * SEQ:(c + 1) * SEQ].rearrange("s (r p) -> s r p", p=64),
                                        tm[:, c, ds(g * 4, 4)].unsqueeze(2).to_broadcast([P, 4, 64]), ALU.mult)
                    if not (isinstance(g, int) and g < 2):
                        dve.wait_ge(s_xde, g + (GROUPS * q - 1))
                    V.tensor_copy(btm[:], bank[1][:, 0:SEQ].rearrange("s (c n) -> s c n", c=2))
                    V.tensor_tensor(cbm[:], bank[2][:, 0:3 * P], tri[:], ALU.mult).then_inc(s_xd, 1)
                    dve.wait_ge(s_ar, g + (GROUPS * q + 1))
                    for r in range(4):
                        at_ = G[0][:, r // 2, (r % 2) * SEQ:(r % 2 + 1) * SEQ]
                        V.tensor_scalar(seg[:, r, 0:SEQ], at_, tm[:, 2, ds(g * 4 + r, 1)], 0.0, ALU.subtract, ALU.min)
                        f = V.tensor_scalar(seg[:, r, SEQ:3 * P], at_[:, P:SEQ], tm[:, 3, ds(g * 4 + r, 1)], 0.0, ALU.subtract, ALU.min)
                    f.then_inc(s_seg, 1)

                def mid(g, b):
                    dve.wait_ge(s_exp, g + (GROUPS * q + 1))
                    seg = grp[f"seg{b}"][:, 0:DH, :]
                    V.tensor_tensor(seg, seg, bc(grp[f"cbm{b}"][:], DH), ALU.mult).then_inc(s_M, 1)

                def back(g, b):
                    dve.wait_ge(s_back, g + (GROUPS * q + 1))
                    y = S[f"T{b}"]
                    for t in range(2):
                        V.scalar_tensor_tensor(y[:, t, seq], xbc[:, ds(g * 2 + t, 1), seq].rearrange("p o t -> p (o t)"),
                                               hv[:, ds(g * 2 + t, 1), 16:17].rearrange("p o v -> p (o v)"), G[1][:, t, seq], ALU.mult, ALU.add)
                    dve.drain()
                    if not (isinstance(g, int) and g < 2):
                        dve.wait_ge(s_sto[b], g * 8 + (8 * GROUPS * q - 8 * b))
                    zz = zs[:, ds(g * 2, 2), seq]
                    V.scalar_tensor_tensor(zz, y[:, :, seq], 0.5, zz, ALU.mult, ALU.mult)
                    V.tensor_copy(grp[f"stout{b}"][:], G[1][:, :, SEQ:3 * P]).then_inc(s_yev, 1)
                skewed(V, GROUPS, front, back, mid)
                for b in range(2):
                    dve.wait_ge(s_sto[b], 8 * GROUPS * (q + 1))
                dve.wait_ge(s_brT, q + 1)
                for a in range(2):
                    dve.wait_ge(s_brH, 2 * q + a + 1)
                    f = V.tensor_tensor(bcr["bcL"][:, a * D:(a + 1) * D], A[a][0:NB].rearrange("b a n -> b (a n)"),
                                        bcr["bcH"][:, a * D:(a + 1) * D].bitcast(F32), ALU.subtract)
                f.then_inc(s_brE, 1)
                xdts, ys, dx, xs = hv2["xdts"], hv2["ys"], hv3["dx"], xbc[:, 0:XT, smpl]
                V.tensor_tensor(xdts[:], xs, hv[:, :, 0:8], ALU.mult)
                V.tensor_tensor(dx[:], xs, hv[:, :, 16:17].to_broadcast([P, XT, NB]), ALU.mult)
                dve.drain().then_inc(s_bcf, 2)
                dve.nop().then_inc(s_ot, 2)

                def outer(n):
                    bb = (A[0], G[0])[n % 2]
                    dve.wait_ge(s_bb, n + NB * q + 1)
                    V.tensor_tensor(otm[f"out{n % 2}"][:].rearrange("p (g e) n -> p g e n", e=2),
                                    bb[:].rearrange("p a (g n) -> p (a g) n", n=P).unsqueeze(2).to_broadcast([P, GROUPS, 2, P]),
                                    xdts[:, :, n].rearrange("p (g e) -> p g e", e=2).unsqueeze(3).to_broadcast([P, GROUPS, 2, P]),
                                    ALU.mult).then_inc(s_ot, 1)

                def contract(n):
                    cc, ysb = (A[1], G[1])[n % 2], hv2[f"ysb{n % 2}"]
                    dve.wait_ge(s_bc, n + NB * q + 1)
                    dve.wait_ge(s_hn, n + NB * q + 1)
                    for t in range(XT):
                        w = slice((t // 2 % 4) * P, (t // 2 % 4) * P + P)
                        f = V.tensor_tensor_reduce(otm[f"out{n % 2}"][:, t, :], stx[n][:, t, :], cc[:, t // 8, w], 1.0, 0.0,
                                                   ALU.mult, ALU.add, ysb[:, t:t + 1])
                    f.then_inc(s_bcf, 1)
                    dve.drain()
                    V.tensor_copy(ys[:, :, n], ysb[:])
                outer(0)
                for n in range(NB):
                    if n + 1 < NB:
                        outer(n + 1)
                    contract(n)
                dve.drain()
                V.tensor_tensor(xdts[:], dx[:], ys[:], ALU.add)
                dve.drain()
                V.scalar_tensor_tensor(zs[:, :, smpl], xdts[:], 0.5, zs[:, :, smpl], ALU.mult, ALU.mult)
                dve.drain().then_inc(s_yz, 1)
                for g in range(GROUPS):
                    dve.wait_ge(s_ysq, GROUPS * q + g + 1)
                    V.tensor_tensor(ysq["ysq"][:, 2 * g, :], ysq["ysq"][:, 2 * g, :], ysq["ysq"][:, 2 * g + 1, :], ALU.add).then_inc(s_yss, 1)
                dve.wait_ge(s_gr, q + 1)
                V.reciprocal(gnb["grs"][:], gnb["grs"][:]).then_inc(s_gs, 1)

                def yn_low(g):
                    dve.wait_ge(s_yh, g + (GROUPS * q + 1))
                    V.tensor_tensor(ysp["yL"][:, 2 * g:2 * g + 2, :], zs[:, 2 * g:2 * g + 2, :], ysp["yH"][:, 2 * g:2 * g + 2, :].bitcast(F32), ALU.subtract).then_inc(s_mixl, 1)
                for g in range(GROUPS):
                    dve.wait_ge(s_gb, GROUPS * q + g + 1)
                    for t in range(2):
                        c = 64 + XT * q + 2 * g + t
                        f = V.scalar_tensor_tensor(zs[:, 2 * g + t, :], zs[:, 2 * g + t, :], colB[:, c:c + 1],
                                                   bank[g % 4][:, 0:T], ALU.mult, ALU.mult)
                    f.then_inc(s_yn, 1)
                    if g:
                        yn_low(g - 1)
                yn_low(GROUPS - 1)
                evacs_out(stage[i, "ssd_out"], add_h, 3 * i + 1)

            def moba():
                qkv, att = M["qkv"], M["att"]

                def qkv_out(r, p):
                    V.tensor_tensor(qkv[:, ds(r * 2, 2), :], G[p][:, :, 0:T], bc(rstd[:], 2), ALU.mult).then_inc(s_ev, 1)
                evacs(stage[1, "qkv"], None, qkv_out, norm=3)

                def front(hh, b):
                    dve.wait_ge(s_mtp, hh + 1)
                    if not (isinstance(hh, int) and hh < 2):
                        dve.wait_ge(s_mo, hh - 1)
                        dve.wait_ge(s_kst[b], hh * 16 - 16 * b)
                    sc, mx, nm = mh[f"sc{b}"], mh[f"mx{b}"], mh[f"nm{b}"]
                    b0, b1, b2 = head_banks[b]
                    V.tensor_copy(mh[f"kvt{b}"][:], b0.rearrange("p (j d) -> p j d", j=4))
                    V.tensor_copy(M["rowS"][:, :, ds(hh * P, P)], b1[0:NB, 0:3 * P].rearrange("p (j d) -> p j d", j=3))
                    V.tensor_tensor(sc[:], b2[:, 0:3 * P], amask[:], ALU.add)
                    dve.drain()
                    V.tensor_reduce(mx[:, 0:1], sc[:, 0:P], AX, ALU.max)
                    V.tensor_reduce(mx[:, 1:2], sc[:, P:3 * P], AX, ALU.max)
                    dve.drain()
                    V.tensor_scalar(nm[:], mx[:], -SCALE, None, ALU.mult).then_inc(s_msc, 1)

                def mid(hh, b):
                    dve.wait_ge(s_mex, hh + 1)
                    sc, rs, ri = mh[f"sc{b}"], mh[f"rs{b}"], mh[f"ri{b}"]
                    V.reciprocal(ri[:], rs[:])
                    dve.drain()
                    V.tensor_scalar(sc[:, 0:P], sc[:, 0:P], ri[:, 0:1], None, ALU.mult)
                    V.tensor_scalar(sc[:, P:3 * P], sc[:, P:3 * P], ri[:, 1:2], None, ALU.mult).then_inc(s_mP, 1)

                def back(hh, b):
                    dve.wait_ge(s_mo, hh + 1)
                    V.tensor_copy(att[:, ds(hh, 1), 0:SEQ].rearrange("p o t -> p (o t)"), bank[4][:, 0:SEQ]).then_inc(s_moe, 1)
                def turn(hh, b):
                    front(hh, b)
                    mid(hh, b)
                    back(hh - 1, 1 - b)
                front(0, 0)
                mid(0, 0)
                turn(1, 1)
                with V.Fori(1, MH // 2) as it:
                    turn(it * 2, 0)
                    turn(it * 2 + 1, 1)
                back(MH - 1, 1)
                for b in range(2):
                    dve.wait_ge(s_kst[b], 16 * MH)
                S_ = slice(SEQ, T)
                V.tensor_tensor(ms["qk"][:], qkv[:, 0:8, S_].rearrange("p h b -> p b h"), qkv[:, 8:16, S_].rearrange("p h b -> p b h"), ALU.mult).then_inc(s_qk, 1)
                dve.nop().then_inc(s_kd, 16)
                dve.drain().then_inc(s_att, 1)
                with V.Fori(0, NB // 2) as it:
                    for b in range(2):
                        n = it * 2 + b
                        dve.wait_ge(s_qbc, n + 1)
                        for j in range(PAGES):
                            dve.wait_ge(s_pg[j], n * 16 + 16)
                            V.tensor_tensor(pg[f"pg{j}"][:, 0:4, :], pg[f"pg{j}"][:, 0:4, :],
                                            A[b][:, 0, :].rearrange("p (h d) -> p h d", h=4), ALU.mult).then_inc(s_km, 1)
                            for hh in range(4, MH):
                                f = V.tensor_tensor_reduce(pg[f"pg{j}"][:, hh, :], pg[f"pg{j}"][:, hh, :], A[b][:, hh // 4, (hh % 4) * P:(hh % 4 + 1) * P],
                                                           1.0, 0.0, ALU.mult, ALU.add, ms[f"sq{b}"][:, j, hh:hh + 1])
                            f.then_inc(s_kd, 1)
                        dve.drain()
                        dve.wait_ge(s_ka, n * PAGES + PAGES)
                        V.tensor_copy(ms["sS"][:, :, ds(n * 8, 8)], ms[f"sq{b}"][:])
                dve.drain().then_inc(s_kd, 1)
                sR, gs, geq, gsc = ms["sR"], ms["gsum"], ms["geq"], ms["gsc"]
                dve.wait_ge(s_sT, 1)
                V.tensor_copy(sR[:, 0:1024], A[0][0:64].rearrange("p a n -> p (a n)"))
                V.tensor_copy(sR[:, 1024:1025], bank[4][0:64, 0:1])
                dve.drain()
                blocks = sR[:, 0:1024].rearrange("p (n k) -> p n k", n=BLOCKS)
                V.tensor_reduce(gs[:], blocks, AX, ALU.add)
                dve.drain()
                V.tensor_reduce(gsc[:, 0:1], gs[:], AX, ALU.min)
                dve.drain()
                V.scalar_tensor_tensor(geq[:], gs[:], gsc[:, 0:1], blockno[:], ALU.is_equal, ALU.mult)
                dve.drain()
                V.tensor_reduce(gsc[:, 1:2], geq[:], AX, ALU.max)
                dve.drain()
                V.tensor_scalar(geq[:], geq[:], gsc[:, 1:2], -BIG, ALU.is_equal, ALU.mult)
                dve.drain()
                V.tensor_tensor(blocks, blocks, geq[:].unsqueeze(2).to_broadcast([64, BLOCKS, 256]), ALU.add)
                dve.drain()
                V.tensor_reduce(gsc[:, 4:5], sR[:, 0:1025], AX, ALU.max)
                dve.drain()
                V.tensor_scalar(gsc[:, 2:3], gsc[:, 4:5], -SCALE, None, ALU.mult).then_inc(s_sR, 1)
                dve.wait_ge(s_sE, 1)
                V.reciprocal(gsc[:, 5:6], gsc[:, 3:4])
                dve.drain()
                V.tensor_scalar(sR[:, 0:1025], sR[:, 0:1025], gsc[:, 5:6], None, ALU.mult)
                dve.drain()
                V.tensor_scalar(ms["dg"][:], ident[0:64, 0:64], sR[:, 1024:1025], None, ALU.mult).then_inc(s_sP, 1)
                dve.wait_ge(s_sPT, 1)
                V.tensor_copy(ms["pT8"][:], bank[2].rearrange("p (j c) -> p j c", j=PAGES))
                V.tensor_copy(ms["bco"][:], bank[5][:, 0:64])
                dve.drain()
                V.tensor_copy(ms["pH8"][:], ms["pT8"][:])
                dve.drain()
                V.tensor_tensor(ms["pL8"][:], ms["pT8"][:], ms["pH8"][:].bitcast(F32), ALU.subtract)
                ov = ms["ov"][:].rearrange("p (b h) -> p b h", h=MH)
                V.tensor_tensor(ov, qkv[:, 16:24, S_].rearrange("p h b -> p b h"), ms["bco"][:].rearrange("p (b h) -> p b h", h=MH), ALU.mult)
                dve.drain()

                def pick(n, b):
                    for a, part in enumerate(("pH8", "pL8")):
                        V.tensor_scalar(pn[:, b, a], ms["pT8"][:], 0.0, None, ALU.mult)
                    dve.drain()
                    for a, part in enumerate(("pH8", "pL8")):
                        f = V.tensor_copy(pn[:, b, a, :, ds(n * MH, MH)], ms[part][:, :, ds(n * MH, MH)].bitcast(F32))
                    f.then_inc(s_ptn, 1)

                def values(n, b, following=True):
                    for j in range(PAGES):
                        if j == 2 and following:
                            if not (isinstance(n, int) and n == 0):
                                dve.wait_ge(s_vd, n * PAGES)
                            pick(n + 1, 1 - b)
                        dve.wait_ge(s_vh, n * PAGES + (j + 1))
                        V.tensor_tensor(vL[j % 4][:], pg[f"pg{j}"][:].rearrange("p (c h) d -> p c (h d)", c=2),
                                        vH[j % 4][:].bitcast(F32), ALU.subtract).then_inc(s_vl, 1)
                pick(0, 0)
                values(0, 0)
                with V.Fori(0, NB // 2 - 1) as it:
                    values(it * 2 + 1, 1)
                    values(it * 2 + 2, 0)
                values(NB - 1, 1, following=False)
                dve.wait_ge(s_mixh, 1)
                V.tensor_tensor(ao["oL"][:, :, 0:SEQ], att[:, :, 0:SEQ], ao["oH"][:, :, 0:SEQ].bitcast(F32), ALU.subtract)
                dve.wait_ge(s_vd, NB * PAGES)
                V.tensor_copy(sR[:, 512:1024], G[1][0:64, 1, :]).then_inc(s_vo, 1)
                dve.wait_ge(s_vt, 1)
                for hh in range(MH):
                    sums = bank[2][:, hh * 64:(hh + 1) * 64].rearrange("p (b h) -> p h b", h=MH)
                    V.tensor_tensor(att[:, hh, S_], sums[:, hh, :], ov[:, :, hh], ALU.add)
                dve.drain().then_inc(s_att, 1)
                dve.wait_ge(s_mixh, 2)
                V.tensor_tensor(ao["oL"][:, :, S_], att[:, :, S_], ao["oH"][:, :, S_].bitcast(F32), ALU.subtract).then_inc(s_mixl, 1)
                evacs_out(stage[1, "wo"], add_h, 4)

            def lru():
                st = stage[2, "lru_in"]
                XR, xc, la, Gt, ga = L["XR"], L["xc"], L["la"], L["Gt"], L["a2"]

                def gelu_in(u):
                    pair = slice(2 * u, 2 * u + 2)
                    V.tensor_tensor(ga[:, pair], Gt[:, pair], Gt[:, pair], ALU.mult)
                    dve.drain()
                    V.tensor_scalar(ga[:, pair], ga[:, pair], GELU_B, 1.0, ALU.mult, ALU.add)
                    dve.drain()
                    V.tensor_tensor(ga[:, pair], ga[:, pair], Gt[:, pair], ALU.mult).then_inc(s_lgl, 1)

                def gelu_out(u):
                    pair = slice(2 * u, 2 * u + 2)
                    dve.wait_ge(s_lgt, u + 1)
                    V.scalar_tensor_tensor(Gt[:, pair], ga[:, pair], 1.0, Gt[:, pair], ALU.add, ALU.mult)

                def sample_conv():
                    dve.wait_ge(s_lT, 1)
                    V.tensor_copy(L["lstT"][:], bank[2][:, 0:192].rearrange("p (k s) -> p k s", s=24))
                    V.tensor_copy(L["lh0"][:], bank[2][:, 192:256].rearrange("p (k b) -> p k b", b=8)).then_inc(s_lTe, 1)
                    dve.drain()
                    for k in range(3):
                        V.tensor_tensor(L["lpr"][:, :, :, k], L["lstT"][:].rearrange("p t (b k) -> p t b k", k=3)[:, :, :, k],
                                        colB[:, k * KT:(k + 1) * KT].unsqueeze(2).to_broadcast([P, KT, NB]), ALU.mult)
                    dve.drain()
                    V.tensor_reduce(L["lspre"][:], L["lpr"][:], AX, ALU.add)
                    dve.drain()
                    V.tensor_tensor(L["lspre"][:], L["lspre"][:], colB[:, 32:40].unsqueeze(2).to_broadcast([P, KT, NB]), ALU.add)
                    dve.drain()
                for u in range(4):
                    split(st, 0, u)
                    if u == 0:
                        rms(6)
                        V.memset(L["XR"][:, :, 0:3], 0.0)
                    dve.wait_ge(s_mm, st["g0"] + u + 1)
                    V.tensor_tensor(Gt[:, 2 * u:2 * u + 2, :], G[(u + st["c0"]) % 2][:, :, 0:T], bc(rstd[:], 2), ALU.mult).then_inc(s_ev, 1)
                    dve.drain()
                    gelu_in(u)
                    if u:
                        gelu_out(u - 1)
                halves = (slice(0, 4), slice(4, 8))
                thr, thi, hs = L["thr"], L["thi"], L["hs"]

                def log_a(n):
                    for k in range(4 * n, 4 * n + 4):
                        dve.wait_ge(s_lth, k + 1)
                        f = V.tensor_scalar(la[:, k, :], thr[:, k, :], 1.0, lsp["ch"][:, k:k + 1], ALU.add, ALU.mult)
                    f.then_inc(s_lla, 1)
                    V.scalar_tensor_tensor(thi[:, halves[n]], thi[:, halves[n]], 1.0, xc[:, halves[n]], ALU.add, ALU.mult)
                for u in range(4):
                    dve.wait_ge(s_mm, st["g0"] + 4 + u + 1)
                    V.tensor_tensor(XR[:, 2 * u:2 * u + 2, 3:3 + T], G[(u + st["c0"]) % 2][:, :, 0:T], bc(rstd[:], 2), ALU.mult).then_inc(s_ev, 1)
                    if u < 3:
                        split(st, 1, u)
                    if u == 0:
                        gelu_out(3)
                        sample_conv()
                    if u == 3:
                        log_a(0)
                    dve.wait_ge(s_lt0, 2 * u + 2)
                    for w in range(1, CW):
                        for k in (2 * u, 2 * u + 1):
                            V.scalar_tensor_tensor(xc[:, k, 0:SEQ], XR[:, k, w:w + SEQ], colB[:, w * KT + k:w * KT + k + 1], xc[:, k, 0:SEQ], ALU.mult, ALU.add)
                        dve.drain()
                    for k in (2 * u, 2 * u + 1):
                        V.scalar_tensor_tensor(xc[:, k, SEQ:T], XR[:, k, 3 + SEQ:3 + T], colB[:, 3 * KT + k:3 * KT + k + 1], L["lspre"][:, k, :],
                                               ALU.mult, ALU.add).then_inc(s_lc, 1)
                dve.drain()
                log_a(1)
                for n, s4 in enumerate(halves):
                    dve.wait_ge(s_la, n + 1)
                    V.scalar_tensor_tensor(thr[:, s4], L["a2"][:, s4], 1.0, thr[:, s4], ALU.add, ALU.mult).then_inc(s_lv, 1)
                dve.drain()

                def low_half(n):
                    dve.wait_ge(s_mixh, 2 + n + 1)
                    V.tensor_tensor(lo2["oL"][:, halves[n]], xc[:, halves[n]], lo_["oH"][:, halves[n]].bitcast(F32), ALU.subtract)
                for n, s4 in enumerate(halves):
                    dve.wait_ge(s_lsq, n + 1)
                    V.scalar_tensor_tensor(thi[:, s4], thi[:, s4], 0.5, thr[:, s4], ALU.mult, ALU.mult)
                    dve.wait_ge(s_lb, n + 1)
                    V.tensor_tensor(L["lh0"][:, s4], L["lh0"][:, s4], la[:, s4, SEQ:T], ALU.mult)
                    dve.drain()
                    for k in range(4 * n, 4 * n + 4):
                        V.tensor_tensor_scan(hs[:, k, 0:SEQ], la[:, k, 0:SEQ], thi[:, k, 0:SEQ], 0.0, ALU.mult, ALU.add)
                    V.tensor_tensor(hs[:, s4, SEQ:T], L["lh0"][:, s4], thi[:, s4, SEQ:T], ALU.add)
                    dve.drain()
                    V.scalar_tensor_tensor(xc[:, s4], Gt[:, s4], 0.5, hs[:, s4], ALU.mult, ALU.mult).then_inc(s_ly, 1)
                low_half(0)
                low_half(1)
                dve.drain().then_inc(s_mixl, 1)
                split(st, 1, 3)
                evacs_out(stage[2, "lru_out"], add_h, 7)

            def decay():
                lp = [lsp[f"lp{k}"] for k in range(6)]
                lam = colB[:, 40:48]
                V.tensor_scalar(lp[0], lam, -1.0, None, ALU.mult)
                dve.drain()
                V.tensor_tensor(lp[1], lp[0], lam, ALU.min).then_inc(s_lsp, 1)
                dve.wait_ge(s_lse, 1)
                softplus(lp[0], lp[2], lp[3], lp[4], lp[5], lsp["ch"][:])
                V.tensor_scalar(lsp["ch"][:], lsp["ch"][:], -4.0, None, ALU.mult)
                V.tensor_scalar(lsp["bah"][:], colB[:, 48:56], 0.5, None, ALU.mult)
                V.tensor_scalar(lsp["bxh"][:], colB[:, 56:64], 0.5, None, ALU.mult)

            def mlp_ple(i):

                def low_act(r, b):
                    dve.wait_ge(s_ac, r + (16 * i + 1))
                    dve.wait_ge(s_aH, r + (16 * i + 1))
                    V.tensor_tensor(aL[:, ds(r * 2, 2), :], ml[f"ac{b}"][:], aH[:, ds(r * 2, 2), :].bitcast(F32), ALU.subtract).then_inc(s_aL, 1)
                evacs(stage[i, "up"], low_act, norm=3 * i + 1)
                if i == 1:
                    decay()
                dve.wait_ge(s_pT, i + 1)
                V.tensor_copy(ml["pT"][:], A[0][:, :, 0:T]).then_inc(s_pTe, 1)

                def down(r, p):
                    V.tensor_tensor(ml["t1"][:], G[p][:, :, 0:T], bc(rstd[:], 2), ALU.mult).then_inc(s_ev, 1)
                    dve.drain()
                    hr = h[:, ds(r * 2, 2), :]
                    V.tensor_tensor(hr, hr, ml["t1"][:], ALU.add)
                evacs_out(stage[i, "down"], down, 3 * i + 2)
                st = stage[i, "gate"]
                t1 = ml["t1"]
                for r in range(4):
                    if r == 0:
                        split(st, 0, r)
                        rms(3 * i + 2)
                    dve.wait_ge(s_mm, st["g0"] + r + 1)
                    V.tensor_tensor(t1[:], G[(r + st["c0"]) % 2][:, :, 0:T], bc(rstd[:], 2), ALU.mult).then_inc(s_ev, 1)
                    dve.wait_ge(s_tg, 4 * i + r + 1)
                    dve.wait_ge(s_pj, 4 * i + r + 1)
                    V.scalar_tensor_tensor(t1[:], t1[:], 1.0, A[(r + 1) % 2][:, :, 0:T], ALU.add, ALU.mult).then_inc(s_pje, 1)
                    dve.drain()
                    hr = h[:, 2 * r:2 * r + 2, :]
                    V.scalar_tensor_tensor(hr, t1[:], 0.5, hr, ALU.mult, ALU.add)
                    gained(3 * i + 3, r)
                    if r in (1, 2):
                        split(st, 0, r)
                    low(3 * i + 3, r)
                    if r == 3:
                        split(st, 0, r)

            for i in range(DEPTH):
                if i in SSD_LAYERS:
                    ssd(i, i // 3)
                elif i == 1:
                    moba()
                else:
                    lru()
                mlp_ple(i)
            rms(12)
            for k in range(KT):
                V.scalar_tensor_tensor(fin["yfin"][:, k, :], h[:, k, :], colA[:, 96 + k:97 + k], rstd[:], ALU.mult, ALU.mult).then_inc(s_fin, 1)
            dve.wait_ge(s_finT, 1)
            V.tensor_copy(fin["yrow"][:, 1, :], G[1][:].rearrange("p a b -> p (a b)")).then_inc(s_finE, 1)


INPUTS = ["x_prompt", "x_sample", "state_ssd_conv", "state_ssd", "cache_k", "cache_v", "page_table", "state_lru_conv",
          "state_lru", "p_prompt", "p_sample", "norm_mix", "norm_mlp", "norm_ple", "norm_final", "ssd_w_in",
          "ssd_conv_w", "ssd_conv_b", "ssd_dt_bias", "ssd_a_log", "ssd_d", "ssd_norm", "ssd_w_out", "moba_w_qkv",
          "moba_w_o", "lru_w_in", "lru_conv_w", "lru_conv_b", "lru_w_a", "lru_b_a", "lru_w_x", "lru_b_x",
          "lru_lambda", "lru_w_out", "mlp_w_up", "mlp_w_down", "ple_w_proj", "ple_w_gate"]
OUTPUTS = [("y_p", (1, 256, 1024)), ("y_s", (8, 1, 1024)),
           ("ssd_conv_p", (2, 1, 3, 4096)), ("ssd_state_p", (2, 1, 32, 64, 128)),
           ("k_p", (1, 1, 256, 8, 128)), ("v_p", (1, 1, 256, 8, 128)),
           ("lru_conv_p", (1, 1, 3, 1024)), ("lru_state_p", (1, 1, 1024)),
           ("ssd_conv_s", (2, 8, 3, 4096)), ("ssd_state_s", (2, 8, 32, 64, 128)),
           ("k_s", (1, 8, 1, 8, 128)), ("v_s", (1, 8, 1, 8, 128)),
           ("lru_conv_s", (1, 8, 3, 1024)), ("lru_state_s", (1, 8, 1024))]


def kernel(**inputs):
    import numpy as np
    import concourse.bacc as bacc
    from concourse.bass_utils import run_bass_kernel_spmd

    nc = bacc.Bacc("TRN2", target_bir_lowering=False, num_devices=1)
    arrays, t_in, t_out = {}, {}, {}
    for name in INPUTS:
        a = np.ascontiguousarray(inputs[name])
        arrays[f"in_{name}"] = a
        t_in[name] = nc.dram_tensor(f"in_{name}", a.shape, mybir.dt.from_np(a.dtype), kind="ExternalInput").ap()
    for name, shape in OUTPUTS:
        t_out[name] = nc.dram_tensor(f"out_{name}", shape, F32, kind="ExternalOutput").ap()
    build_trunk(nc, t_in, t_out)
    r = run_bass_kernel_spmd(nc, [arrays], core_ids=[0])
    return tuple(r.results[0][f"out_{name}"] for name, _ in OUTPUTS)
```
